# Optimizing a Trainium2 kernel written in Bass

```python
import math
import jax, jax.numpy as jnp
from jax import lax
import numpy as np

D_MODEL = 1024
BATCH = 1
SEQ = 256
DEPTH = 2

CHUNK = 64
Q_BLOCK = 128
HEAD_DIM = 64
FOX_HEADS = 12
FOX_WIDTH = FOX_HEADS * HEAD_DIM
DIFF_HEADS = 6
DIFF_QK_WIDTH = DIFF_HEADS * 2 * HEAD_DIM
DIFF_V_DIM = 2 * HEAD_DIM
DIFF_V_WIDTH = DIFF_HEADS * DIFF_V_DIM
MEM_HEADS = 4
MEM_WIDTH = MEM_HEADS * HEAD_DIM
MEM_TOKENS = 256
MIX_WIDTH = FOX_WIDTH + MEM_WIDTH
ROPE_THETA = 500000.0
ROT_DIM = HEAD_DIM // 4
D_FF = 256 * ((8 * D_MODEL // 3 + 255) // 256)
N_EXPERTS = 8
TOP_K = 2
EXPERT_FF = 7 * D_MODEL // 2
N_A = DEPTH // 2
N_B = DEPTH - N_A
N_DENSE = (DEPTH + 1) // 2
N_MOE = DEPTH // 2
EPS = 1e-5
MAX_START = 4096

kernel_name = "yoco_fox_diffattn_mem_moe_trunk"

def rmsnorm(x, g):
    xf = x.astype(jnp.float32)
    y = xf * lax.rsqrt(jnp.mean(xf * xf, axis=-1, keepdims=True) + EPS)
    return (y * g.astype(jnp.float32)).astype(x.dtype)

def rotary_partial(x, positions):
    half = ROT_DIM // 2
    inv_freq = ROPE_THETA ** (-(jnp.arange(half, dtype=jnp.float32) * 2.0 / ROT_DIM))
    ang = positions.astype(jnp.float32)[:, :, None] * inv_freq
    cos = jnp.cos(ang)[:, :, None, :]
    sin = jnp.sin(ang)[:, :, None, :]
    xf = x.astype(jnp.float32)
    x1, x2 = xf[..., :half], xf[..., half:ROT_DIM]
    out = jnp.concatenate([x1 * cos - x2 * sin, x2 * cos + x1 * sin, xf[..., ROT_DIM:]], axis=-1)
    return out.astype(x.dtype)

def masked_softmax(s, mask):
    return jax.nn.softmax(jnp.where(mask, s, -jnp.inf), axis=-1)

def forgetting_attention(q, k, v, log_f):
    S = q.shape[1]
    scale = HEAD_DIM ** -0.5
    cum = jnp.cumsum(log_f, axis=1).transpose(0, 2, 1)
    pos = jnp.arange(S)
    outs = []
    for i in range(S // Q_BLOCK):
        lo, hi = i * Q_BLOCK, (i + 1) * Q_BLOCK
        s = jnp.einsum('bqhd,bkhd->bhqk', q[:, lo:hi], k[:, :hi]).astype(jnp.float32) * scale
        s = s + cum[:, :, lo:hi, None] - cum[:, :, None, :hi]
        mask = pos[None, :hi] <= pos[lo:hi, None]
        p = masked_softmax(s, mask)
        outs.append(jnp.einsum('bhqk,bkhd->bqhd', p.astype(v.dtype), v[:, :hi]))
    return jnp.concatenate(outs, axis=1)

def differential_attention(q1, q2, k1, k2, v, lam):
    S = q1.shape[1]
    scale = HEAD_DIM ** -0.5
    chunk_id = jnp.arange(S) // CHUNK
    outs = []
    for i in range(S // Q_BLOCK):
        lo, hi = i * Q_BLOCK, (i + 1) * Q_BLOCK
        mask = chunk_id[None, :hi] <= chunk_id[lo:hi, None]
        s1 = jnp.einsum('bqhd,bkhd->bhqk', q1[:, lo:hi], k1[:, :hi]).astype(jnp.float32) * scale
        s2 = jnp.einsum('bqhd,bkhd->bhqk', q2[:, lo:hi], k2[:, :hi]).astype(jnp.float32) * scale
        a = masked_softmax(s1, mask) - lam * masked_softmax(s2, mask)
        outs.append(jnp.einsum('bhqk,bkhd->bqhd', a.astype(v.dtype), v[:, :hi]))
    return jnp.concatenate(outs, axis=1)

def memory_attention(q, mk, mv):
    s = jnp.einsum('bqhd,bmhd->bhqm', q, mk).astype(jnp.float32) * (HEAD_DIM ** -0.5)
    p = jax.nn.softmax(s, axis=-1)
    return jnp.einsum('bhqm,bmhd->bqhd', p.astype(mv.dtype), mv)

def swiglu(h, w_gate_up, w_down):
    g, u = jnp.split(h @ w_gate_up, 2, axis=-1)
    return (jax.nn.silu(g) * u) @ w_down

def moe_swiglu(h, w_router, w_gate_up, w_down):
    B, S, D = h.shape
    t = h.reshape(B * S, D)
    logits = (t @ w_router).astype(jnp.float32)
    top_val, top_idx = lax.top_k(logits, TOP_K)
    gates = jax.nn.softmax(top_val, axis=-1)
    combine = jnp.sum(jax.nn.one_hot(top_idx, N_EXPERTS, dtype=jnp.float32) * gates[..., None], axis=1)
    y = jnp.zeros_like(t)
    for e in range(N_EXPERTS):
        y = y + combine[:, e:e + 1].astype(t.dtype) * swiglu(t, w_gate_up[e], w_down[e])
    return y.reshape(B, S, D)

def setup_inputs(seed: int = 0) -> dict:
    key = jax.random.key(seed)
    ks = jax.random.split(key, 26)
    f32 = jnp.float32

    def w(k, shape, fan_in):
        return jax.random.normal(k, shape, f32) * (fan_in ** -0.5)

    def gain(k, shape):
        return 1.0 + 0.02 * jax.random.normal(k, shape, f32)

    start = jax.random.randint(ks[2], (BATCH, 1), 0, MAX_START, dtype=jnp.int32)
    positions = start + jnp.arange(SEQ, dtype=jnp.int32)[None, :]
    a_cols = 3 * FOX_WIDTH + FOX_HEADS + MEM_WIDTH
    return {
        "x": jax.random.normal(ks[0], (BATCH, SEQ, D_MODEL), f32),
        "mem": jax.random.normal(ks[1], (BATCH, MEM_TOKENS, D_MODEL), f32),
        "positions": positions,
        "mix_norm_g": gain(ks[3], (DEPTH, D_MODEL)),
        "ffn_norm_g": gain(ks[4], (DEPTH, D_MODEL)),
        "mem_norm_g": gain(ks[5], (DEPTH, D_MODEL)),
        "w_mem_kv": w(ks[6], (DEPTH, D_MODEL, 2 * MEM_WIDTH), D_MODEL),
        "w_out": w(ks[7], (DEPTH, MIX_WIDTH, D_MODEL), MIX_WIDTH),
        "w_in_a": w(ks[8], (N_A, D_MODEL, a_cols), D_MODEL),
        "b_forget": 0.1 * jax.random.normal(ks[9], (N_A, FOX_HEADS), f32),
        "w_q_b": w(ks[10], (N_B, D_MODEL, DIFF_QK_WIDTH + MEM_WIDTH), D_MODEL),
        "lambda_q1": 0.1 * jax.random.normal(ks[11], (N_B, HEAD_DIM), f32),
        "lambda_k1": 0.1 * jax.random.normal(ks[12], (N_B, HEAD_DIM), f32),
        "lambda_q2": 0.1 * jax.random.normal(ks[13], (N_B, HEAD_DIM), f32),
        "lambda_k2": 0.1 * jax.random.normal(ks[14], (N_B, HEAD_DIM), f32),
        "subln_g": gain(ks[15], (N_B, DIFF_V_DIM)),
        "kv_norm_g": gain(ks[16], (D_MODEL,)),
        "w_kv_shared": w(ks[17], (D_MODEL, DIFF_QK_WIDTH + DIFF_V_WIDTH), D_MODEL),
        "w_gate_up_dense": w(ks[18], (N_DENSE, D_MODEL, 2 * D_FF), D_MODEL),
        "w_down_dense": w(ks[19], (N_DENSE, D_FF, D_MODEL), D_FF),
        "w_router": w(ks[20], (N_MOE, D_MODEL, N_EXPERTS), D_MODEL),
        "w_gate_up_moe": w(ks[21], (N_MOE, N_EXPERTS, D_MODEL, 2 * EXPERT_FF), D_MODEL),
        "w_down_moe": w(ks[22], (N_MOE, N_EXPERTS, EXPERT_FF, D_MODEL), EXPERT_FF),
        "final_norm_g": gain(ks[23], (D_MODEL,)),
    }

def reference(x, mem, positions, mix_norm_g, ffn_norm_g, mem_norm_g, w_mem_kv, w_out,
              w_in_a, b_forget, w_q_b, lambda_q1, lambda_k1, lambda_q2, lambda_k2, subln_g,
              kv_norm_g, w_kv_shared, w_gate_up_dense, w_down_dense, w_router,
              w_gate_up_moe, w_down_moe, final_norm_g):
    B, S, _ = x.shape
    f32 = jnp.float32
    shared_k1 = shared_k2 = shared_v = None
    for l in range(DEPTH):
        h = rmsnorm(x, mix_norm_g[l])
        m = rmsnorm(mem, mem_norm_g[l])
        mkv = (m @ w_mem_kv[l]).reshape(B, MEM_TOKENS, 2, MEM_HEADS, HEAD_DIM)
        mk, mv = mkv[:, :, 0], mkv[:, :, 1]
        if l < N_A:
            proj = h @ w_in_a[l]
            q, k, v, fl, qm = jnp.split(
                proj, [FOX_WIDTH, 2 * FOX_WIDTH, 3 * FOX_WIDTH, 3 * FOX_WIDTH + FOX_HEADS], axis=-1)
            log_f = jax.nn.log_sigmoid(fl.astype(f32) + b_forget[l].astype(f32))
            y_self = forgetting_attention(
                q.reshape(B, S, FOX_HEADS, HEAD_DIM),
                k.reshape(B, S, FOX_HEADS, HEAD_DIM),
                v.reshape(B, S, FOX_HEADS, HEAD_DIM), log_f).reshape(B, S, FOX_WIDTH)
        else:
            j = l - N_A
            proj = h @ w_q_b[j]
            qd, qm = jnp.split(proj, [DIFF_QK_WIDTH], axis=-1)
            qd = qd.reshape(B, S, DIFF_HEADS, 2, HEAD_DIM)
            q1 = rotary_partial(qd[:, :, :, 0], positions)
            q2 = rotary_partial(qd[:, :, :, 1], positions)
            lam_init = 0.8 - 0.6 * math.exp(-0.3 * l)
            lam = (jnp.exp(jnp.sum(lambda_q1[j].astype(f32) * lambda_k1[j].astype(f32)))
                   - jnp.exp(jnp.sum(lambda_q2[j].astype(f32) * lambda_k2[j].astype(f32)))
                   + lam_init)
            o = differential_attention(q1, q2, shared_k1, shared_k2, shared_v, lam)
            o = rmsnorm(o, subln_g[j]) * (1.0 - lam_init)
            y_self = o.reshape(B, S, DIFF_V_WIDTH)
        y_mem = memory_attention(qm.reshape(B, S, MEM_HEADS, HEAD_DIM), mk, mv).reshape(B, S, MEM_WIDTH)
        x = x + jnp.concatenate([y_self, y_mem], axis=-1) @ w_out[l]

        h = rmsnorm(x, ffn_norm_g[l])
        if l % 2 == 0:
            x = x + swiglu(h, w_gate_up_dense[l // 2], w_down_dense[l // 2])
        else:
            x = x + moe_swiglu(h, w_router[l // 2], w_gate_up_moe[l // 2], w_down_moe[l // 2])

        if l == N_A - 1:
            kvs = rmsnorm(x, kv_norm_g) @ w_kv_shared
            kd, vs = jnp.split(kvs, [DIFF_QK_WIDTH], axis=-1)
            kd = kd.reshape(B, S, DIFF_HEADS, 2, HEAD_DIM)
            shared_k1 = rotary_partial(kd[:, :, :, 0], positions)
            shared_k2 = rotary_partial(kd[:, :, :, 1], positions)
            shared_v = vs.reshape(B, S, DIFF_HEADS, DIFF_V_DIM)
    return rmsnorm(x, final_norm_g)


_drawn_inputs = setup_inputs


def setup_inputs(seed=0):
    import zlib

    import numpy as np

    out = dict(_drawn_inputs(seed))
    spreads = {}
    factors = {'mem_norm_g': 5.764,
     'subln_g': 18.918,
     'kv_norm_g': 2.936,
     'final_norm_g': 8.448,
     'ffn_norm_g': 3.191}
    for name, (base, spread) in spreads.items():
        noise = np.random.default_rng([zlib.crc32(name.encode()), seed]).standard_normal(out[name].shape)
        drawn = base * np.exp(spread * noise) if base else spread * noise
        out[name] = __import__('jax').numpy.asarray(drawn.astype(out[name].dtype))
    for name, factor in factors.items():
        out[name] = (out[name] * factor).astype(out[name].dtype)
    return out
```

```python
import math
from contextlib import ExitStack

import concourse.bass as bass
from concourse import mybir
import numpy as np

P = 128
F32, F32R, BF16 = mybir.dt.float32, mybir.dt.float32r, mybir.dt.bfloat16
I32, U32 = mybir.dt.int32, mybir.dt.uint32
ALU, ACT, AX = mybir.AluOpType, mybir.ActivationFunctionType, mybir.AxisListType

D, SEQ, MEM = 1024, 256, 256
KC = D // P
NT = SEQ // P
HD = 64
FOX_H, DIFF_H, MEM_H = 12, 6, 4
FOX_W, MEM_W = FOX_H * HD, MEM_H * HD
DV = 2 * HD
D_FF, N_EXP, E_FF = 2816, 8, 3584
ROT = 16
HALF = ROT // 2
THETA = 500000.0
EPS = 1e-5
SCALE = HD ** -0.5
NEG = -1.0e30
LAM_INIT = 0.8 - 0.6 * math.exp(-0.3)

UNIT = 2048
RAW, SPLIT = 6, 3
WIDE = 256

PROJ = ([("mk", 0), ("mv", 0), ("mk", 1), ("mv", 1)]
        + [("q", i) for i in range(3)] + [("k", i) for i in range(3)] + [("v", i) for i in range(3)] + [("qm", 0)]
        + [("out", i) for i in range(4)]
        + [("kd", i) for i in range(3)] + [("vd", i) for i in range(3)]
        + [("qd", i) for i in range(3)] + [("qm", 1)]
        + [("out", i) for i in range(4)])
P_MEM, P_A, P_OUT0, P_KV, P_QB, P_OUT1, P_END = 0, 4, 14, 18, 24, 28, 32
FFN_STEPS = D_FF // WIDE
FFN_UNITS = 3 * FFN_STEPS
U_FFN = P_KV
U_KV = U_FFN + FFN_UNITS
U_MOE = U_KV + (P_END - P_KV)
MOE_STEPS = E_FF // 512
MOE_UNITS = 6 * MOE_STEPS
TB = 14
FILL = list(np.cumsum([4, 4, 4, 8, 4, 4, 4, 5, 4]))
NORM_FILL = [0, 1, 2, 4, 5, 6, 8]
FILL_BUF = [0, 1, 0, 1, 0, 1, 0, 1, 0]


def unit_of(p):
    return p if p < P_KV else U_KV + p - P_KV


def fill_of(p):
    for f, end in ((0, 2), (1, 4), (2, P_OUT0), (3, P_KV), (5, P_QB), (6, P_OUT1), (7, P_END)):
        if p < end:
            return f


def ffn_pos(kind, j):
    if kind == "D":
        return 4 + 3 * j if j < FFN_STEPS - 1 else FFN_UNITS - 1
    base = 0 if j == 0 else 3 * j - 1
    return base + (kind == "U")


def moe_pos(kind, j, a):
    if kind == "D":
        return (8 + 6 * j if j < MOE_STEPS - 1 else MOE_UNITS - 2) + a
    base = 0 if j == 0 else 6 * j - 2
    return base + 2 * (kind == "U") + a


def attention_plan(layer):
    if layer == 0:
        scores = [("fox", h) for h in range(FOX_H)] + [("mem", h) for h in range(MEM_H)]
        outs, last = scores, list(range(16))
    else:
        scores = [("diff", h) for h in range(2 * DIFF_H)] + [("mem", h) for h in range(MEM_H)]
        outs = [("diff", h) for h in range(DIFF_H)] + [("mem", h) for h in range(MEM_H)]
        last = [2 * r + 1 for r in range(DIFF_H)] + [12 + h for h in range(MEM_H)]
    return scores, outs, last


S_BASE = [0, 16]
R_BASE = [0, 16]


def build(nc, x, mem, positions, mix_norm_g, ffn_norm_g, mem_norm_g, w_mem_kv, w_out, w_in_a, b_forget, w_q_b,
          lambda_q1, lambda_k1, lambda_q2, lambda_k2, subln_g, kv_norm_g, w_kv_shared, w_gate_up_dense,
          w_down_dense, w_router, w_gate_up_moe, w_down_moe, final_norm_g, out):
    with ExitStack() as ctx:
        def sb(name, shape, dt=F32):
            return ctx.enter_context(nc.sbuf_tensor(name, shape, dt))

        def sem(name):
            return ctx.enter_context(nc.semaphore(name))

        raw = sb("raw", [P, RAW, UNIT])
        whi = sb("whi", [P, SPLIT, UNIT], F32R)
        wlo = sb("wlo", [P, SPLIT, UNIT], F32R)
        X = sb("X", [P, NT, D])
        hn = sb("hn", [P, NT, D])
        gain = sb("gain", [P, D])
        op_hi = [sb(f"op_hi{i}", [P, KC, SEQ], F32R) for i in range(2)]
        op_lo = [sb(f"op_lo{i}", [P, KC, SEQ], F32R) for i in range(2)]
        tok = sb("tok", [P, NT, D])
        mkT = [sb(f"mkT{i}", [P, 2, MEM]) for i in range(2)]
        mv = [sb(f"mv{i}", [P, 2, MEM_W]) for i in range(2)]
        qT = sb("qT", [P, 6, SEQ])
        kT = sb("kT", [P, 6, SEQ])
        v = sb("v", [P, NT, FOX_W])
        qmT = sb("qmT", [P, 2, SEQ])
        prob = [sb(f"prob{i}", [P, 512]) for i in range(3)]
        probT = [sb(f"probT{i}", [P, 512]) for i in range(2)]
        h2T_hi = [sb(f"h2T_hi{i}", [P, 512], F32R) for i in range(2)]
        h2T_lo = [sb(f"h2T_lo{i}", [P, 512], F32R) for i in range(2)]
        gate_act, h2 = prob[0:2], probT[0:2]
        ye = qT[:, 0:4, :].rearrange("p a b -> p (a b)")
        slot_oh = kT[:, 0, :].rearrange("p (t s) -> p t s", t=NT)
        slot_ohT = kT[:, 1, :]
        xg_hi, xg_lo = op_hi[1], op_lo[1]

        ident = sb("ident", [P, P])
        ident_bf = sb("ident_bf", [P, P], BF16)
        upper = sb("upper", [P, SEQ])
        upper_bf = sb("upper_bf", [P, P], BF16)
        ones_bf = sb("ones_bf", [P, P], BF16)
        causal = sb("causal", [P, P], BF16)
        chunked = sb("chunked", [P, P], BF16)
        small_w = sb("small_w", [P, KC, 20])
        small_hi = sb("small_hi", [P, KC, 20], F32R)
        small_lo = sb("small_lo", [P, KC, 20], F32R)
        b_f = sb("b_f", [P, FOX_H])
        subln = sb("subln", [P, DV])
        lam_v = sb("lam_v", [P, 4, HD])
        lam = sb("lam", [P, 8])
        pos_i = sb("pos_i", [P, NT], I32)
        pos_f = sb("pos_f", [P, NT])
        inv_f = sb("inv_f", [P, HALF])
        ang = sb("ang", [P, 3, NT, HALF])
        cosv = sb("cosv", [P, NT, HALF])
        sinv = sb("sinv", [P, NT, HALF])
        rot = prob[2][:, 0:4 * 12 * HALF].rearrange("p (a h n) -> p a h n", a=4, h=12)
        stat = sb("stat", [P, 8, 4, NT])
        fg = sb("fg", [P, 3, NT, FOX_H])
        ncum = sb("ncum", [FOX_H, SEQ])
        negm = sb("negm", [P, 32, NT])
        rsum = sb("rsum", [P, 32, NT])
        rinv = sb("rinv", [P, 32, NT])
        o_ss = sb("o_ss", [P, 4, NT * DIFF_H])
        lg = sb("lg", [P, NT, N_EXP])
        top = sb("top", [P, NT, 8])
        top_i = sb("top_i", [P, NT, 8], U32)
        top_f = sb("top_f", [P, NT, 8])
        gates = sb("gates", [P, NT, 4])
        oh = sb("oh", [P, 2, NT, N_EXP])
        comb = sb("comb", [P, NT, N_EXP])
        member = sb("member", [P, NT, N_EXP + 1])
        member_bf = sb("member_bf", [P, NT, N_EXP], BF16)
        rank = sb("rank", [P, NT, N_EXP + 1])
        iota8 = sb("iota8", [P, N_EXP])
        slot_no = sb("slot_no", [P, SEQ])
        over = sb("over", [P, 2])
        over_i = sb("over_i", [P, 1], I32)

        bank = [ctx.enter_context(nc.psum_tensor(f"bank{i}", [P, 512], F32)) for i in range(8)]

        raw_in = [sem(f"raw_in{i}") for i in range(RAW)]
        hi_ready = sem("hi_ready")
        lo_ready = sem("lo_ready")
        unit_used = sem("unit_used")
        x_in, mem_in, small_in, gain_in = sem("x_in"), sem("mem_in"), sem("small_in"), sem("gain_in")
        consts = sem("consts")
        masks = sem("masks")
        small_hi_ready, small_lo_ready = sem("small_hi_ready"), sem("small_lo_ready")
        norm_ss = sem("norm_ss")
        norm_var = sem("norm_var")
        norm_std = sem("norm_std")
        hn_ready = sem("hn_ready")
        tr_ready = sem("tr_ready")
        fill_hi = sem("fill_hi")
        fill_lo = sem("fill_lo")
        proj_out = sem("proj_out")
        fl_ready, fl_sum, fl_ln, logf_ready = sem("fl_ready"), sem("fl_sum"), sem("fl_ln"), sem("logf_ready")
        cum_ready, ncum_ready = sem("cum_ready"), sem("ncum_ready")
        lam_ready, lam_exp, ang_ready, sin_ready = sem("lam_ready"), sem("lam_exp"), sem("ang_ready"), sem("sin_ready")
        rot_ready = sem("rot_ready")
        qk_tr = sem("qk_tr")
        qk_out = sem("qk_out")
        score_ready = sem("score_ready")
        rowmax = sem("rowmax")
        exp_done = sem("exp_done")
        prob_ready = sem("prob_ready")
        pT_ready = sem("pT_ready")
        pT_out = sem("pT_out")
        pv_ready = sem("pv_ready")
        o_out = sem("o_out")
        o_norm = sem("o_norm")
        o_tr = sem("o_tr")
        silu_done = sem("silu_done")
        mul_done = sem("mul_done")
        h2_hi, h2_lo = sem("h2_hi"), sem("h2_lo")
        x_added = sem("x_added")
        logit_ready, top_ready, gate_exp = sem("logit_ready"), sem("top_ready"), sem("gate_exp")
        member_ready, rank_ready, route_ready = sem("member_ready"), sem("rank_ready"), sem("route_ready")
        oh_ready = sem("oh_ready")
        tb_ready = sem("tb_ready")
        ohT_out = sem("ohT_out")
        xg_hi_ready, xg_lo_ready = sem("xg_hi_ready"), sem("xg_lo_ready")
        ye_act, ye_dve = sem("ye_act"), sem("ye_dve")
        x_final = sem("x_final")
        out_done = sem("out_done")
        act_step, dve_step = sem("act_step"), sem("dve_step")

        def rows(w):
            return w.rearrange("(k p) n -> p k n", p=P)

        mem_kv_v = [rows(w_mem_kv[i]) for i in range(2)]
        in_a_v, q_b_v, kv_v = rows(w_in_a[0]), rows(w_q_b[0]), rows(w_kv_shared)
        out_v = [rows(w_out[i]) for i in range(2)]
        gu_v, down_v = rows(w_gate_up_dense[0]), rows(w_down_dense[0])

        def proj_source(p):
            what, i = PROJ[p]
            c = WIDE * i
            if what in ("mk", "mv"):
                c = MEM_W * (what == "mv")
                return mem_kv_v[i][:, :, c:c + WIDE]
            if what in ("q", "k", "v"):
                c += FOX_W * "qkv".index(what)
                return in_a_v[:, :, c:c + WIDE]
            if what == "qm" and i == 0:
                return in_a_v[:, :, 3 * FOX_W + FOX_H:3 * FOX_W + FOX_H + MEM_W]
            if what == "qm":
                return q_b_v[:, :, FOX_W:FOX_W + MEM_W]
            if what == "out":
                return out_v[p >= P_OUT1][:, :, c:c + WIDE]
            if what == "kd":
                return kv_v[:, :, c:c + WIDE]
            if what == "vd":
                return kv_v[:, :, FOX_W + c:FOX_W + c + WIDE]
            return q_b_v[:, :, c:c + WIDE]

        def wide(t3, slot):
            return t3[:, slot, :].rearrange("p (k n) -> p k n", k=KC)

        block = ctx.enter_context(nc.Block())

        @block.sync
        def _(sp):
            def load(c, turns, src, shape):
                if not (isinstance(turns, int) and c + RAW * turns < RAW):
                    sp.wait_ge(lo_ready, c + RAW * turns - RAW + 1)
                dst = raw[:, c % RAW, :].rearrange("p (k n) -> p k n", k=shape)
                sp.dma_start(dst, src).then_inc(raw_in[c % RAW], 16)

            sp.dma_start(tok[:], mem[0].rearrange("(t p) d -> p t d", p=P)).then_inc(mem_in, 16)
            for p in range(P_KV):
                load(unit_of(p), 0, proj_source(p), KC)
                if p == 1:
                    sp.dma_start(X[:], x[0].rearrange("(t p) d -> p t d", p=P)).then_inc(x_in, 16)

            def ffn_load(kind, j, turns=0, moved=0):
                c = U_FFN + ffn_pos(kind, j)
                if kind == "D":
                    src = down_v[:, bass.ds(2 * (j + moved), 2), :]
                    return load(c, turns, src, 2)
                col = (D_FF if kind == "U" else 0) + WIDE * (j + moved)
                load(c, turns, gu_v[:, :, bass.ds(col, WIDE)], KC)

            ffn_load("G", 0)
            ffn_load("U", 0)
            with sp.Fori(0, (FFN_STEPS - 1) // 2) as it:
                for j in (1, 2):
                    ffn_load("G", j, it, 2 * it)
                    ffn_load("U", j, it, 2 * it)
                    ffn_load("D", j - 1, it, 2 * it)
            ffn_load("D", FFN_STEPS - 1)
            for p in range(P_KV, P_END):
                load(unit_of(p), 0, proj_source(p), KC)

            def expert_loads(ps):
                with sp.Fori(0, N_EXP) as e:
                    gu_e = w_gate_up_moe[0].rearrange("e (k p) n -> e p k n", p=P)[bass.ds(e, 1)].squeeze(0)
                    dn_e = w_down_moe[0].rearrange("e (k p) n -> e p k n", p=P)[bass.ds(e, 1)].squeeze(0)
                    base = U_MOE + ps * N_EXP * MOE_UNITS

                    def go(kind, j):
                        for a in range(2):
                            c = base + moe_pos(kind, j, a)
                            if kind == "D":
                                src = dn_e[:, 4 * j + 2 * a:4 * j + 2 * a + 2, :]
                            else:
                                col = (E_FF if kind == "U" else 0) + 512 * j
                                src = gu_e[:, 4 * a:4 * a + 4, col:col + 512]
                            load(c, (MOE_UNITS // RAW) * e, src, 2 if kind == "D" else 4)

                    for j in range(MOE_STEPS):
                        go("G", j)
                        go("U", j)
                        if j:
                            go("D", j - 1)
                    go("D", MOE_STEPS - 1)

            expert_loads(0)
            sp.wait_ge(route_ready, 1)
            flag = sp.value_load(over_i[0:1, 0:1], min_val=0, max_val=1)
            with sp.If(flag == 1):
                expert_loads(1)
            sp.wait_ge(hn_ready, 16)
            sp.dma_start(out[0].rearrange("(t p) d -> p t d", p=P), hn[:]).then_inc(out_done, 16)
            sp.wait_ge(out_done, 16)

        @block.gpsimd
        def _(pool):
            gains = [mem_norm_g[0], mem_norm_g[1], mix_norm_g[0], ffn_norm_g[0], kv_norm_g, mix_norm_g[1],
                     ffn_norm_g[1], final_norm_g]

            def load_gain(n):
                if n:
                    pool.wait_ge(hn_ready, 2 * n)
                g = gains[n].rearrange("(a d) -> a d", a=1)
                pool.dma_start(gain[:], g.to_broadcast([P, D])).then_inc(gain_in, 16)

            load_gain(0)
            smalls = [
                (small_w[:, :, 0:FOX_H], in_a_v[:, :, 3 * FOX_W:3 * FOX_W + FOX_H]),
                (small_w[:, :, FOX_H:20], rows(w_router[0])),
                (b_f[:], b_forget[0:1, :].to_broadcast([P, FOX_H])),
                (subln[:], subln_g[0:1, :].to_broadcast([P, DV])),
                (pos_i[:], positions[0].rearrange("(t p) -> p t", p=P)),
            ] + [(lam_v[:, i, :], l[0:1, :].to_broadcast([P, HD]))
                 for i, l in enumerate((lambda_q1, lambda_k1, lambda_q2, lambda_k2))]
            assert len(smalls) == 9
            with nc.allow_non_contiguous_dma("small columns"):
                for dst, src in smalls:
                    pool.dma_start(dst, src).then_inc(small_in, 16)

            g = nc.gpsimd
            g.memset(ident[:], 0.0).then_inc(masks, 1)
            g.memset(upper[:], 1.0).then_inc(masks, 1)
            g.memset(ones_bf[:], 1.0).then_inc(masks, 1)
            g.memset(causal[:], 0.0).then_inc(masks, 1)
            g.memset(chunked[:], 0.0).then_inc(masks, 1)
            pool.wait_ge(masks, 5)
            g.affine_select(out=ident[:], in_=ident[:], compare_op=ALU.not_equal, fill=1.0, base=0,
                            pattern=[[-1, P]], channel_multiplier=1).then_inc(masks, 1)
            g.affine_select(out=upper[:], in_=upper[:], compare_op=ALU.is_ge, fill=0.0, base=0,
                            pattern=[[1, SEQ]], channel_multiplier=-1).then_inc(masks, 1)
            g.affine_select(out=causal[:], in_=causal[:], compare_op=ALU.is_ge, fill=NEG, base=0,
                            pattern=[[-1, P]], channel_multiplier=1).then_inc(masks, 1)
            g.affine_select(out=chunked[:, HD:P], in_=chunked[:, HD:P], compare_op=ALU.is_ge, fill=NEG, base=-HD,
                            pattern=[[0, HD]], channel_multiplier=1).then_inc(masks, 1)
            pool.wait_ge(masks, 9)
            g.tensor_copy(ident_bf[:], ident[:]).then_inc(masks, 1)
            g.tensor_copy(upper_bf[:], upper[:, 0:P]).then_inc(masks, 1)
            g.iota(iota8[:], pattern=[[1, N_EXP]], base=0, channel_multiplier=0,
                   allow_small_or_imprecise_dtypes=True).then_inc(masks, 1)
            for i in range(HALF):
                f = float(np.float32(THETA) ** np.float32(-(np.float32(i) * np.float32(2.0) / np.float32(ROT))))
                g.memset(inv_f[:, i:i + 1], f).then_inc(masks, 1)
            g.iota(slot_no[:], pattern=[[1, SEQ]], base=0, channel_multiplier=0,
                   allow_small_or_imprecise_dtypes=True).then_inc(masks, 1)
            g.memset(member[:, :, N_EXP:N_EXP + 1], 0.0).then_inc(masks, 1)
            pool.wait_ge(masks, 14 + HALF)
            g.memset(rank[:, :, N_EXP:N_EXP + 1], 0.0).then_inc(consts, 1)
            for n in range(1, 8):
                load_gain(n)

        @block.scalar
        def _(act):
            a = nc.scalar
            own = [0]

            def step(ins):
                own[0] += 1
                ins.then_inc(act_step, 1)
                act.wait_ge(act_step, own[0])

            def split_hi(c, turns=0):
                r = c // RAW + 1 + turns
                act.wait_ge(raw_in[c % RAW], 16 * r)
                if not (isinstance(turns, int) and c + RAW * turns < SPLIT):
                    act.wait_ge(unit_used, c + RAW * turns - SPLIT + 1)
                a.copy(whi[:, c % SPLIT, :], raw[:, c % RAW, :]).then_inc(hi_ready, 1)

            def norm_act(n, src, ready):
                if n:
                    act.wait_ge(tr_ready, 4 * n)
                for s, val in ready:
                    act.wait_ge(s, val)
                for t in range(NT):
                    a.activation(hn[:, t, :], src[:, t, :], ACT.Square,
                                 accum_out=stat[:, n, 0, t:t + 1]).then_inc(norm_ss, 1)
                act.wait_ge(norm_var, n + 1 + (n > 5))
                a.activation(stat[:, n, 2, :], stat[:, n, 1, :], ACT.Sqrt).then_inc(norm_std, 1)

            def norm_fill_hi(n):
                if n < 7:
                    buf = op_hi[FILL_BUF[NORM_FILL[n]]]
                    for g in range(4):
                        act.wait_ge(tr_ready, 4 * n + g + 1)
                        t, h = g // 2, g % 2
                        a.copy(buf[:, 4 * h:4 * h + 4, t * P:(t + 1) * P],
                               bank[g][:].rearrange("p (c n) -> p c n", c=4)).then_inc(fill_hi, 1)

            def split_until(n, state=[0]):
                while state[0] < n:
                    split_hi(unit_of(state[0]))
                    state[0] += 1

            norm_act(0, tok, [(mem_in, 16)])
            split_until(2)
            norm_fill_hi(0)
            act.wait_ge(small_in, 16 * 9)
            a.copy(small_hi[:], small_w[:]).then_inc(small_hi_ready, 1)
            split_until(3)
            norm_act(1, tok, [])
            norm_fill_hi(1)
            norm_act(2, X, [(x_in, 16)])
            split_until(5)
            act.wait_ge(unit_used, 2)
            norm_fill_hi(2)
            act.wait_ge(lam_ready, 1)
            a.activation(lam[:, 2:4], lam[:, 0:2], ACT.Exp).then_inc(lam_exp, 1)
            split_until(P_A + 8)
            act.wait_ge(ang_ready, 1)
            a.activation(sinv[:], ang[:, 1], ACT.Sin)
            a.activation(cosv[:], ang[:, 2], ACT.Sin).then_inc(sin_ready, 1)
            split_until(P_OUT0 + 3)
            act.wait_ge(fl_sum, 1)
            step(a.activation(fg[:, 1], fg[:, 1], ACT.Exp))
            a.activation(fg[:, 1], fg[:, 1], ACT.Ln, bias=1.0).then_inc(fl_ln, 1)

            def attention_act(layer):
                scores, outs, last = attention_plan(layer)
                sb0, rb0 = S_BASE[layer], R_BASE[layer]
                done = [0]

                def exps(upto):
                    while done[0] <= min(upto, len(scores) - 1):
                        s = done[0]
                        g = sb0 + s
                        act.wait_ge(rowmax, g + 1)
                        if s >= 3:
                            owner = min(r for r in range(len(outs)) if last[r] >= s - 3)
                            act.wait_ge(pT_ready, rb0 + owner + 1)
                        elif layer:
                            act.wait_ge(pT_ready, rb0)
                        w0 = P if scores[s][0] != "mem" else MEM
                        w1 = MEM
                        a.activation(prob[s % 3][:, 0:w0], bank[s % 3][:, 0:w0], ACT.Exp,
                                     bias=negm[:, g, 0:1], accum_out=rsum[:, g, 0:1])
                        a.activation(prob[s % 3][:, w0:w0 + w1], bank[s % 3][:, w0:w0 + w1], ACT.Exp,
                                     bias=negm[:, g, 1:2], accum_out=rsum[:, g, 1:2]).then_inc(exp_done, 1)
                        done[0] += 1

                def fill(r):
                    kind, h = outs[r]
                    if kind == "diff" or h % 2 == 0:
                        return
                    c = h // 2 + (6 if kind == "mem" else 0)
                    act.wait_ge(pv_ready, rb0 + r + 1)
                    a.copy(op_hi[1][:, c, :], bank[5 + (r // 2) % 2][:, 0:SEQ]).then_inc(fill_hi, 1)

                for r in range(len(outs)):
                    exps((last[r - 1] if r else -1) + 3)
                    w = 512 if outs[r][0] == "mem" else 384
                    act.wait_ge(pT_ready, rb0 + r + 1)
                    if rb0 + r >= 2:
                        act.wait_ge(pv_ready, rb0 + r - 1)
                    a.copy(probT[r % 2][:, 0:w], bank[3 + r % 2][:, 0:w]).then_inc(pT_out, 1)
                    if r:
                        fill(r - 1)
                fill(len(outs) - 1)

            act.wait_ge(unit_used, 4)
            attention_act(0)
            split_until(P_KV)
            split_hi(U_FFN)
            split_hi(U_FFN + 1)
            norm_act(3, X, [(proj_out, P_KV)])
            norm_fill_hi(3)

            def ffn_silu(j, turns=0):
                act.wait_ge(unit_used, U_FFN + ffn_pos("G", j) + 1 + RAW * turns)
                a.activation(gate_act[j % 2][:], bank[4 + 2 * (j % 2)][:], ACT.Silu).then_inc(silu_done, 1)

            def ffn_h2_hi(j, moved=0):
                act.wait_ge(mul_done, j + 1 + moved)
                a.copy(h2T_hi[j % 2][:], h2[j % 2][:]).then_inc(h2_hi, 1)

            ffn_silu(0)
            with act.Fori(0, (FFN_STEPS - 1) // 2) as it:
                for j in (1, 2):
                    split_hi(U_FFN + ffn_pos("G", j), it)
                    ffn_h2_hi(j - 1, 2 * it)
                    split_hi(U_FFN + ffn_pos("U", j), it)
                    ffn_silu(j, it)
                    split_hi(U_FFN + ffn_pos("D", j - 1), it)
            split_hi(U_FFN + FFN_UNITS - 1)
            ffn_h2_hi(FFN_STEPS - 1)

            split_hi(U_KV)
            split_hi(U_KV + 1)
            norm_act(4, X, [(x_added, 4)])
            norm_fill_hi(4)
            for u in range(2, 9):
                split_hi(U_KV + u)
            norm_act(5, X, [])
            norm_fill_hi(5)
            for u in range(9, 13):
                split_hi(U_KV + u)
            attention_act(1)
            act.wait_ge(norm_var, 7)
            a.activation(o_ss[:, 2], o_ss[:, 1], ACT.Sqrt).then_inc(norm_std, 1)
            for b in range(3):
                act.wait_ge(o_tr, b + 1)
                a.copy(op_hi[1][:, 2 * b:2 * b + 2, :],
                       bank[b][:].rearrange("p (c n) -> p c n", c=2)).then_inc(fill_hi, 1)
            split_hi(U_KV + 13)
            norm_act(6, X, [(proj_out, P_END)])
            norm_fill_hi(6)
            act.wait_ge(top_ready, 1)
            a.activation(gates[:, :, 1], gates[:, :, 0], ACT.Exp).then_inc(gate_exp, 1)

            def experts_act(ps):
                ub = U_MOE + ps * N_EXP * MOE_UNITS
                tb = 2 * (ps + 1) + TB * N_EXP * ps
                hb = FFN_STEPS + MOE_STEPS * N_EXP * ps

                def gathered_hi(tbase):
                    for i in range(2):
                        act.wait_ge(tb_ready, tbase + i + 1)
                        a.copy(xg_hi[:, 4 * i:4 * i + 4, 0:P],
                               bank[7 - i][:].rearrange("p (c n) -> p c n", c=4)).then_inc(xg_hi_ready, 1)

                gathered_hi(tb - 2)
                with act.Fori(0, N_EXP) as e:
                    turns = (MOE_UNITS // RAW) * e

                    def hi(kind, j, k):
                        split_hi(ub + moe_pos(kind, j, k), turns)

                    def evac_T(j):
                        idx = 1 + j if j < MOE_STEPS - 1 else 9
                        act.wait_ge(tb_ready, tb + TB * e + idx + 1)
                        b = 7 - j % 2
                        a.copy(h2T_hi[j % 2][:], bank[b][:]).then_inc(h2_hi, 1)

                    for j in range(MOE_STEPS):
                        hi("G", j, 0)
                        hi("G", j, 1)
                        hi("U", j, 0)
                        if j == 0:
                            act.wait_ge(tb_ready, tb + TB * e + 1)
                            a.copy(slot_ohT, bank[6][:, 0:SEQ]).then_inc(ohT_out, 1)
                        else:
                            evac_T(j - 1)
                        hi("U", j, 1)
                        if j:
                            hi("D", j - 1, 0)
                        act.wait_ge(unit_used, ub + moe_pos("G", j, 1) + 1 + MOE_UNITS * e)
                        act.wait_ge(mul_done, hb + MOE_STEPS * e + max(j - 1, 0))
                        a.activation(gate_act[j % 2][:], bank[2 + 2 * (j % 2)][:], ACT.Silu).then_inc(silu_done, 1)
                        if j:
                            hi("D", j - 1, 1)
                    hi("D", MOE_STEPS - 1, 0)
                    hi("D", MOE_STEPS - 1, 1)
                    gathered_hi(tb + TB * e + 7)
                    evac_T(MOE_STEPS - 1)
                    act.wait_ge(unit_used, ub + MOE_UNITS + MOE_UNITS * e)
                    a.copy(ye[:, 0:512], bank[0][:]).then_inc(ye_act, 1)

            experts_act(0)
            act.wait_ge(route_ready, 1)
            flag = act.value_load(over_i[0:1, 0:1], min_val=0, max_val=1)
            with act.If(flag == 1):
                experts_act(1)
            act.wait_ge(x_final, 1)
            for t in range(NT):
                a.activation(hn[:, t, :], X[:, t, :], ACT.Square,
                             accum_out=stat[:, 7, 0, t:t + 1]).then_inc(norm_ss, 1)
            act.wait_ge(norm_var, 9)
            a.activation(stat[:, 7, 2, :], stat[:, 7, 1, :], ACT.Sqrt).then_inc(norm_std, 1)

        @block.vector
        def _(dve):
            d = nc.vector
            own = [0]

            def step(ins):
                own[0] += 1
                ins.then_inc(dve_step, 1)
                dve.wait_ge(dve_step, own[0])

            def split_lo(c, turns=0):
                dve.wait_ge(hi_ready, c + RAW * turns + 1)
                d.tensor_tensor(wlo[:, c % SPLIT, :], raw[:, c % RAW, :], whi[:, c % SPLIT, :].bitcast(F32),
                                ALU.subtract).then_inc(lo_ready, 1)

            def split_until(n, state=[0]):
                while state[0] < n:
                    split_lo(unit_of(state[0]))
                    state[0] += 1

            def norm_dve(n, src, eps_count):
                dve.wait_ge(norm_ss, 2 * n + 2)
                d.tensor_scalar(stat[:, n, 1, :], stat[:, n, 0, :], 1.0 / D, EPS, ALU.mult,
                                ALU.add).then_inc(norm_var, 1)
                dve.wait_ge(norm_std, eps_count)
                step(d.reciprocal(stat[:, n, 3, :], stat[:, n, 2, :]))
                dve.wait_ge(gain_in, 16 * (n + 1))
                for t in range(NT):
                    d.scalar_tensor_tensor(out=hn[:, t, :], in0=src[:, t, :], scalar=stat[:, n, 3, t:t + 1],
                                           in1=gain[:], op0=ALU.mult, op1=ALU.mult).then_inc(hn_ready, 1)

            def norm_fill_lo(n):
                f = NORM_FILL[n]
                hi, lo = op_hi[FILL_BUF[f]], op_lo[FILL_BUF[f]]
                for g in range(4):
                    t, h = g // 2, g % 2
                    dve.wait_ge(fill_hi, int(FILL[f]) - 3 + g)
                    d.tensor_tensor(lo[:, 4 * h:4 * h + 4, t * P:(t + 1) * P],
                                    bank[g][:].rearrange("p (c n) -> p c n", c=4),
                                    hi[:, 4 * h:4 * h + 4, t * P:(t + 1) * P].bitcast(F32),
                                    ALU.subtract).then_inc(fill_lo, 1)

            def take(p):
                what, i = PROJ[p]
                dve.wait_ge(unit_used, unit_of(p) + 1)
                b2 = bank[4 + p % 4][:].rearrange("p (c n) -> p c n", c=2)
                cols = slice(WIDE * i, WIDE * (i + 1))
                if what == "mk":
                    ins = d.tensor_copy(mkT[i][:], b2)
                elif what == "mv":
                    ins = d.tensor_copy(mv[i][:], b2)
                elif what == "q":
                    ins = d.tensor_scalar(qT[:, 2 * i:2 * i + 2, :], b2, SCALE, None, ALU.mult)
                elif what == "k":
                    ins = d.tensor_copy(kT[:, 2 * i:2 * i + 2, :], b2)
                elif what in ("v", "vd"):
                    ins = d.tensor_copy(v[:, :, cols], b2)
                elif what == "qm":
                    ins = d.tensor_scalar(qmT[:], b2, SCALE, None, ALU.mult)
                elif what == "out":
                    ins = d.tensor_tensor(X[:, :, cols], X[:, :, cols], b2, ALU.add)
                elif what == "kd":
                    ins = d.tensor_copy(tok[:, :, cols], b2)
                else:
                    ins = d.tensor_scalar(tok[:, :, cols], b2, SCALE, None, ALU.mult)
                ins.then_inc(proj_out, 1)

            norm_dve(0, tok, 1)
            split_until(2)
            norm_fill_lo(0)
            dve.wait_ge(small_hi_ready, 1)
            d.tensor_tensor(small_lo[:], small_w[:], small_hi[:].bitcast(F32), ALU.subtract).then_inc(small_lo_ready, 1)
            split_until(3)
            take(0)
            norm_dve(1, tok, 2)
            take(1)
            norm_fill_lo(1)
            norm_dve(2, X, 3)
            split_until(4)
            take(2)
            norm_fill_lo(2)
            split_until(5)
            take(3)
            dve.wait_ge(small_in, 16 * 9)
            lam4 = lam_v[:].rearrange("p (a b) n -> p a b n", a=2)
            step(d.tensor_tensor(lam4[:, :, 0, :], lam4[:, :, 0, :], lam4[:, :, 1, :], ALU.mult))
            d.tensor_reduce(lam[:, 0:2], lam4[:, :, 0, :], AX.X, ALU.add).then_inc(lam_ready, 1)
            dve.wait_ge(consts, 1)
            step(d.tensor_copy(pos_f[:], pos_i[:]))
            for t in range(NT):
                step(d.tensor_scalar(ang[:, 0, t, :], inv_f[:], pos_f[:, t:t + 1], None, ALU.mult))
            two_pi = 2 * math.pi
            c1 = 6.28125
            c2 = float(np.float32(np.float64(two_pi - c1) * 2 ** 20 // 1 / 2 ** 20))
            c3 = float(np.float32(two_pi - c1 - c2))
            magic = float(3 * 2 ** 22)
            for w, shift in ((1, 0.0), (2, 0.25)):
                turn = rot[:, w, 0:NT, :]
                step(d.tensor_scalar(turn, ang[:, 0], 1.0 / two_pi, shift, ALU.mult, ALU.add))
                step(d.tensor_scalar(turn, turn, magic, None, ALU.add))
                step(d.tensor_scalar(turn, turn, magic, None, ALU.subtract))
                prev = ang[:, 0]
                for c in (c1, c2, c3):
                    step(d.scalar_tensor_tensor(out=ang[:, w], in0=turn, scalar=-c, in1=prev, op0=ALU.mult,
                                                op1=ALU.add))
                    prev = ang[:, w]
                if w == 2:
                    step(d.tensor_scalar(ang[:, w], ang[:, w], math.pi / 2, None, ALU.add))
                ins = d.tensor_scalar(ang[:, w], ang[:, w], 3.1415925, -3.1415925, ALU.min, ALU.max)
                if w == 2:
                    ins.then_inc(ang_ready, 1)
                else:
                    step(ins)
            dve.wait_ge(lam_exp, 1)
            step(d.tensor_tensor(lam[:, 4:5], lam[:, 3:4], lam[:, 2:3], ALU.subtract))
            step(d.tensor_scalar(lam[:, 5:6], lam[:, 4:5], LAM_INIT, None, ALU.subtract))
            neg_lam = lam[:, 5:6]

            split_until(P_A + 3)
            for p in range(P_A, P_OUT0):
                take(p)
                split_until(min(p + 4, P_OUT0 + 3))

            dve.wait_ge(fl_ready, 1)
            for t in range(NT):
                step(d.tensor_tensor(fg[:, 0, t, :], bank[3][:, FOX_H * t:FOX_H * (t + 1)], b_f[:], ALU.add))
            step(d.tensor_scalar(fg[:, 2], fg[:, 0], -1.0, None, ALU.mult))
            d.tensor_tensor(fg[:, 1], fg[:, 0], fg[:, 2], ALU.min).then_inc(fl_sum, 1)
            dve.wait_ge(fl_ln, 1)
            dve.wait_ge(fl_sum, 1)
            d.scalar_tensor_tensor(out=fg[:, 2], in0=fg[:, 0], scalar=0.0, in1=fg[:, 1], op0=ALU.min,
                                   op1=ALU.subtract).then_inc(logf_ready, 1)
            dve.wait_ge(cum_ready, 1)
            d.tensor_scalar(ncum[:], bank[3][0:FOX_H, 256:512], -1.0, None, ALU.mult).then_inc(ncum_ready, 1)

            def attention_dve(layer):
                scores, outs, last = attention_plan(layer)
                sb0, rb0 = S_BASE[layer], R_BASE[layer]
                done = [0]

                def maxima(upto):
                    while done[0] <= min(upto, len(scores) - 1):
                        s = done[0]
                        g = sb0 + s
                        dve.wait_ge(score_ready, g + 1)
                        w0 = P if scores[s][0] != "mem" else MEM
                        d.tensor_reduce(negm[:, g, 0:1], bank[s % 3][:, 0:w0], AX.X, ALU.max, negate=True)
                        d.tensor_reduce(negm[:, g, 1:2], bank[s % 3][:, w0:w0 + MEM], AX.X, ALU.max,
                                        negate=True).then_inc(rowmax, 1)
                        done[0] += 1

                def fill(r):
                    kind, h = outs[r]
                    if kind == "diff":
                        dve.wait_ge(pv_ready, rb0 + r + 1)
                        d.tensor_copy(tok[:, :, DV * h:DV * (h + 1)],
                                      bank[5 + r % 2][:, 0:256].rearrange("p (t n) -> p t n", t=NT)).then_inc(o_out, 1)
                        return
                    if h % 2 == 0:
                        return
                    c = h // 2 + (6 if kind == "mem" else 0)
                    base = int(FILL[2] if layer == 0 else FILL[6])
                    dve.wait_ge(fill_hi, base + (c + 1 if layer == 0 else c - 5))
                    d.tensor_tensor(op_lo[1][:, c, :], bank[5 + (r // 2) % 2][:, 0:SEQ],
                                    op_hi[1][:, c, :].bitcast(F32), ALU.subtract).then_inc(fill_lo, 1)

                for r in range(len(outs)):
                    maxima((last[r - 1] if r else -1) + 3)
                    kind, h = outs[r]
                    s = last[r]
                    g = sb0 + s
                    dve.wait_ge(exp_done, g + 1)
                    w0 = P if kind != "mem" else MEM
                    if kind == "diff":
                        step(d.reciprocal(rinv[:, g - 1:g + 1, :], rsum[:, g - 1:g + 1, :]))
                        step(d.tensor_scalar(rinv[:, g, :], rinv[:, g, :], neg_lam, None, ALU.mult))
                        p1, p2 = prob[(s - 1) % 3], prob[s % 3]
                        for t, (c, w) in enumerate(((0, P), (P, MEM))):
                            step(d.tensor_scalar(p1[:, c:c + w], p1[:, c:c + w], rinv[:, g - 1, t:t + 1], None,
                                                 ALU.mult))
                            ins = d.scalar_tensor_tensor(out=p1[:, c:c + w], in0=p2[:, c:c + w],
                                                         scalar=rinv[:, g, t:t + 1], in1=p1[:, c:c + w],
                                                         op0=ALU.mult, op1=ALU.add)
                        ins.then_inc(prob_ready, 1)
                    else:
                        step(d.reciprocal(rinv[:, g, :], rsum[:, g, :]))
                        pr = prob[s % 3]
                        d.tensor_scalar(pr[:, 0:w0], pr[:, 0:w0], rinv[:, g, 0:1], None, ALU.mult)
                        d.tensor_scalar(pr[:, w0:w0 + MEM], pr[:, w0:w0 + MEM], rinv[:, g, 1:2], None,
                                        ALU.mult).then_inc(prob_ready, 1)
                    if r:
                        fill(r - 1)
                fill(len(outs) - 1)

            attention_dve(0)
            split_until(P_KV)
            for p in range(P_OUT0, P_KV):
                take(p)
                if p in (P_OUT0 + 1, P_OUT0 + 2):
                    split_lo(U_FFN + p - P_OUT0 - 1)
            dve.wait_ge(proj_out, P_KV)
            norm_dve(3, X, 4)
            norm_fill_lo(3)

            def ffn_mul(j, turns=0, moved=0):
                dve.wait_ge(unit_used, U_FFN + ffn_pos("U", j) + 1 + RAW * turns)
                dve.wait_ge(silu_done, j + 1 + moved)
                if j:
                    dve.wait_ge(h2_lo, j + moved)
                d.tensor_tensor(h2[j % 2][:], gate_act[j % 2][:], bank[5 + 2 * (j % 2)][:],
                                ALU.mult).then_inc(mul_done, 1)

            def ffn_h2_lo(j, moved=0):
                dve.wait_ge(h2_hi, j + 1 + moved)
                d.tensor_tensor(h2T_lo[j % 2][:], h2[j % 2][:], h2T_hi[j % 2][:].bitcast(F32),
                                ALU.subtract).then_inc(h2_lo, 1)

            ffn_mul(0)
            with dve.Fori(0, (FFN_STEPS - 1) // 2) as it:
                for j in (1, 2):
                    split_lo(U_FFN + ffn_pos("G", j), it)
                    ffn_h2_lo(j - 1, 2 * it)
                    split_lo(U_FFN + ffn_pos("U", j), it)
                    split_lo(U_FFN + ffn_pos("D", j - 1), it)
                    ffn_mul(j, it, 2 * it)
            split_lo(U_FFN + FFN_UNITS - 1)
            ffn_h2_lo(FFN_STEPS - 1)
            split_lo(U_KV)
            split_lo(U_KV + 1)
            dve.wait_ge(unit_used, U_KV)
            for t in range(NT):
                for h in range(2):
                    cols = slice(512 * h, 512 * (h + 1))
                    d.tensor_tensor(X[:, t, cols], X[:, t, cols], bank[2 * t + h][:], ALU.add).then_inc(x_added, 1)
            dve.wait_ge(x_added, 4)
            norm_dve(4, X, 5)
            norm_fill_lo(4)

            def rotate(count):
                for t in range(NT):
                    heads = tok[:, t, 0:FOX_W].rearrange("p (h n) -> p h n", n=HD)
                    x1, x2 = heads[:, :, 0:HALF], heads[:, :, HALF:ROT]
                    cos = cosv[:, t:t + 1, :].to_broadcast([P, 12, HALF])
                    sin = sinv[:, t:t + 1, :].to_broadcast([P, 12, HALF])
                    for i, (a, b) in enumerate(((x1, cos), (x2, sin), (x2, cos), (x1, sin))):
                        ins = d.tensor_tensor(rot[:, i], a, b, ALU.mult)
                        step(ins)
                    step(d.tensor_tensor(x1, rot[:, 0], rot[:, 1], ALU.subtract))
                    ins = d.tensor_tensor(x2, rot[:, 2], rot[:, 3], ALU.add)
                    if t == NT - 1:
                        ins.then_inc(rot_ready, 1)
                        dve.wait_ge(rot_ready, count)
                    else:
                        step(ins)

            for u in range(2, 6):
                split_lo(U_KV + u)
            for p in range(P_KV, P_KV + 3):
                take(p)
            dve.wait_ge(proj_out, P_KV + 3)
            dve.wait_ge(sin_ready, 1)
            rotate(1)

            def qk_take(first, dst):
                for b in range(3):
                    dve.wait_ge(qk_tr, first + b + 1)
                    d.tensor_copy(dst[:, 2 * b:2 * b + 2, :],
                                  bank[b][:].rearrange("p (c n) -> p c n", c=2)).then_inc(qk_out, 1)

            for p in range(P_KV + 3, P_QB):
                take(p)
                split_lo(U_KV + 6 + p - P_KV - 3)
            qk_take(0, kT)
            norm_dve(5, X, 6)
            norm_fill_lo(5)
            split_lo(U_KV + 9)
            for p in range(P_QB, P_OUT1):
                take(p)
                if p > P_QB:
                    split_lo(U_KV + 10 + p - P_QB - 1)
            dve.wait_ge(proj_out, P_OUT1)
            rotate(2)
            qk_take(3, qT)
            attention_dve(1)

            dve.wait_ge(o_out, DIFF_H)
            o4 = tok[:, :, 0:FOX_W].rearrange("p t (h n) -> p t h n", n=DV)
            sq4 = hn[:, :, 0:FOX_W].rearrange("p t (h n) -> p t h n", n=DV)
            for t in range(NT):
                step(d.tensor_tensor(sq4[:, t], o4[:, t], o4[:, t], ALU.mult))
                step(d.tensor_reduce(o_ss[:, 0, DIFF_H * t:DIFF_H * (t + 1)], sq4[:, t], AX.X, ALU.add))
            d.tensor_scalar(o_ss[:, 1], o_ss[:, 0], 1.0 / DV, EPS, ALU.mult, ALU.add).then_inc(norm_var, 1)
            dve.wait_ge(norm_std, 7)
            step(d.reciprocal(o_ss[:, 3], o_ss[:, 2]))
            for t in range(NT):
                g = subln[:].unsqueeze(1).to_broadcast([P, DIFF_H, DV])
                step(d.scalar_tensor_tensor(out=o4[:, t], in0=o4[:, t], scalar=1.0 - LAM_INIT, in1=g,
                                            op0=ALU.mult, op1=ALU.mult))
                r = o_ss[:, 3, DIFF_H * t:DIFF_H * (t + 1)].unsqueeze(2).to_broadcast([P, DIFF_H, DV])
                d.tensor_tensor(o4[:, t], o4[:, t], r, ALU.mult).then_inc(o_norm, 1)
            for b in range(3):
                dve.wait_ge(fill_hi, int(FILL[6]) + 3 + b)
                d.tensor_tensor(op_lo[1][:, 2 * b:2 * b + 2, :], bank[b][:].rearrange("p (c n) -> p c n", c=2),
                                op_hi[1][:, 2 * b:2 * b + 2, :].bitcast(F32), ALU.subtract).then_inc(fill_lo, 1)
            split_lo(U_KV + 13)
            for p in range(P_OUT1, P_END):
                take(p)
            dve.wait_ge(proj_out, P_END)
            norm_dve(6, X, 8)
            norm_fill_lo(6)

            dve.wait_ge(logit_ready, 1)
            step(d.tensor_copy(lg[:], bank[4][:, 0:NT * N_EXP].rearrange("p (t n) -> p t n", t=NT)))
            for t in range(NT):
                step(d.max(out=top[:, t, :], in_=lg[:, t, :]))
                step(d.max_index(out=top_i[:, t, :], in_max=top[:, t, :], in_values=lg[:, t, :]))
            step(d.tensor_copy(top_f[:], top_i[:]))
            d.tensor_tensor(gates[:, :, 0], top[:, :, 1], top[:, :, 0], ALU.subtract).then_inc(top_ready, 1)
            for t in range(NT):
                for i in range(2):
                    step(d.tensor_scalar(oh[:, i, t, :], iota8[:], top_f[:, t, i:i + 1], None, ALU.is_equal))
            step(d.tensor_tensor(member[:, :, 0:N_EXP], oh[:, 0], oh[:, 1], ALU.add))
            d.tensor_copy(member_bf[:], member[:, :, 0:N_EXP]).then_inc(member_ready, 1)
            dve.wait_ge(gate_exp, 1)
            step(d.tensor_scalar(gates[:, :, 2], gates[:, :, 1], 1.0, None, ALU.add))
            step(d.reciprocal(gates[:, :, 2], gates[:, :, 2]))
            step(d.tensor_tensor(gates[:, :, 3], gates[:, :, 1], gates[:, :, 2], ALU.mult))
            for t in range(NT):
                step(d.tensor_scalar(comb[:, t, :], oh[:, 0, t, :], gates[:, t, 2:3], None, ALU.mult))
                step(d.scalar_tensor_tensor(out=comb[:, t, :], in0=oh[:, 1, t, :], scalar=gates[:, t, 3:4],
                                            in1=comb[:, t, :], op0=ALU.mult, op1=ALU.add))
            dve.wait_ge(rank_ready, 1)
            step(d.tensor_scalar(rank[:, :, 0:N_EXP], bank[4][:, 32:32 + NT * N_EXP].rearrange("p (t n) -> p t n", t=NT),
                                 1.0, None, ALU.subtract))
            step(d.tensor_reduce(over[:, 0:1], bank[4][:, 64:64 + N_EXP], AX.X, ALU.max))
            step(d.tensor_scalar(over[:, 1:2], over[:, 0:1], float(P), None, ALU.is_gt))
            d.tensor_copy(over_i[:], over[:, 1:2]).then_inc(route_ready, 1)

            def experts_dve(ps):
                ub = U_MOE + ps * N_EXP * MOE_UNITS
                tb = 2 * (ps + 1) + TB * N_EXP * ps
                hb = FFN_STEPS + MOE_STEPS * N_EXP * ps
                xb = 2 * (N_EXP + 1) * ps
                ab = 4 + 4 * N_EXP * ps

                def one_hot(e):
                    for t in range(NT):
                        ins = d.tensor_scalar(slot_oh[:, t, :], slot_no[:, P * ps:P * (ps + 1)],
                                              rank[:, t, bass.ds(e, 1)], member[:, t, bass.ds(e, 1)],
                                              ALU.is_equal, ALU.mult)
                    ins.then_inc(oh_ready, 1)

                def gathered_lo(count):
                    for i in range(2):
                        dve.wait_ge(xg_hi_ready, count + i + 1)
                        d.tensor_tensor(xg_lo[:, 4 * i:4 * i + 4, 0:P],
                                        bank[7 - i][:].rearrange("p (c n) -> p c n", c=4),
                                        xg_hi[:, 4 * i:4 * i + 4, 0:P].bitcast(F32),
                                        ALU.subtract).then_inc(xg_lo_ready, 1)

                one_hot(0)
                gathered_lo(xb)
                with dve.Fori(0, N_EXP) as e:
                    turns = (MOE_UNITS // RAW) * e

                    def lo(kind, j, k):
                        split_lo(ub + moe_pos(kind, j, k), turns)

                    def evac_T(j):
                        dve.wait_ge(h2_hi, hb + MOE_STEPS * e + j + 1)
                        d.tensor_tensor(h2T_lo[j % 2][:], bank[7 - j % 2][:], h2T_hi[j % 2][:].bitcast(F32),
                                        ALU.subtract).then_inc(h2_lo, 1)

                    for j in range(MOE_STEPS):
                        lo("G", j, 0)
                        lo("G", j, 1)
                        lo("U", j, 0)
                        if j:
                            evac_T(j - 1)
                        lo("U", j, 1)
                        if j == 3:
                            dve.wait_ge(tb_ready, tb + TB * e + 1)
                            one_hot(e + 1)
                        if j:
                            lo("D", j - 1, 0)
                            lo("D", j - 1, 1)
                        dve.wait_ge(unit_used, ub + moe_pos("U", j, 1) + 1 + MOE_UNITS * e)
                        dve.wait_ge(silu_done, hb + MOE_STEPS * e + j + 1)
                        dve.wait_ge(tb_ready, tb + TB * e + j)
                        d.tensor_tensor(h2[j % 2][:], gate_act[j % 2][:], bank[3 + 2 * (j % 2)][:],
                                        ALU.mult).then_inc(mul_done, 1)
                    lo("D", MOE_STEPS - 1, 0)
                    lo("D", MOE_STEPS - 1, 1)
                    gathered_lo(xb + 2 + 2 * e)
                    evac_T(MOE_STEPS - 1)
                    dve.wait_ge(unit_used, ub + MOE_UNITS + MOE_UNITS * e)
                    d.tensor_copy(ye[:, 512:1024], bank[1][:]).then_inc(ye_dve, 1)
                    for i in range(4):
                        t, h = i // 2, i % 2
                        cols = slice(512 * h, 512 * (h + 1))
                        dve.wait_ge(tb_ready, tb + TB * e + 11 + i)
                        dve.wait_ge(x_added, ab + 4 * e)
                        d.scalar_tensor_tensor(out=X[:, t, cols], in0=bank[6 + i % 2][:],
                                               scalar=comb[:, t, bass.ds(e, 1)], in1=X[:, t, cols],
                                               op0=ALU.mult, op1=ALU.add).then_inc(x_added, 1)
                dve.wait_ge(x_added, ab + 4 * N_EXP)

            experts_dve(0)
            dve.wait_ge(route_ready, 1)
            flag = dve.value_load(over_i[0:1, 0:1], min_val=0, max_val=1)
            with dve.If(flag == 1):
                experts_dve(1)
            d.memset(over[:, 1:2], 0.0).then_inc(x_final, 1)
            norm_dve(7, X, 9)

        @block.tensor
        def _(pe):
            m = nc.tensor

            def product(dst, pairs, start=True, stop=True):
                n = len(pairs)
                for i, ((sh, sl), (mh, ml)) in enumerate(pairs):
                    m.matmul(dst, sh, mh, start=start and i == 0, stop=False)
                    m.matmul(dst, sh, ml, start=False, stop=False)
                    last = m.matmul(dst, sl, mh, start=False, stop=stop and i == n - 1)
                return last

            def norm_transposes(n):
                if n:
                    pe.wait_ge(fill_lo, int(FILL[NORM_FILL[n] - 1]))
                for g in range(4):
                    t, h = g // 2, g % 2
                    pe.wait_ge(hn_ready, 2 * n + t + 1)
                    for c in range(4):
                        k = 4 * h + c
                        last = m.transpose(bank[g][:, P * c:P * (c + 1)], hn[:, t, P * k:P * (k + 1)], ident[:])
                    last.then_inc(tr_ready, 1)

            def project(p):
                what, _ = PROJ[p]
                f = fill_of(p)
                hi, lo = op_hi[FILL_BUF[f]], op_lo[FILL_BUF[f]]
                u = unit_of(p)
                pe.wait_ge(fill_lo, int(FILL[f]))
                pe.wait_ge(lo_ready, u + 1)
                if p >= 4:
                    pe.wait_ge(proj_out, p - 3)
                wh, wl = wide(whi, u % SPLIT), wide(wlo, u % SPLIT)
                b = bank[4 + p % 4]
                for c in range(2):
                    dst = b[:, WIDE * c:WIDE * (c + 1)]
                    sl = slice(P * c, P * (c + 1))
                    if what in ("mk", "q", "k", "qm"):
                        last = product(dst, [((wh[:, k, sl], wl[:, k, sl]), (hi[:, k, :], lo[:, k, :]))
                                             for k in range(KC)])
                    else:
                        last = product(dst, [((hi[:, k, sl], lo[:, k, sl]), (wh[:, k, :], wl[:, k, :]))
                                             for k in range(KC)])
                last.then_inc(unit_used, 1)

            def small_product(dst, f, lo_col, hi_col):
                hi, lo = op_hi[FILL_BUF[f]], op_lo[FILL_BUF[f]]
                n = hi_col - lo_col
                for t in range(NT):
                    sl = slice(P * t, P * (t + 1))
                    last = product(dst[:, n * t:n * (t + 1)],
                                   [((hi[:, k, sl], lo[:, k, sl]),
                                     (small_hi[:, k, lo_col:hi_col], small_lo[:, k, lo_col:hi_col]))
                                    for k in range(KC)])
                return last

            def attention_pe(layer):
                scores, outs, last_s = attention_plan(layer)
                sb0, rb0 = S_BASE[layer], R_BASE[layer]
                done = [0]

                def score(s):
                    kind, h = scores[s]
                    g = sb0 + s
                    if s >= 3:
                        pe.wait_ge(exp_done, g - 2)
                    b = bank[s % 3]
                    po, c = HD * (h % 2), h // 2
                    for t in range(NT):
                        sl = slice(P * t, P * (t + 1))
                        if kind == "mem":
                            mm = m.matmul(b[:, MEM * t:MEM * (t + 1)], qmT[po:po + HD, c, sl],
                                          mkT[layer][po:po + HD, c, :], start=True, stop=True)
                            continue
                        w = P * (t + 1)
                        o0 = P * t
                        m.matmul(b[:, o0:o0 + w], qT[po:po + HD, c, sl], kT[po:po + HD, c, 0:w], start=True,
                                 stop=False)
                        if kind == "fox":
                            m.matmul(b[:, o0:o0 + w], ident[0:FOX_H, h:h + 1].to_broadcast([FOX_H, P]),
                                     ncum[:, 0:w], start=False, stop=False)
                        mask = causal if kind == "fox" else chunked
                        mm = m.matmul(b[:, o0 + w - P:o0 + w], ident_bf[:], mask[:], start=False, stop=True)
                    mm.then_inc(score_ready, 1)

                def scores_until(upto):
                    while done[0] <= min(upto, len(scores) - 1):
                        score(done[0])
                        done[0] += 1

                def transposes(r):
                    kind, h = outs[r]
                    g = rb0 + r
                    pe.wait_ge(prob_ready, g + 1)
                    if g >= 2:
                        pe.wait_ge(pT_out, g - 1)
                    src = prob[(last_s[r] - (kind == "diff")) % 3]
                    b = bank[3 + r % 2]
                    for i in range(4 if kind == "mem" else 3):
                        j = 2 * (i % 2) + i // 2 if kind == "mem" else i
                        tr = m.transpose(b[:, P * j:P * (j + 1)], src[:, P * i:P * (i + 1)], ident[:])
                    tr.then_inc(pT_ready, 1)

                def values(r):
                    kind, h = outs[r]
                    g = rb0 + r
                    pe.wait_ge(pT_out, g + 1)
                    pT = probT[r % 2]
                    if kind == "diff":
                        if r >= 2:
                            pe.wait_ge(o_out, r - 1)
                        b = bank[5 + r % 2]
                        cols = slice(DV * h, DV * (h + 1))
                        m.matmul(b[:, 0:P], pT[:, 0:P], v[:, 0, cols], start=True, stop=True)
                        m.matmul(b[:, P:2 * P], pT[:, P:2 * P], v[:, 0, cols], start=True, stop=False)
                        mm = m.matmul(b[:, P:2 * P], pT[:, 2 * P:3 * P], v[:, 1, cols], start=False, stop=True)
                    else:
                        pair = r // 2
                        if layer == 0 and pair >= 2:
                            pe.wait_ge(fill_lo, int(FILL[2]) + pair - 1)
                        if layer == 1:
                            pe.wait_ge(o_out, DIFF_H)
                        b = bank[5 + pair % 2]
                        po = HD * (h % 2)
                        cols = slice(HD * h, HD * (h + 1))
                        val = v if kind == "fox" else mv[layer]
                        m.matmul(b[po:po + HD, 0:SEQ], val[:, 0, cols], pT[:, 0:SEQ], start=True, stop=False)
                        if kind == "fox":
                            mm = m.matmul(b[po:po + HD, P:SEQ], val[:, 1, cols], pT[:, 2 * P:3 * P], start=False,
                                          stop=True)
                        else:
                            mm = m.matmul(b[po:po + HD, 0:SEQ], val[:, 1, cols], pT[:, SEQ:2 * SEQ], start=False,
                                          stop=True)
                    mm.then_inc(pv_ready, 1)

                scores_until(2)
                for r in range(len(outs)):
                    transposes(r)
                    if r:
                        values(r - 1)
                    scores_until(last_s[r] + 3)
                values(len(outs) - 1)

            pe.wait_ge(consts, 1)
            norm_transposes(0)
            project(0)
            project(1)
            norm_transposes(1)
            project(2)
            project(3)
            norm_transposes(2)
            for p in range(P_A, P_OUT0):
                project(p)
            pe.wait_ge(small_lo_ready, 1)
            pe.wait_ge(small_hi_ready, 1)
            small_product(bank[3], 2, 0, FOX_H).then_inc(fl_ready, 1)
            pe.wait_ge(logf_ready, 1)
            m.matmul(bank[3][0:FOX_H, 256:512], fg[:, 2, 0, :], upper[:], start=True, stop=False)
            m.matmul(bank[3][0:FOX_H, 384:512], fg[:, 2, 1, :], upper[:, 0:P], start=False,
                     stop=True).then_inc(cum_ready, 1)
            pe.wait_ge(ncum_ready, 1)
            pe.wait_ge(proj_out, P_OUT0)
            attention_pe(0)
            for p in range(P_OUT0, P_KV):
                project(p)
            norm_transposes(3)
            pe.wait_ge(fill_lo, int(FILL[4]))
            pe.wait_ge(proj_out, P_KV)

            hi, lo = op_hi[0], op_lo[0]

            def ffn_up(kind, j, it=0):
                c = U_FFN + ffn_pos(kind, j)
                pe.wait_ge(lo_ready, c + RAW * it + 1)
                wh, wl = wide(whi, c % SPLIT), wide(wlo, c % SPLIT)
                b = bank[4 + 2 * (j % 2) + (kind == "U")]
                for c2 in range(2):
                    sl = slice(P * c2, P * (c2 + 1))
                    last = product(b[:, WIDE * c2:WIDE * (c2 + 1)],
                                   [((wh[:, k, sl], wl[:, k, sl]), (hi[:, k, :], lo[:, k, :])) for k in range(KC)])
                last.then_inc(unit_used, 1)

            def ffn_down(j, it=0, moved=0, first=False, final=False):
                c = U_FFN + ffn_pos("D", j)
                pe.wait_ge(h2_lo, j + 1 + moved)
                pe.wait_ge(lo_ready, c + RAW * it + 1)
                wh = whi[:, c % SPLIT, :].rearrange("p (k n) -> p k n", k=2)
                wl = wlo[:, c % SPLIT, :].rearrange("p (k n) -> p k n", k=2)
                for t in range(NT):
                    for h in range(2):
                        cols = slice(512 * h, 512 * (h + 1))
                        sls = [slice(WIDE * k + P * t, WIDE * k + P * (t + 1)) for k in range(2)]
                        last = product(bank[2 * t + h][:],
                                       [((h2T_hi[j % 2][:, s], h2T_lo[j % 2][:, s]), (wh[:, k, cols], wl[:, k, cols]))
                                        for k, s in enumerate(sls)], start=first, stop=final)
                last.then_inc(unit_used, 1)

            def ffn_pair(it, first=False):
                for j in (1, 2):
                    if j == 2 or not first:
                        pe.wait_ge(mul_done, j - 1 + 2 * it)
                    ffn_up("G", j, it)
                    ffn_up("U", j, it)
                    ffn_down(j - 1, it, 2 * it, first=first and j == 1)

            ffn_up("G", 0)
            ffn_up("U", 0)
            ffn_pair(0, first=True)
            with pe.Fori(1, (FFN_STEPS - 1) // 2) as it:
                ffn_pair(it)
            ffn_down(FFN_STEPS - 1, 0, 0, final=True)

            def tok_transposes(ready, val, sem_out):
                pe.wait_ge(ready, val)
                for b in range(3):
                    for c in range(2):
                        for t in range(NT):
                            k = 2 * b + c
                            last = m.transpose(bank[b][:, WIDE * c + P * t:WIDE * c + P * (t + 1)],
                                               tok[:, t, P * k:P * (k + 1)], ident[:])
                    last.then_inc(sem_out, 1)

            norm_transposes(4)
            for p in range(P_KV, P_QB):
                project(p)
            tok_transposes(rot_ready, 1, qk_tr)
            pe.wait_ge(qk_out, 3)
            norm_transposes(5)
            for p in range(P_QB, P_OUT1):
                project(p)
            tok_transposes(rot_ready, 2, qk_tr)
            pe.wait_ge(qk_out, 6)
            pe.wait_ge(proj_out, P_OUT1)
            attention_pe(1)
            tok_transposes(o_norm, 2, o_tr)
            for p in range(P_OUT1, P_END):
                project(p)
            norm_transposes(6)
            pe.wait_ge(fill_lo, int(FILL[8]))
            pe.wait_ge(proj_out, P_END)
            small_product(bank[4], 8, FOX_H, FOX_H + N_EXP).then_inc(logit_ready, 1)
            pe.wait_ge(member_ready, 1)
            b = bank[4]
            m.matmul(b[:, 32:40], upper_bf[:], member_bf[:, 0, :], start=True, stop=True)
            m.matmul(b[:, 40:48], ones_bf[:], member_bf[:, 0, :], start=True, stop=False)
            m.matmul(b[:, 40:48], upper_bf[:], member_bf[:, 1, :], start=False, stop=True)
            m.matmul(b[:, 64:72], ones_bf[:], member_bf[:, 0, :], start=True, stop=False)
            m.matmul(b[:, 64:72], ones_bf[:], member_bf[:, 1, :], start=False, stop=True).then_inc(rank_ready, 1)
            pe.wait_ge(route_ready, 1)

            def experts_pe(ps):
                ub = U_MOE + ps * N_EXP * MOE_UNITS
                hb = FFN_STEPS + MOE_STEPS * N_EXP * ps
                xb = 2 * (N_EXP + 1) * ps
                ab = 4 + 4 * N_EXP * ps
                ob = (N_EXP + 1) * ps
                eb = N_EXP * ps

                def gather(waits):
                    for i in range(2):
                        for s, val in waits[i]:
                            pe.wait_ge(s, val)
                        for c in range(4):
                            k = 4 * i + c
                            for t in range(NT):
                                last = m.matmul(bank[7 - i][:, P * c:P * (c + 1)], hn[:, t, P * k:P * (k + 1)],
                                                slot_oh[:, t, :], start=t == 0, stop=t == NT - 1)
                        last.then_inc(tb_ready, 1)

                gather([[(oh_ready, ob + 1)], []])
                with pe.Fori(0, N_EXP) as e:
                    def up(kind, j, a):
                        c = ub + moe_pos(kind, j, a)
                        pe.wait_ge(lo_ready, c + MOE_UNITS * e + 1)
                        wh = whi[:, c % SPLIT, :].rearrange("p (k n) -> p k n", k=4)
                        wl = wlo[:, c % SPLIT, :].rearrange("p (k n) -> p k n", k=4)
                        product(bank[2 + 2 * (j % 2) + (kind == "U")][:],
                                [((xg_hi[:, 4 * a + k, 0:P], xg_lo[:, 4 * a + k, 0:P]), (wh[:, k, :], wl[:, k, :]))
                                 for k in range(4)], start=a == 0, stop=a == 1).then_inc(unit_used, 1)

                    def down(j, a):
                        c = ub + moe_pos("D", j, a)
                        pe.wait_ge(h2_lo, hb + MOE_STEPS * e + j + 1)
                        pe.wait_ge(lo_ready, c + MOE_UNITS * e + 1)
                        wh = whi[:, c % SPLIT, :].rearrange("p (k n) -> p k n", k=2)
                        wl = wlo[:, c % SPLIT, :].rearrange("p (k n) -> p k n", k=2)
                        for h in range(2):
                            cols = slice(512 * h, 512 * (h + 1))
                            sls = [slice(P * (2 * a + k), P * (2 * a + k + 1)) for k in range(2)]
                            last = product(bank[h][:],
                                           [((h2T_hi[j % 2][:, s], h2T_lo[j % 2][:, s]),
                                             (wh[:, k, cols], wl[:, k, cols])) for k, s in enumerate(sls)],
                                           start=j == 0 and a == 0, stop=j == MOE_STEPS - 1 and a == 1)
                        last.then_inc(unit_used, 1)

                    def h2_transposes(j):
                        pe.wait_ge(mul_done, hb + MOE_STEPS * e + j + 1)
                        if j == 1:
                            pe.wait_ge(ohT_out, eb + e + 1)
                        elif 2 <= j < MOE_STEPS - 1:
                            pe.wait_ge(h2_lo, hb + MOE_STEPS * e + j - 1)
                        elif j == MOE_STEPS - 1:
                            pe.wait_ge(xg_lo_ready, xb + 2 * e + 3)
                        for c in range(4):
                            last = m.transpose(bank[7 - j % 2][:, P * c:P * (c + 1)],
                                               h2[j % 2][:, P * c:P * (c + 1)], ident[:])
                        last.then_inc(tb_ready, 1)

                    pe.wait_ge(xg_lo_ready, xb + 2 * e + 2)
                    for j in range(MOE_STEPS):
                        pe.wait_ge(mul_done, hb + MOE_STEPS * e + max(j - 1, 0))
                        up("G", j, 0)
                        if j == 0:
                            pe.wait_ge(x_added, ab + 4 * e)
                            pe.wait_ge(oh_ready, ob + e + 1)
                            for t in range(NT):
                                last = m.transpose(bank[6][:, P * t:P * (t + 1)], slot_oh[:, t, :], ident[:])
                            last.then_inc(tb_ready, 1)
                        else:
                            h2_transposes(j - 1)
                        up("G", j, 1)
                        up("U", j, 0)
                        up("U", j, 1)
                        if j:
                            down(j - 1, 0)
                            down(j - 1, 1)
                    gather([[(oh_ready, ob + e + 2), (h2_lo, hb + MOE_STEPS * e + 5)],
                            [(h2_lo, hb + MOE_STEPS * e + 6)]])
                    h2_transposes(MOE_STEPS - 1)
                    down(MOE_STEPS - 1, 0)
                    down(MOE_STEPS - 1, 1)
                    pe.wait_ge(ohT_out, eb + e + 1)
                    pe.wait_ge(ye_act, eb + e + 1)
                    pe.wait_ge(ye_dve, eb + e + 1)
                    for i in range(4):
                        s, val = [(xg_lo_ready, xb + 2 * e + 4), (h2_lo, hb + MOE_STEPS * e + 7),
                                  (x_added, ab + 4 * e + 1), (x_added, ab + 4 * e + 2)][i]
                        pe.wait_ge(s, val)
                        t, h = i // 2, i % 2
                        m.matmul(bank[6 + i % 2][:], slot_ohT[:, P * t:P * (t + 1)], ye[:, 512 * h:512 * (h + 1)],
                                 start=True, stop=True).then_inc(tb_ready, 1)

            experts_pe(0)
            flag = pe.value_load(over_i[0:1, 0:1], min_val=0, max_val=1)
            with pe.If(flag == 1):
                experts_pe(1)


_INS = ["x", "mem", "positions", "mix_norm_g", "ffn_norm_g", "mem_norm_g", "w_mem_kv", "w_out", "w_in_a", "b_forget",
        "w_q_b", "lambda_q1", "lambda_k1", "lambda_q2", "lambda_k2", "subln_g", "kv_norm_g", "w_kv_shared",
        "w_gate_up_dense", "w_down_dense", "w_router", "w_gate_up_moe", "w_down_moe", "final_norm_g"]


def kernel(**inputs):
    import concourse.bacc as _bacc
    from concourse import mybir as _mybir
    from concourse.bass_utils import run_bass_kernel_spmd as _run

    nc = _bacc.Bacc("TRN2", target_bir_lowering=False, num_devices=1, dynamic_dma_scratch_size=8192)
    arrays, args = {}, []
    for name in _INS:
        a = np.ascontiguousarray(inputs[name])
        arrays[f"in_{name}_dram"] = a
        args.append(nc.dram_tensor(f"in_{name}_dram", a.shape, _mybir.dt.from_np(a.dtype), kind="ExternalInput").ap())
    args.append(nc.dram_tensor("out_0_dram", (1, SEQ, D), F32, kind="ExternalOutput").ap())
    build(nc, *args)
    r = _run(nc, [arrays], core_ids=[0])
    return r.results[0]["out_0_dram"]
```

```python
import math
from contextlib import ExitStack

import concourse.bass as bass
from concourse import mybir
import numpy as np

P = 128
F32, F32R, BF16 = mybir.dt.float32, mybir.dt.float32r, mybir.dt.bfloat16
I32, U32 = mybir.dt.int32, mybir.dt.uint32
ALU, ACT, AX = mybir.AluOpType, mybir.ActivationFunctionType, mybir.AxisListType

D, SEQ, MEM = 1024, 256, 256
KC = D // P
NT = SEQ // P
HD = 64
FOX_H, DIFF_H, MEM_H = 12, 6, 4
FOX_W, MEM_W = FOX_H * HD, MEM_H * HD
DV = 2 * HD
D_FF, N_EXP, E_FF = 2816, 8, 3584
ROT = 16
HALF = ROT // 2
THETA = 500000.0
EPS = 1e-5
SCALE = HD ** -0.5
NEG = -1.0e30
LAM_INIT = 0.8 - 0.6 * math.exp(-0.3)

UNIT = 2048
RAW, SPLIT = 6, 3
AHEAD = 4
WIDE = 256

PROJ = ([("mk", 0), ("mv", 0), ("mk", 1), ("mv", 1)]
        + [("q", i) for i in range(3)] + [("k", i) for i in range(3)] + [("v", i) for i in range(3)] + [("qm", 0)]
        + [("out", i) for i in range(4)]
        + [("kd", i) for i in range(3)] + [("qd", i) for i in range(3)]
        + [("vd", i) for i in range(3)] + [("qm", 1)]
        + [("out", i) for i in range(4)])
P_MEM, P_A, P_OUT0, P_KV, P_QD, P_VD, P_OUT1, P_END = 0, 4, 14, 18, 21, 24, 28, 32
FFN_STEPS = D_FF // WIDE
FFN_UNITS = 3 * FFN_STEPS
U_FFN = P_KV
U_KV = U_FFN + FFN_UNITS
U_MOE = U_KV + (P_END - P_KV)
MOE_STEPS = E_FF // 512
MOE_UNITS = 6 * MOE_STEPS
TB_USES = (["T0", "oneT"] + [f"T{j}" for j in range(1, 6)] + ["gather0", "gather1", "T6"]
           + [f"back{i}" for i in range(4)])
TB = len(TB_USES)
FILL = list(np.cumsum([4, 4, 4, 8, 4, 4, 4, 5, 4]))
NORM_FILL = [0, 1, 2, 4, 5, 6, 8]
FILL_BUF = [0, 1, 0, 1, 0, 1, 0, 0, 1]


def unit_of(p):
    return p if p < P_KV else U_KV + p - P_KV


def fill_of(p):
    if P_KV <= p < P_OUT1:
        return 5 if PROJ[p][0] in ("kd", "vd") else 6
    for f, end in ((0, 2), (1, 4), (2, P_OUT0), (3, P_KV), (7, P_END)):
        if p < end:
            return f


def ffn_pos(kind, j):
    if kind == "D":
        return 4 + 3 * j if j < FFN_STEPS - 1 else FFN_UNITS - 1
    base = 0 if j == 0 else 3 * j - 1
    return base + (kind == "U")


def moe_pos(kind, j, a):
    if kind == "D":
        return (8 + 6 * j if j < MOE_STEPS - 1 else MOE_UNITS - 2) + a
    base = 0 if j == 0 else 6 * j - 2
    return base + 2 * (kind == "U") + a


def tb_count(use):
    return TB_USES.index(use) + 1


def tb_bank(use):
    return 6 + tb_count(use) % 2


def attention_plan(layer):
    if layer == 0:
        scores = [("fox", h) for h in range(FOX_H)] + [("mem", h) for h in range(MEM_H)]
        outs, last = scores, list(range(16))
    else:
        scores = [("diff", h) for h in range(2 * DIFF_H)] + [("mem", h) for h in range(MEM_H)]
        outs = [("diff", h) for h in range(DIFF_H)] + [("mem", h) for h in range(MEM_H)]
        last = [2 * r + 1 for r in range(DIFF_H)] + [12 + h for h in range(MEM_H)]
    return scores, outs, last


Y_BUF = [FILL_BUF[3], FILL_BUF[7]]
S_BASE = [0, 16]
R_BASE = [0, 16]


def build(nc, x, mem, positions, mix_norm_g, ffn_norm_g, mem_norm_g, w_mem_kv, w_out, w_in_a, b_forget, w_q_b,
          lambda_q1, lambda_k1, lambda_q2, lambda_k2, subln_g, kv_norm_g, w_kv_shared, w_gate_up_dense,
          w_down_dense, w_router, w_gate_up_moe, w_down_moe, final_norm_g, out):
    with ExitStack() as ctx:
        def sb(name, shape, dt=F32):
            return ctx.enter_context(nc.sbuf_tensor(name, shape, dt))

        def sem(name):
            return ctx.enter_context(nc.semaphore(name))

        raw = sb("raw", [P, RAW, UNIT])
        whi = sb("whi", [P, SPLIT, UNIT], F32R)
        wlo = sb("wlo", [P, SPLIT, UNIT], F32R)
        X = sb("X", [P, NT, D])
        hn = sb("hn", [P, NT, D])
        gain = sb("gain", [P, D])
        op_hi = [sb(f"op_hi{i}", [P, KC, SEQ], F32R) for i in range(2)]
        op_lo = [sb(f"op_lo{i}", [P, KC, SEQ], F32R) for i in range(2)]
        tok = sb("tok", [P, NT, D])
        mkT = [sb(f"mkT{i}", [P, 2, MEM]) for i in range(2)]
        mv = [sb(f"mv{i}", [P, 2, MEM_W]) for i in range(2)]
        qT = sb("qT", [P, 6, SEQ])
        kT = sb("kT", [P, 6, SEQ])
        v = sb("v", [P, NT, FOX_W])
        qmT = sb("qmT", [P, 2, SEQ])
        prob = [sb(f"prob{i}", [P, 512]) for i in range(AHEAD)]
        probT = [sb(f"probT{i}", [P, 512]) for i in range(2)]
        h2T_hi = [sb(f"h2T_hi{i}", [P, 512], F32R) for i in range(2)]
        h2T_lo = [sb(f"h2T_lo{i}", [P, 512], F32R) for i in range(2)]
        gate_act, h2 = prob[0:2], probT[0:2]
        slot_oh = sb("slot_oh", [P, NT, P], F32R)
        slot_ohT = sb("slot_ohT", [P, SEQ], F32R)
        qtok = hn
        small_T = prob[3][0:FOX_H, 0:SEQ]
        hn_hi, hn_lo = (o[0][:].rearrange("p k n -> p (k n)").rearrange("p (t d) -> p t d", t=NT)
                        for o in (op_hi, op_lo))
        xg_hi, xg_lo = op_hi[1][:, :, 0:P], op_lo[1][:, :, 0:P]
        ye_hi, ye_lo = op_hi[1][:, :, P:2 * P], op_lo[1][:, :, P:2 * P]

        ident = sb("ident", [P, P])
        ident_bf = sb("ident_bf", [P, P], BF16)
        upper = sb("upper", [P, SEQ])
        slot_no = upper
        upper_bf = sb("upper_bf", [P, P], BF16)
        ones_bf = sb("ones_bf", [P, P], BF16)
        causal = sb("causal", [P, P], BF16)
        chunked = sb("chunked", [P, P], BF16)
        small_w = sb("small_w", [P, KC, 20])
        small_hi = sb("small_hi", [P, KC, 20], F32R)
        small_lo = sb("small_lo", [P, KC, 20], F32R)
        b_f = sb("b_f", [P, FOX_H])
        subln = sb("subln", [P, DV])
        lam_v = prob[1][:, 0:4 * HD].rearrange("p (a n) -> p a n", a=4)
        lam = sb("lam", [P, 8])
        pos_i = sb("pos_i", [P, NT], I32)
        pos_f = sb("pos_f", [P, NT])
        inv_f = sb("inv_f", [P, HALF])
        ang = sb("ang", [P, 3, NT, HALF])
        cosv = sb("cosv", [P, NT, HALF])
        sinv = sb("sinv", [P, NT, HALF])
        rot = prob[2][:, 0:4 * 12 * HALF].rearrange("p (a h n) -> p a h n", a=4, h=12)
        stat = sb("stat", [P, 8, 4, NT])
        fg = sb("fg", [P, 3, NT, FOX_H])
        ncum = sb("ncum", [FOX_H, SEQ])
        negm = sb("negm", [P, 32, NT])
        rsum = sb("rsum", [P, 32, NT])
        rinv = sb("rinv", [P, 32, NT])
        o_sq = hn[:, :, FOX_W:D].rearrange("p t (i n) -> p i t n", i=2)
        o_ss = sb("o_ss", [P, 4, NT * DIFF_H])
        lg = sb("lg", [P, NT, N_EXP])
        top = sb("top", [P, NT, 8])
        top_i = sb("top_i", [P, NT, 8], U32)
        top_f = sb("top_f", [P, NT, 8])
        gates = sb("gates", [P, NT, 4])
        oh = sb("oh", [P, 2, NT, N_EXP])
        comb = sb("comb", [P, NT, N_EXP])
        member = sb("member", [P, NT, N_EXP + 1])
        member_bf = sb("member_bf", [P, NT, N_EXP], BF16)
        rank = sb("rank", [P, NT, N_EXP + 1])
        iota8 = sb("iota8", [P, N_EXP])
        over = sb("over", [P, 2])
        over_i = sb("over_i", [P, 1], I32)

        bank = [ctx.enter_context(nc.psum_tensor(f"bank{i}", [P, 512], F32)) for i in range(8)]
        score_bank = [bank[0], bank[1], bank[2], bank[7]]

        raw_in = [sem(f"raw_in{i}") for i in range(RAW)]
        hi_ready = sem("hi_ready")
        lo_ready = sem("lo_ready")
        unit_used = sem("unit_used")
        x_in, mem_in, small_in, gain_in = sem("x_in"), sem("mem_in"), sem("small_in"), sem("gain_in")
        consts = sem("consts")
        masks = sem("masks")
        small_hi_ready, small_lo_ready = sem("small_hi_ready"), sem("small_lo_ready")
        norm_ss = sem("norm_ss")
        norm_var = sem("norm_var")
        norm_std = sem("norm_std")
        hn_ready = sem("hn_ready")
        tr_ready = sem("tr_ready")
        fill_hi = sem("fill_hi")
        fill_lo = sem("fill_lo")
        proj_out = sem("proj_out")
        flT_ready, flT_out = sem("flT_ready"), sem("flT_out")
        logitT_ready, logitT_out = sem("logitT_ready"), sem("logitT_out")
        fl_ready, fl_sum, fl_ln, logf_ready = sem("fl_ready"), sem("fl_sum"), sem("fl_ln"), sem("logf_ready")
        cum_ready, ncum_ready = sem("cum_ready"), sem("ncum_ready")
        lam_ready, lam_exp, ang_ready, sin_ready = sem("lam_ready"), sem("lam_exp"), sem("ang_ready"), sem("sin_ready")
        rot_ready = sem("rot_ready")
        qk_tr = sem("qk_tr")
        qk_out = sem("qk_out")
        score_ready = sem("score_ready")
        rowmax = sem("rowmax")
        exp_done = sem("exp_done")
        prob_ready = sem("prob_ready")
        pT_ready = sem("pT_ready")
        pT_out = sem("pT_out")
        pv_ready = sem("pv_ready")
        o_out = sem("o_out")
        o_squared = sem("o_squared")
        o_norm = sem("o_norm")
        o_tr = sem("o_tr")
        silu_done = sem("silu_done")
        mul_done = sem("mul_done")
        h2_hi, h2_lo = sem("h2_hi"), sem("h2_lo")
        x_added = sem("x_added")
        logit_ready, top_ready, gate_exp = sem("logit_ready"), sem("top_ready"), sem("gate_exp")
        member_ready, rank_ready, route_ready = sem("member_ready"), sem("rank_ready"), sem("route_ready")
        oh_ready = sem("oh_ready")
        tb_ready = sem("tb_ready")
        ohT_out = sem("ohT_out")
        xg_hi_ready, xg_lo_ready = sem("xg_hi_ready"), sem("xg_lo_ready")
        ye_hi_ready, ye_lo_ready = sem("ye_hi_ready"), sem("ye_lo_ready")
        hn_hi_ready, hn_lo_ready = sem("hn_hi_ready"), sem("hn_lo_ready")
        slots_ready = sem("slots_ready")
        x_final = sem("x_final")
        out_done = sem("out_done")
        act_step, dve_step = sem("act_step"), sem("dve_step")

        def ss_count(n):
            return n + 1 - (n > 4)

        def rows(w):
            return w.rearrange("(k p) n -> p k n", p=P)

        mem_kv_v = [rows(w_mem_kv[i]) for i in range(2)]
        in_a_v, q_b_v, kv_v = rows(w_in_a[0]), rows(w_q_b[0]), rows(w_kv_shared)
        out_v = [rows(w_out[i]) for i in range(2)]
        gu_v, down_v = rows(w_gate_up_dense[0]), rows(w_down_dense[0])

        def proj_source(p):
            what, i = PROJ[p]
            c = WIDE * i
            if what in ("mk", "mv"):
                c = MEM_W * (what == "mv")
                return mem_kv_v[i][:, :, c:c + WIDE]
            if what in ("q", "k", "v"):
                c += FOX_W * "qkv".index(what)
                return in_a_v[:, :, c:c + WIDE]
            if what == "qm" and i == 0:
                return in_a_v[:, :, 3 * FOX_W + FOX_H:3 * FOX_W + FOX_H + MEM_W]
            if what == "qm":
                return q_b_v[:, :, FOX_W:FOX_W + MEM_W]
            if what == "out":
                return out_v[p >= P_OUT1][:, :, c:c + WIDE]
            if what == "kd":
                return kv_v[:, :, c:c + WIDE]
            if what == "vd":
                return kv_v[:, :, FOX_W + c:FOX_W + c + WIDE]
            return q_b_v[:, :, c:c + WIDE]

        def wide(t3, slot):
            return t3[:, slot, :].rearrange("p (k n) -> p k n", k=KC)

        block = ctx.enter_context(nc.Block())

        @block.sync
        def _(sp):
            def load(c, turns, src, shape):
                if not (isinstance(turns, int) and c + RAW * turns < RAW):
                    sp.wait_ge(lo_ready, c + RAW * turns - RAW + 1)
                dst = raw[:, c % RAW, :].rearrange("p (k n) -> p k n", k=shape)
                sp.dma_start(dst, src).then_inc(raw_in[c % RAW], 16)

            sp.dma_start(tok[:], mem[0].rearrange("(t p) d -> p t d", p=P)).then_inc(mem_in, 16)
            for p in range(P_KV):
                load(unit_of(p), 0, proj_source(p), KC)
                if p == 1:
                    sp.dma_start(X[:], x[0].rearrange("(t p) d -> p t d", p=P)).then_inc(x_in, 16)

            def ffn_load(kind, j, turns=0, moved=0):
                c = U_FFN + ffn_pos(kind, j)
                if kind == "D":
                    src = down_v[:, bass.ds(2 * (j + moved), 2), :]
                    return load(c, turns, src, 2)
                col = (D_FF if kind == "U" else 0) + WIDE * (j + moved)
                load(c, turns, gu_v[:, :, bass.ds(col, WIDE)], KC)

            ffn_load("G", 0)
            ffn_load("U", 0)
            with sp.Fori(0, (FFN_STEPS - 1) // 2) as it:
                for j in (1, 2):
                    ffn_load("G", j, it, 2 * it)
                    ffn_load("U", j, it, 2 * it)
                    ffn_load("D", j - 1, it, 2 * it)
            ffn_load("D", FFN_STEPS - 1)
            for p in range(P_KV, P_END):
                load(unit_of(p), 0, proj_source(p), KC)

            def expert_loads(ps):
                with sp.Fori(0, N_EXP) as e:
                    gu_e = w_gate_up_moe[0].rearrange("e (k p) n -> e p k n", p=P)[bass.ds(e, 1)].squeeze(0)
                    dn_e = w_down_moe[0].rearrange("e (k p) n -> e p k n", p=P)[bass.ds(e, 1)].squeeze(0)
                    base = U_MOE + ps * N_EXP * MOE_UNITS

                    def go(kind, j):
                        for a in range(2):
                            c = base + moe_pos(kind, j, a)
                            if kind == "D":
                                src = dn_e[:, 4 * j + 2 * a:4 * j + 2 * a + 2, :]
                            else:
                                col = (E_FF if kind == "U" else 0) + 512 * j
                                src = gu_e[:, 4 * a:4 * a + 4, col:col + 512]
                            load(c, (MOE_UNITS // RAW) * e, src, 2 if kind == "D" else 4)

                    for j in range(MOE_STEPS):
                        go("G", j)
                        go("U", j)
                        if j:
                            go("D", j - 1)
                    go("D", MOE_STEPS - 1)

            expert_loads(0)
            sp.wait_ge(route_ready, 1)
            flag = sp.value_load(over_i[0:1, 0:1], min_val=0, max_val=1)
            with sp.If(flag == 1):
                expert_loads(1)
            sp.wait_ge(hn_ready, 16)
            sp.dma_start(out[0].rearrange("(t p) d -> p t d", p=P), hn[:]).then_inc(out_done, 16)
            sp.wait_ge(out_done, 16)

        @block.gpsimd
        def _(pool):
            gains = [mem_norm_g[0], mem_norm_g[1], mix_norm_g[0], ffn_norm_g[0], kv_norm_g, mix_norm_g[1],
                     ffn_norm_g[1], final_norm_g]

            def load_gain(n):
                if n:
                    pool.wait_ge(hn_ready, 2 * n)
                g = gains[n].rearrange("(a d) -> a d", a=1)
                pool.dma_start(gain[:], g.to_broadcast([P, D])).then_inc(gain_in, 16)

            load_gain(0)
            smalls = [
                (small_w[:, :, 0:FOX_H], in_a_v[:, :, 3 * FOX_W:3 * FOX_W + FOX_H]),
                (small_w[:, :, FOX_H:20], rows(w_router[0])),
                (b_f[:], b_forget[0:1, :].to_broadcast([P, FOX_H])),
                (subln[:], subln_g[0:1, :].to_broadcast([P, DV])),
                (pos_i[:], positions[0].rearrange("(t p) -> p t", p=P)),
            ] + [(lam_v[:, i, :], l[0:1, :].to_broadcast([P, HD]))
                 for i, l in enumerate((lambda_q1, lambda_k1, lambda_q2, lambda_k2))]
            assert len(smalls) == 9
            with nc.allow_non_contiguous_dma("small columns"):
                for dst, src in smalls:
                    pool.dma_start(dst, src).then_inc(small_in, 16)

            g = nc.gpsimd
            g.memset(ident[:], 0.0).then_inc(masks, 1)
            g.memset(upper[:], 1.0).then_inc(masks, 1)
            g.memset(ones_bf[:], 1.0).then_inc(masks, 1)
            g.memset(causal[:], 0.0).then_inc(masks, 1)
            g.memset(chunked[:], 0.0).then_inc(masks, 1)
            pool.wait_ge(masks, 5)
            g.affine_select(out=ident[:], in_=ident[:], compare_op=ALU.not_equal, fill=1.0, base=0,
                            pattern=[[-1, P]], channel_multiplier=1).then_inc(masks, 1)
            g.affine_select(out=upper[:], in_=upper[:], compare_op=ALU.is_ge, fill=0.0, base=0,
                            pattern=[[1, SEQ]], channel_multiplier=-1).then_inc(masks, 1)
            g.affine_select(out=causal[:], in_=causal[:], compare_op=ALU.is_ge, fill=NEG, base=0,
                            pattern=[[-1, P]], channel_multiplier=1).then_inc(masks, 1)
            g.affine_select(out=chunked[:, HD:P], in_=chunked[:, HD:P], compare_op=ALU.is_ge, fill=NEG, base=-HD,
                            pattern=[[0, HD]], channel_multiplier=1).then_inc(masks, 1)
            pool.wait_ge(masks, 9)
            g.tensor_copy(ident_bf[:], ident[:]).then_inc(masks, 1)
            g.tensor_copy(upper_bf[:], upper[:, 0:P]).then_inc(masks, 1)
            g.iota(iota8[:], pattern=[[1, N_EXP]], base=0, channel_multiplier=0,
                   allow_small_or_imprecise_dtypes=True).then_inc(masks, 1)
            for i in range(HALF):
                f = float(np.float32(THETA) ** np.float32(-(np.float32(i) * np.float32(2.0) / np.float32(ROT))))
                g.memset(inv_f[:, i:i + 1], f).then_inc(masks, 1)
            g.memset(member[:, :, N_EXP:N_EXP + 1], 0.0).then_inc(masks, 1)
            pool.wait_ge(masks, 13 + HALF)
            g.memset(rank[:, :, N_EXP:N_EXP + 1], 0.0).then_inc(consts, 1)
            for n in range(1, 8):
                load_gain(n)
                if n == 3:
                    pool.wait_ge(cum_ready, 1)
                    g.iota(slot_no[:], pattern=[[1, SEQ]], base=0, channel_multiplier=0,
                           allow_small_or_imprecise_dtypes=True).then_inc(slots_ready, 1)

        @block.scalar
        def _(act):
            a = nc.scalar
            own = [0]

            def step(ins):
                own[0] += 1
                ins.then_inc(act_step, 1)
                act.wait_ge(act_step, own[0])

            def split_hi(c, turns=0):
                r = c // RAW + 1 + turns
                act.wait_ge(raw_in[c % RAW], 16 * r)
                if not (isinstance(turns, int) and c + RAW * turns < SPLIT):
                    act.wait_ge(unit_used, c + RAW * turns - SPLIT + 1)
                a.copy(whi[:, c % SPLIT, :], raw[:, c % RAW, :]).then_inc(hi_ready, 1)

            def norm_act(n, src, ready):
                if n:
                    act.wait_ge(tr_ready, 4 * n)
                for s, val in ready:
                    act.wait_ge(s, val)
                for t in range(NT):
                    a.activation(hn[:, t, :], src[:, t, :], ACT.Square,
                                 accum_out=stat[:, n, 0, t:t + 1]).then_inc(norm_ss, 1)
                act.wait_ge(norm_var, ss_count(n) + (n > 4))
                a.activation(stat[:, n, 2, :], stat[:, n, 1, :], ACT.Sqrt).then_inc(norm_std, 1)

            def norm_fill_hi(n):
                if n < 7:
                    buf = op_hi[FILL_BUF[NORM_FILL[n]]]
                    for g in range(4):
                        act.wait_ge(tr_ready, 4 * n + g + 1)
                        t, h = g // 2, g % 2
                        a.copy(buf[:, 4 * h:4 * h + 4, t * P:(t + 1) * P],
                               bank[g][:].rearrange("p (c n) -> p c n", c=4)).then_inc(fill_hi, 1)

            def split_until(n, state=[0]):
                while state[0] < n:
                    split_hi(unit_of(state[0]))
                    state[0] += 1

            norm_act(0, tok, [(mem_in, 16)])
            split_until(2)
            norm_fill_hi(0)
            act.wait_ge(small_in, 16 * 9)
            a.copy(small_hi[:], small_w[:]).then_inc(small_hi_ready, 1)
            split_until(3)
            norm_act(1, tok, [])
            norm_fill_hi(1)
            norm_act(2, X, [(x_in, 16)])
            split_until(5)
            act.wait_ge(unit_used, 2)
            norm_fill_hi(2)
            split_until(P_A + 5)
            act.wait_ge(lam_ready, 1)
            a.activation(lam[:, 2:4], lam[:, 0:2], ACT.Exp).then_inc(lam_exp, 1)
            act.wait_ge(fl_sum, 1)
            step(a.activation(fg[:, 1], fg[:, 1], ACT.Exp))
            a.activation(fg[:, 1], fg[:, 1], ACT.Ln, bias=1.0).then_inc(fl_ln, 1)
            split_until(P_A + 11)
            act.wait_ge(ang_ready, 1)
            a.activation(sinv[:], ang[:, 1], ACT.Sin)
            a.activation(cosv[:], ang[:, 2], ACT.Sin).then_inc(sin_ready, 1)
            split_until(P_OUT0 + 3)

            def attention_act(layer):
                scores, outs, last = attention_plan(layer)
                sb0, rb0 = S_BASE[layer], R_BASE[layer]
                done = [0]

                def exps(upto):
                    while done[0] <= min(upto, len(scores) - 1):
                        s = done[0]
                        g = sb0 + s
                        act.wait_ge(rowmax, g + 1)
                        if s >= AHEAD:
                            owner = min(r for r in range(len(outs)) if last[r] >= s - AHEAD)
                            act.wait_ge(pT_ready, rb0 + owner + 1)
                        elif layer:
                            act.wait_ge(pT_ready, rb0)
                        w0 = P if scores[s][0] != "mem" else MEM
                        w1 = MEM
                        a.activation(prob[s % AHEAD][:, 0:w0], score_bank[s % AHEAD][:, 0:w0], ACT.Exp,
                                     bias=negm[:, g, 0:1], accum_out=rsum[:, g, 0:1])
                        a.activation(prob[s % AHEAD][:, w0:w0 + w1], score_bank[s % AHEAD][:, w0:w0 + w1], ACT.Exp,
                                     bias=negm[:, g, 1:2], accum_out=rsum[:, g, 1:2]).then_inc(exp_done, 1)
                        done[0] += 1

                def fill(r):
                    kind, h = outs[r]
                    if kind == "diff":
                        act.wait_ge(o_out, r + 1)
                        for t in range(NT):
                            ins = a.activation(o_sq[:, r % 2, t, :], tok[:, t, DV * h:DV * (h + 1)], ACT.Square,
                                               accum_out=o_ss[:, 0, DIFF_H * t + h:DIFF_H * t + h + 1])
                        ins.then_inc(o_squared, 1)
                        return
                    if h % 2 == 0:
                        return
                    c = h // 2 + (6 if kind == "mem" else 0)
                    act.wait_ge(pv_ready, rb0 + r + 1)
                    a.copy(op_hi[Y_BUF[layer]][:, c, :], bank[5 + (r // 2) % 2][:, 0:SEQ]).then_inc(fill_hi, 1)

                exps(AHEAD - 1)
                for r in range(len(outs)):
                    w = 512 if outs[r][0] == "mem" else 384
                    act.wait_ge(pT_ready, rb0 + r + 1)
                    if rb0 + r >= 2:
                        act.wait_ge(pv_ready, rb0 + r - 1)
                    a.copy(probT[r % 2][:, 0:w], bank[3 + r % 2][:, 0:w]).then_inc(pT_out, 1)
                    if r:
                        fill(r - 1)
                    exps(last[r] + AHEAD)
                    if layer and r == DIFF_H:
                        act.wait_ge(norm_var, 6)
                        a.activation(o_ss[:, 2], o_ss[:, 1], ACT.Sqrt).then_inc(norm_std, 1)
                fill(len(outs) - 1)

            act.wait_ge(unit_used, 4)
            attention_act(0)
            split_until(P_KV)
            split_hi(U_FFN)
            split_hi(U_FFN + 1)
            norm_act(3, X, [(proj_out, P_KV)])
            norm_fill_hi(3)

            def ffn_silu(j, turns=0):
                act.wait_ge(unit_used, U_FFN + ffn_pos("G", j) + 1 + RAW * turns)
                a.activation(gate_act[j % 2][:], bank[4 + 2 * (j % 2)][:], ACT.Silu).then_inc(silu_done, 1)

            def ffn_h2_hi(j, moved=0):
                act.wait_ge(mul_done, j + 1 + moved)
                a.copy(h2T_hi[j % 2][:], h2[j % 2][:]).then_inc(h2_hi, 1)

            ffn_silu(0)
            with act.Fori(0, (FFN_STEPS - 1) // 2) as it:
                for j in (1, 2):
                    split_hi(U_FFN + ffn_pos("G", j), it)
                    ffn_h2_hi(j - 1, 2 * it)
                    split_hi(U_FFN + ffn_pos("U", j), it)
                    ffn_silu(j, it)
                    split_hi(U_FFN + ffn_pos("D", j - 1), it)
            split_hi(U_FFN + FFN_UNITS - 1)
            ffn_h2_hi(FFN_STEPS - 1)

            split_hi(U_KV)
            split_hi(U_KV + 1)
            norm_act(4, X, [(x_added, 4)])
            norm_fill_hi(4)
            split_hi(U_KV + 2)
            split_hi(U_KV + 3)
            norm_fill_hi(5)
            for u in range(4, 12):
                split_hi(U_KV + u)
            attention_act(1)
            for b in range(3):
                act.wait_ge(o_tr, b + 1)
                a.copy(op_hi[Y_BUF[1]][:, 2 * b:2 * b + 2, :],
                       bank[b][:].rearrange("p (c n) -> p c n", c=2)).then_inc(fill_hi, 1)
            split_hi(U_KV + 12)
            split_hi(U_KV + 13)
            split_hi(U_MOE)
            split_hi(U_MOE + 1)
            norm_act(6, X, [(proj_out, P_END)])
            norm_fill_hi(6)
            a.copy(hn_hi, hn[:]).then_inc(hn_hi_ready, 1)
            split_hi(U_MOE + 2)
            act.wait_ge(top_ready, 1)
            a.activation(gates[:, :, 1], gates[:, :, 0], ACT.Exp).then_inc(gate_exp, 1)

            def experts_act(ps):
                ub = U_MOE + ps * N_EXP * MOE_UNITS
                tb = 2 * (ps + 1) + TB * N_EXP * ps
                hb = FFN_STEPS + MOE_STEPS * N_EXP * ps

                def halves(use, base, dst, done):
                    for i in range(2):
                        act.wait_ge(tb_ready, base + tb_count(f"{use}{i}"))
                        a.copy(dst[:, 4 * i:4 * i + 4, :],
                               bank[tb_bank(f"{use}{i}")][:].rearrange("p (c n) -> p c n", c=4)).then_inc(done, 1)

                def output_hi(e):
                    act.wait_ge(unit_used, ub + MOE_UNITS * e)
                    for i in range(2):
                        a.copy(ye_hi[:, 4 * i:4 * i + 4, :],
                               bank[i][:].rearrange("p (c n) -> p c n", c=4)).then_inc(ye_hi_ready, 1)

                def expert(e, turns, first=False):
                    def hi(kind, j, k):
                        if not (first and ps == 0 and moe_pos(kind, j, k) < 3):
                            split_hi(ub + moe_pos(kind, j, k), turns)

                    def evac_T(j):
                        act.wait_ge(tb_ready, tb + TB * e + tb_count(f"T{j}"))
                        a.copy(h2T_hi[j % 2][:], bank[tb_bank(f"T{j}")][:]).then_inc(h2_hi, 1)

                    def silu(j):
                        act.wait_ge(unit_used, ub + moe_pos("G", j, 1) + 1 + MOE_UNITS * e)
                        act.wait_ge(mul_done, hb + MOE_STEPS * e + max(j - 1, 0))
                        a.activation(gate_act[j % 2][:], bank[2 + 2 * (j % 2)][:], ACT.Silu).then_inc(silu_done, 1)

                    hi("G", 0, 0)
                    hi("G", 0, 1)
                    if not first:
                        output_hi(e)
                    hi("U", 0, 0)
                    hi("U", 0, 1)
                    hi("G", 1, 0)
                    silu(0)
                    for j in range(1, MOE_STEPS):
                        if j > 1:
                            hi("G", j, 0)
                        hi("G", j, 1)
                        hi("U", j, 0)
                        evac_T(j - 1)
                        hi("U", j, 1)
                        hi("D", j - 1, 0)
                        silu(j)
                        hi("D", j - 1, 1)
                        if j == 1:
                            act.wait_ge(tb_ready, tb + TB * e + tb_count("oneT"))
                            a.copy(slot_ohT[:], bank[tb_bank("oneT")][:, 0:SEQ]).then_inc(ohT_out, 1)
                    halves("gather", tb + TB * e, xg_hi, xg_hi_ready)
                    hi("D", MOE_STEPS - 1, 0)
                    evac_T(MOE_STEPS - 1)
                    hi("D", MOE_STEPS - 1, 1)

                halves("gather", tb - tb_count("gather1"), xg_hi, xg_hi_ready)
                expert(0, 0, first=True)
                with act.Fori(1, N_EXP) as e:
                    expert(e, (MOE_UNITS // RAW) * e)
                output_hi(N_EXP)

            experts_act(0)
            act.wait_ge(route_ready, 1)
            flag = act.value_load(over_i[0:1, 0:1], min_val=0, max_val=1)
            with act.If(flag == 1):
                experts_act(1)
            act.wait_ge(x_final, 1)
            for t in range(NT):
                a.activation(hn[:, t, :], X[:, t, :], ACT.Square,
                             accum_out=stat[:, 7, 0, t:t + 1]).then_inc(norm_ss, 1)
            act.wait_ge(norm_var, 8)
            a.activation(stat[:, 7, 2, :], stat[:, 7, 1, :], ACT.Sqrt).then_inc(norm_std, 1)

        @block.vector
        def _(dve):
            d = nc.vector
            own = [0]

            def step(ins):
                own[0] += 1
                ins.then_inc(dve_step, 1)
                dve.wait_ge(dve_step, own[0])

            def split_lo(c, turns=0):
                dve.wait_ge(hi_ready, c + RAW * turns + 1)
                d.tensor_tensor(wlo[:, c % SPLIT, :], raw[:, c % RAW, :], whi[:, c % SPLIT, :].bitcast(F32),
                                ALU.subtract).then_inc(lo_ready, 1)

            def split_until(n, state=[0]):
                while state[0] < n:
                    split_lo(unit_of(state[0]))
                    state[0] += 1

            def norm_dve(n, src, eps_count):
                dve.wait_ge(norm_ss, 2 * ss_count(n))
                d.tensor_scalar(stat[:, n, 1, :], stat[:, n, 0, :], 1.0 / D, EPS, ALU.mult,
                                ALU.add).then_inc(norm_var, 1)
                dve.wait_ge(norm_std, eps_count)
                step(d.reciprocal(stat[:, n, 3, :], stat[:, n, 2, :]))
                apply_norm(n, src, n)

            def apply_norm(n, src, of):
                dve.wait_ge(gain_in, 16 * (n + 1))
                for t in range(NT):
                    d.scalar_tensor_tensor(out=hn[:, t, :], in0=src[:, t, :], scalar=stat[:, of, 3, t:t + 1],
                                           in1=gain[:], op0=ALU.mult, op1=ALU.mult).then_inc(hn_ready, 1)

            def norm_fill_lo(n):
                f = NORM_FILL[n]
                hi, lo = op_hi[FILL_BUF[f]], op_lo[FILL_BUF[f]]
                for g in range(4):
                    t, h = g // 2, g % 2
                    dve.wait_ge(fill_hi, int(FILL[f]) - 3 + g)
                    d.tensor_tensor(lo[:, 4 * h:4 * h + 4, t * P:(t + 1) * P],
                                    bank[g][:].rearrange("p (c n) -> p c n", c=4),
                                    hi[:, 4 * h:4 * h + 4, t * P:(t + 1) * P].bitcast(F32),
                                    ALU.subtract).then_inc(fill_lo, 1)

            def take(p):
                what, i = PROJ[p]
                dve.wait_ge(unit_used, unit_of(p) + 1)
                b2 = bank[4 + p % 4][:].rearrange("p (c n) -> p c n", c=2)
                cols = slice(WIDE * i, WIDE * (i + 1))
                if what == "mk":
                    ins = d.tensor_copy(mkT[i][:], b2)
                elif what == "mv":
                    ins = d.tensor_copy(mv[i][:], b2)
                elif what == "q":
                    ins = d.tensor_scalar(qT[:, 2 * i:2 * i + 2, :], b2, SCALE, None, ALU.mult)
                elif what == "k":
                    ins = d.tensor_copy(kT[:, 2 * i:2 * i + 2, :], b2)
                elif what in ("v", "vd"):
                    ins = d.tensor_copy(v[:, :, cols], b2)
                elif what == "qm":
                    ins = d.tensor_scalar(qmT[:], b2, SCALE, None, ALU.mult)
                elif what == "out":
                    ins = d.tensor_tensor(X[:, :, cols], X[:, :, cols], b2, ALU.add)
                elif what == "kd":
                    ins = d.tensor_copy(tok[:, :, cols], b2)
                else:
                    ins = d.tensor_scalar(qtok[:, :, cols], b2, SCALE, None, ALU.mult)
                ins.then_inc(proj_out, 1)

            norm_dve(0, tok, 1)
            split_until(2)
            norm_fill_lo(0)
            dve.wait_ge(small_hi_ready, 1)
            d.tensor_tensor(small_lo[:], small_w[:], small_hi[:].bitcast(F32), ALU.subtract).then_inc(small_lo_ready, 1)
            split_until(3)
            take(0)
            norm_dve(1, tok, 2)
            take(1)
            norm_fill_lo(1)
            norm_dve(2, X, 3)
            split_until(4)
            take(2)
            norm_fill_lo(2)
            split_until(5)
            take(3)
            dve.wait_ge(flT_ready, 1)
            d.tensor_copy(small_T, bank[3][0:FOX_H, 0:SEQ]).then_inc(flT_out, 1)

            def lambda_dots():
                dve.wait_ge(small_in, 16 * 9)
                lam4 = lam_v.rearrange("p (a b) n -> p a b n", a=2)
                step(d.tensor_tensor(lam4[:, :, 0, :], lam4[:, :, 0, :], lam4[:, :, 1, :], ALU.mult))
                d.tensor_reduce(lam[:, 0:2], lam4[:, :, 0, :], AX.X, ALU.add).then_inc(lam_ready, 1)
                d.tensor_scalar(subln[:], subln[:], 1.0 - LAM_INIT, None, ALU.mult)

            def forget_sums():
                dve.wait_ge(fl_ready, 1)
                for t in range(NT):
                    ins = d.tensor_tensor(fg[:, 0, t, :], bank[2][:, FOX_H * t:FOX_H * (t + 1)], b_f[:], ALU.add)
                step(ins)
                step(d.tensor_scalar(fg[:, 2], fg[:, 0], -1.0, None, ALU.mult))
                d.tensor_tensor(fg[:, 1], fg[:, 0], fg[:, 2], ALU.min).then_inc(fl_sum, 1)

            def forget_logs():
                dve.wait_ge(fl_ln, 1)
                dve.wait_ge(fl_sum, 1)
                d.scalar_tensor_tensor(out=fg[:, 2], in0=fg[:, 0], scalar=0.0, in1=fg[:, 1], op0=ALU.min,
                                       op1=ALU.subtract).then_inc(logf_ready, 1)
                dve.wait_ge(lam_exp, 1)
                step(d.tensor_tensor(lam[:, 4:5], lam[:, 3:4], lam[:, 2:3], ALU.subtract))
                step(d.tensor_scalar(lam[:, 5:6], lam[:, 4:5], LAM_INIT, None, ALU.subtract))

            neg_lam = lam[:, 5:6]

            def angles_start():
                dve.wait_ge(small_in, 16 * 9)
                dve.wait_ge(consts, 1)
                step(d.tensor_copy(pos_f[:], pos_i[:]))
                for t in range(NT):
                    ins = d.tensor_scalar(ang[:, 0, t, :], inv_f[:], pos_f[:, t:t + 1], None, ALU.mult)
                step(ins)

            def angles(w):
                two_pi = 2 * math.pi
                c1 = 6.28125
                c2 = float(np.float32(np.float64(two_pi - c1) * 2 ** 20 // 1 / 2 ** 20))
                c3 = float(np.float32(two_pi - c1 - c2))
                magic = float(3 * 2 ** 22)
                turn = rot[:, w, 0:NT, :]
                step(d.tensor_scalar(turn, ang[:, 0], 1.0 / two_pi, 0.25 * (w - 1), ALU.mult, ALU.add))
                step(d.tensor_scalar(turn, turn, magic, None, ALU.add))
                step(d.tensor_scalar(turn, turn, magic, None, ALU.subtract))
                prev = ang[:, 0]
                for c in (c1, c2, c3):
                    step(d.scalar_tensor_tensor(out=ang[:, w], in0=turn, scalar=-c, in1=prev, op0=ALU.mult,
                                                op1=ALU.add))
                    prev = ang[:, w]
                if w == 2:
                    step(d.tensor_scalar(ang[:, w], ang[:, w], math.pi / 2, None, ALU.add))
                ins = d.tensor_scalar(ang[:, w], ang[:, w], 3.1415925, -3.1415925, ALU.min, ALU.max)
                if w == 2:
                    ins.then_inc(ang_ready, 1)
                else:
                    step(ins)

            split_until(P_A + 3)
            for p in range(P_A, P_OUT0):
                take(p)
                split_until(min(p + 4, P_OUT0 + 3))
                if p == P_A:
                    lambda_dots()
                    forget_sums()
                if p == P_A + 2:
                    forget_logs()
                if p == P_A + 4:
                    dve.wait_ge(cum_ready, 1)
                    d.tensor_scalar(ncum[:], bank[3][0:FOX_H, 256:512], -1.0, None, ALU.mult).then_inc(ncum_ready, 1)
                    angles_start()
                if p in (P_A + 5, P_A + 6):
                    angles(p - P_A - 4)

            def attention_dve(layer):
                scores, outs, last = attention_plan(layer)
                sb0, rb0 = S_BASE[layer], R_BASE[layer]
                done = [0]

                def maxima(upto):
                    while done[0] <= min(upto, len(scores) - 1):
                        s = done[0]
                        g = sb0 + s
                        dve.wait_ge(score_ready, g + 1)
                        w0 = P if scores[s][0] != "mem" else MEM
                        d.tensor_reduce(negm[:, g, 0:1], score_bank[s % AHEAD][:, 0:w0], AX.X, ALU.max, negate=True)
                        d.tensor_reduce(negm[:, g, 1:2], score_bank[s % AHEAD][:, w0:w0 + MEM], AX.X, ALU.max,
                                        negate=True).then_inc(rowmax, 1)
                        done[0] += 1

                def fill(r):
                    kind, h = outs[r]
                    if kind == "diff":
                        dve.wait_ge(pv_ready, rb0 + r + 1)
                        d.tensor_copy(tok[:, :, DV * h:DV * (h + 1)],
                                      bank[5 + r % 2][:, 0:256].rearrange("p (t n) -> p t n", t=NT)).then_inc(o_out, 1)
                        return
                    if h % 2 == 0:
                        return
                    c = h // 2 + (6 if kind == "mem" else 0)
                    base = int(FILL[2] if layer == 0 else FILL[6])
                    dve.wait_ge(fill_hi, base + (c + 1 if layer == 0 else c - 5))
                    d.tensor_tensor(op_lo[Y_BUF[layer]][:, c, :], bank[5 + (r // 2) % 2][:, 0:SEQ],
                                    op_hi[Y_BUF[layer]][:, c, :].bitcast(F32), ALU.subtract).then_inc(fill_lo, 1)

                def normalise(r):
                    kind, h = outs[r]
                    s = last[r]
                    g = sb0 + s
                    dve.wait_ge(exp_done, g + 1)
                    w0 = P if kind != "mem" else MEM
                    if kind == "diff":
                        step(d.reciprocal(rinv[:, g - 1:g + 1, :], rsum[:, g - 1:g + 1, :]))
                        step(d.tensor_scalar(rinv[:, g, :], rinv[:, g, :], neg_lam, None, ALU.mult))
                        p1, p2 = prob[(s - 1) % AHEAD], prob[s % AHEAD]
                        for t, (c, w) in enumerate(((0, P), (P, MEM))):
                            step(d.tensor_scalar(p1[:, c:c + w], p1[:, c:c + w], rinv[:, g - 1, t:t + 1], None,
                                                 ALU.mult))
                            ins = d.scalar_tensor_tensor(out=p1[:, c:c + w], in0=p2[:, c:c + w],
                                                         scalar=rinv[:, g, t:t + 1], in1=p1[:, c:c + w],
                                                         op0=ALU.mult, op1=ALU.add)
                        ins.then_inc(prob_ready, 1)
                    else:
                        step(d.reciprocal(rinv[:, g, :], rsum[:, g, :]))
                        pr = prob[s % AHEAD]
                        d.tensor_scalar(pr[:, 0:w0], pr[:, 0:w0], rinv[:, g, 0:1], None, ALU.mult)
                        d.tensor_scalar(pr[:, w0:w0 + MEM], pr[:, w0:w0 + MEM], rinv[:, g, 1:2], None,
                                        ALU.mult).then_inc(prob_ready, 1)

                maxima(AHEAD - 1)
                normalise(0)
                for r in range(len(outs)):
                    if r + 1 < len(outs):
                        normalise(r + 1)
                    if r:
                        fill(r - 1)
                    maxima(last[r] + AHEAD)
                    if layer and r == DIFF_H:
                        sub_norm_var()
                    if layer and r == DIFF_H + 1:
                        sub_norm()
                fill(len(outs) - 1)

            o4 = tok[:, :, 0:FOX_W].rearrange("p t (h n) -> p t h n", n=DV)

            def sub_norm_var():
                dve.wait_ge(o_squared, DIFF_H)
                d.tensor_scalar(o_ss[:, 1], o_ss[:, 0], 1.0 / DV, EPS, ALU.mult, ALU.add).then_inc(norm_var, 1)

            def sub_norm():
                dve.wait_ge(norm_std, 6)
                step(d.reciprocal(o_ss[:, 3], o_ss[:, 2]))
                dve.wait_ge(o_out, DIFF_H)
                for t in range(NT):
                    for h in range(DIFF_H):
                        i = DIFF_H * t + h
                        ins = d.scalar_tensor_tensor(out=o4[:, t, h], in0=o4[:, t, h], scalar=o_ss[:, 3, i:i + 1],
                                                     in1=subln[:], op0=ALU.mult, op1=ALU.mult)
                    ins.then_inc(o_norm, 1)

            attention_dve(0)
            split_until(P_KV)
            for p in range(P_OUT0, P_KV):
                take(p)
                if p in (P_OUT0 + 1, P_OUT0 + 2):
                    split_lo(U_FFN + p - P_OUT0 - 1)
            dve.wait_ge(proj_out, P_KV)
            norm_dve(3, X, 4)
            norm_fill_lo(3)

            def ffn_mul(j, turns=0, moved=0):
                dve.wait_ge(unit_used, U_FFN + ffn_pos("U", j) + 1 + RAW * turns)
                dve.wait_ge(silu_done, j + 1 + moved)
                if j:
                    dve.wait_ge(h2_lo, j + moved)
                d.tensor_tensor(h2[j % 2][:], gate_act[j % 2][:], bank[5 + 2 * (j % 2)][:],
                                ALU.mult).then_inc(mul_done, 1)

            def ffn_h2_lo(j, moved=0):
                dve.wait_ge(h2_hi, j + 1 + moved)
                d.tensor_tensor(h2T_lo[j % 2][:], h2[j % 2][:], h2T_hi[j % 2][:].bitcast(F32),
                                ALU.subtract).then_inc(h2_lo, 1)

            ffn_mul(0)
            with dve.Fori(0, (FFN_STEPS - 1) // 2) as it:
                for j in (1, 2):
                    split_lo(U_FFN + ffn_pos("G", j), it)
                    ffn_h2_lo(j - 1, 2 * it)
                    split_lo(U_FFN + ffn_pos("U", j), it)
                    split_lo(U_FFN + ffn_pos("D", j - 1), it)
                    ffn_mul(j, it, 2 * it)
            split_lo(U_FFN + FFN_UNITS - 1)
            ffn_h2_lo(FFN_STEPS - 1)
            split_lo(U_KV)
            split_lo(U_KV + 1)
            dve.wait_ge(unit_used, U_KV)
            for t in range(NT):
                for h in range(2):
                    cols = slice(512 * h, 512 * (h + 1))
                    d.tensor_tensor(X[:, t, cols], X[:, t, cols], bank[2 * t + h][:], ALU.add).then_inc(x_added, 1)
            dve.wait_ge(x_added, 4)
            norm_dve(4, X, 5)
            norm_fill_lo(4)

            def rotate(qk, count):
                for t in range(NT):
                    heads = qk[:, t, 0:FOX_W].rearrange("p (h n) -> p h n", n=HD)
                    x1, x2 = heads[:, :, 0:HALF], heads[:, :, HALF:ROT]
                    cos = cosv[:, t:t + 1, :].to_broadcast([P, 12, HALF])
                    sin = sinv[:, t:t + 1, :].to_broadcast([P, 12, HALF])
                    for i, (a, b) in enumerate(((x1, cos), (x2, sin), (x2, cos), (x1, sin))):
                        ins = d.tensor_tensor(rot[:, i], a, b, ALU.mult)
                        step(ins)
                    step(d.tensor_tensor(x1, rot[:, 0], rot[:, 1], ALU.subtract))
                    ins = d.tensor_tensor(x2, rot[:, 2], rot[:, 3], ALU.add)
                    if t == NT - 1:
                        ins.then_inc(rot_ready, 1)
                        dve.wait_ge(rot_ready, count)
                    else:
                        step(ins)

            def qk_take(first, dst):
                for b in range(3):
                    dve.wait_ge(qk_tr, first + b + 1)
                    d.tensor_copy(dst[:, 2 * b:2 * b + 2, :],
                                  bank[b][:].rearrange("p (c n) -> p c n", c=2)).then_inc(qk_out, 1)

            split_lo(U_KV + 2)
            apply_norm(5, X, 4)
            take(P_KV)
            split_lo(U_KV + 3)
            take(P_KV + 1)
            norm_fill_lo(5)
            take(P_KV + 2)
            split_lo(U_KV + 4)
            dve.wait_ge(proj_out, P_QD)
            dve.wait_ge(sin_ready, 1)
            rotate(tok, 1)
            split_lo(U_KV + 5)
            take(P_QD)
            split_lo(U_KV + 6)
            take(P_QD + 1)
            split_lo(U_KV + 7)
            take(P_QD + 2)
            qk_take(0, kT)
            dve.wait_ge(proj_out, P_VD)
            rotate(qtok, 2)
            split_lo(U_KV + 8)
            take(P_VD)
            split_lo(U_KV + 9)
            take(P_VD + 1)
            take(P_VD + 2)
            qk_take(3, qT)
            split_lo(U_KV + 10)
            split_lo(U_KV + 11)
            take(P_OUT1 - 1)
            attention_dve(1)
            for b in range(3):
                dve.wait_ge(fill_hi, int(FILL[6]) + 3 + b)
                d.tensor_tensor(op_lo[Y_BUF[1]][:, 2 * b:2 * b + 2, :], bank[b][:].rearrange("p (c n) -> p c n", c=2),
                                op_hi[Y_BUF[1]][:, 2 * b:2 * b + 2, :].bitcast(F32), ALU.subtract).then_inc(fill_lo, 1)
            split_lo(U_KV + 12)
            split_lo(U_KV + 13)
            for p in range(P_OUT1, P_END):
                take(p)
                if p in (P_OUT1 + 1, P_OUT1 + 2):
                    split_lo(U_MOE + p - P_OUT1 - 1)
            dve.wait_ge(proj_out, P_END)
            norm_dve(6, X, 7)
            norm_fill_lo(6)
            dve.wait_ge(logitT_ready, 1)
            d.tensor_copy(small_T[0:N_EXP, :], bank[5][0:N_EXP, 0:SEQ]).then_inc(logitT_out, 1)
            dve.wait_ge(hn_hi_ready, 1)
            d.tensor_tensor(hn_lo, hn[:], hn_hi.bitcast(F32), ALU.subtract).then_inc(hn_lo_ready, 1)
            dve.wait_ge(logit_ready, 1)
            step(d.tensor_copy(lg[:], bank[4][:, 0:NT * N_EXP].rearrange("p (t n) -> p t n", t=NT)))
            for t in range(NT):
                ins = d.max(out=top[:, t, :], in_=lg[:, t, :])
            step(ins)
            for t in range(NT):
                ins = d.max_index(out=top_i[:, t, :], in_max=top[:, t, :], in_values=lg[:, t, :])
            step(ins)
            step(d.tensor_copy(top_f[:], top_i[:]))
            for t in range(NT):
                for i in range(2):
                    ins = d.tensor_scalar(oh[:, i, t, :], iota8[:], top_f[:, t, i:i + 1], None, ALU.is_equal)
            step(ins)
            step(d.tensor_tensor(member[:, :, 0:N_EXP], oh[:, 0], oh[:, 1], ALU.add))
            d.tensor_copy(member_bf[:], member[:, :, 0:N_EXP]).then_inc(member_ready, 1)
            d.tensor_tensor(gates[:, :, 0], top[:, :, 1], top[:, :, 0], ALU.subtract).then_inc(top_ready, 1)
            dve.wait_ge(rank_ready, 1)
            step(d.tensor_scalar(rank[:, :, 0:N_EXP], bank[4][:, 32:32 + NT * N_EXP].rearrange("p (t n) -> p t n", t=NT),
                                 1.0, None, ALU.subtract))

            def combine_weights():
                dve.wait_ge(gate_exp, 1)
                step(d.tensor_scalar(gates[:, :, 2], gates[:, :, 1], 1.0, None, ALU.add))
                step(d.reciprocal(gates[:, :, 2], gates[:, :, 2]))
                step(d.tensor_tensor(gates[:, :, 3], gates[:, :, 1], gates[:, :, 2], ALU.mult))
                for t in range(NT):
                    ins = d.tensor_scalar(comb[:, t, :], oh[:, 0, t, :], gates[:, t, 2:3], None, ALU.mult)
                step(ins)
                for t in range(NT):
                    ins = d.scalar_tensor_tensor(out=comb[:, t, :], in0=oh[:, 1, t, :], scalar=gates[:, t, 3:4],
                                                 in1=comb[:, t, :], op0=ALU.mult, op1=ALU.add)
                step(ins)
                step(d.tensor_reduce(over[:, 0:1], bank[4][:, 64:64 + N_EXP], AX.X, ALU.max))
                step(d.tensor_scalar(over[:, 1:2], over[:, 0:1], float(P), None, ALU.is_gt))
                d.tensor_copy(over_i[:], over[:, 1:2]).then_inc(route_ready, 1)

            def experts_dve(ps):
                ub = U_MOE + ps * N_EXP * MOE_UNITS
                tb = 2 * (ps + 1) + TB * N_EXP * ps
                hb = FFN_STEPS + MOE_STEPS * N_EXP * ps
                xb = 2 * (N_EXP + 1) * ps
                ab = 4 + 4 * N_EXP * ps

                def one_hot(e):
                    for t in range(NT):
                        ins = d.tensor_scalar(slot_oh[:, t, :], slot_no[:, P * ps:P * (ps + 1)],
                                              rank[:, t, bass.ds(e, 1)], member[:, t, bass.ds(e, 1)],
                                              ALU.is_equal, ALU.mult)
                    ins.then_inc(oh_ready, 1)

                def halves(use, count, hi, lo, ready, done):
                    for i in range(2):
                        dve.wait_ge(ready, count + i + 1)
                        b = bank[tb_bank(f"gather{i}")] if use == "gather" else bank[i]
                        d.tensor_tensor(lo[:, 4 * i:4 * i + 4, :], b[:].rearrange("p (c n) -> p c n", c=4),
                                        hi[:, 4 * i:4 * i + 4, :].bitcast(F32), ALU.subtract).then_inc(done, 1)

                def output_lo(e):
                    halves("output", 2 * (N_EXP * ps + e) - 2, ye_hi, ye_lo, ye_hi_ready, ye_lo_ready)

                def add_back(e, i):
                    t, h = i // 2, i % 2
                    cols = slice(512 * h, 512 * (h + 1))
                    dve.wait_ge(tb_ready, tb + TB * e - TB + tb_count(f"back{i}"))
                    dve.wait_ge(x_added, ab + 4 * e - 4)
                    d.scalar_tensor_tensor(out=X[:, t, cols], in0=bank[tb_bank(f"back{i}")][:],
                                           scalar=comb[:, t, bass.ds(e - 1, 1)], in1=X[:, t, cols],
                                           op0=ALU.mult, op1=ALU.add).then_inc(x_added, 1)

                def expert(e, turns, first=False):
                    def lo(kind, j, k):
                        if not (first and ps == 0 and moe_pos(kind, j, k) < 3):
                            split_lo(ub + moe_pos(kind, j, k), turns)

                    def evac_T(j):
                        dve.wait_ge(h2_hi, hb + MOE_STEPS * e + j + 1)
                        d.tensor_tensor(h2T_lo[j % 2][:], bank[tb_bank(f"T{j}")][:], h2T_hi[j % 2][:].bitcast(F32),
                                        ALU.subtract).then_inc(h2_lo, 1)

                    def mul(j):
                        dve.wait_ge(unit_used, ub + moe_pos("U", j, 1) + 1 + MOE_UNITS * e)
                        dve.wait_ge(silu_done, hb + MOE_STEPS * e + j + 1)
                        if j >= 2:
                            dve.wait_ge(tb_ready, tb + TB * e + tb_count(f"T{j - 2}"))
                        elif not first:
                            dve.wait_ge(tb_ready, tb + TB * e - TB + tb_count("T6"))
                        d.tensor_tensor(h2[j % 2][:], gate_act[j % 2][:], bank[3 + 2 * (j % 2)][:],
                                        ALU.mult).then_inc(mul_done, 1)

                    lo("G", 0, 0)
                    lo("G", 0, 1)
                    if not first:
                        output_lo(e)
                    lo("U", 0, 0)
                    lo("U", 0, 1)
                    if not first:
                        add_back(e, 0)
                        add_back(e, 1)
                    lo("G", 1, 0)
                    if not first:
                        add_back(e, 2)
                        add_back(e, 3)
                    mul(0)
                    for j in range(1, MOE_STEPS):
                        if j > 1:
                            lo("G", j, 0)
                        lo("G", j, 1)
                        lo("U", j, 0)
                        evac_T(j - 1)
                        lo("U", j, 1)
                        if j == 3:
                            dve.wait_ge(tb_ready, tb + TB * e + tb_count("oneT"))
                            one_hot(e + 1)
                        lo("D", j - 1, 0)
                        lo("D", j - 1, 1)
                        mul(j)
                    halves("gather", xb + 2 + 2 * e, xg_hi, xg_lo, xg_hi_ready, xg_lo_ready)
                    lo("D", MOE_STEPS - 1, 0)
                    evac_T(MOE_STEPS - 1)
                    lo("D", MOE_STEPS - 1, 1)

                one_hot(0)
                if ps == 0:
                    combine_weights()
                    split_lo(U_MOE + 2)
                halves("gather", xb, xg_hi, xg_lo, xg_hi_ready, xg_lo_ready)
                expert(0, 0, first=True)
                with dve.Fori(1, N_EXP) as e:
                    expert(e, (MOE_UNITS // RAW) * e)
                output_lo(N_EXP)
                for i in range(4):
                    add_back(N_EXP, i)
                dve.wait_ge(x_added, ab + 4 * N_EXP)

            dve.wait_ge(slots_ready, 1)
            experts_dve(0)
            dve.wait_ge(route_ready, 1)
            flag = dve.value_load(over_i[0:1, 0:1], min_val=0, max_val=1)
            with dve.If(flag == 1):
                experts_dve(1)
            d.memset(over[:, 1:2], 0.0).then_inc(x_final, 1)
            norm_dve(7, X, 8)

        @block.tensor
        def _(pe):
            m = nc.tensor

            def product(dst, pairs, start=True, stop=True):
                n = len(pairs)
                for i, ((sh, sl), (mh, ml)) in enumerate(pairs):
                    m.matmul(dst, sh, mh, start=start and i == 0, stop=False)
                    m.matmul(dst, sh, ml, start=False, stop=False)
                    last = m.matmul(dst, sl, mh, start=False, stop=stop and i == n - 1)
                return last

            def norm_transposes(n):
                if n:
                    pe.wait_ge(fill_lo, int(FILL[NORM_FILL[n] - 1]))
                for g in range(4):
                    t, h = g // 2, g % 2
                    pe.wait_ge(hn_ready, 2 * n + t + 1)
                    for c in range(4):
                        k = 4 * h + c
                        last = m.transpose(bank[g][:, P * c:P * (c + 1)], hn[:, t, P * k:P * (k + 1)], ident[:])
                    last.then_inc(tr_ready, 1)

            def project(p):
                what, _ = PROJ[p]
                f = fill_of(p)
                hi, lo = op_hi[FILL_BUF[f]], op_lo[FILL_BUF[f]]
                u = unit_of(p)
                pe.wait_ge(fill_lo, int(FILL[f]))
                pe.wait_ge(lo_ready, u + 1)
                if p >= 4:
                    pe.wait_ge(proj_out, p - 3)
                wh, wl = wide(whi, u % SPLIT), wide(wlo, u % SPLIT)
                b = bank[4 + p % 4]
                for c in range(2):
                    dst = b[:, WIDE * c:WIDE * (c + 1)]
                    sl = slice(P * c, P * (c + 1))
                    if what in ("mk", "q", "k", "qm"):
                        last = product(dst, [((wh[:, k, sl], wl[:, k, sl]), (hi[:, k, :], lo[:, k, :]))
                                             for k in range(KC)])
                    else:
                        last = product(dst, [((hi[:, k, sl], lo[:, k, sl]), (wh[:, k, :], wl[:, k, :]))
                                             for k in range(KC)])
                last.then_inc(unit_used, 1)

            def small_product(dst, f, lo_col, hi_col):
                hi, lo = op_hi[FILL_BUF[f]], op_lo[FILL_BUF[f]]
                return product(dst[0:hi_col - lo_col, 0:SEQ],
                               [((small_hi[:, k, lo_col:hi_col], small_lo[:, k, lo_col:hi_col]),
                                 (hi[:, k, :], lo[:, k, :])) for k in range(KC)])

            def small_transposes(dst, n):
                for t in range(NT):
                    last = m.transpose(dst[:, n * t:n * (t + 1)], small_T[0:n, P * t:P * (t + 1)], ident[0:n, 0:n])
                return last

            def attention_pe(layer):
                scores, outs, last_s = attention_plan(layer)
                sb0, rb0 = S_BASE[layer], R_BASE[layer]
                done = [0]

                def score(s):
                    kind, h = scores[s]
                    g = sb0 + s
                    if s >= AHEAD:
                        pe.wait_ge(exp_done, g + 1 - AHEAD)
                    b = score_bank[s % AHEAD]
                    po, c = HD * (h % 2), h // 2
                    for t in range(NT):
                        sl = slice(P * t, P * (t + 1))
                        if kind == "mem":
                            mm = m.matmul(b[:, MEM * t:MEM * (t + 1)], qmT[po:po + HD, c, sl],
                                          mkT[layer][po:po + HD, c, :], start=True, stop=True)
                            continue
                        w = P * (t + 1)
                        o0 = P * t
                        m.matmul(b[:, o0:o0 + w], qT[po:po + HD, c, sl], kT[po:po + HD, c, 0:w], start=True,
                                 stop=False)
                        if kind == "fox":
                            m.matmul(b[:, o0:o0 + w], ident[0:FOX_H, h:h + 1].to_broadcast([FOX_H, P]),
                                     ncum[:, 0:w], start=False, stop=False)
                        mask = causal if kind == "fox" else chunked
                        mm = m.matmul(b[:, o0 + w - P:o0 + w], ident_bf[:], mask[:], start=False, stop=True)
                    mm.then_inc(score_ready, 1)

                def scores_until(upto):
                    while done[0] <= min(upto, len(scores) - 1):
                        score(done[0])
                        done[0] += 1

                def transposes(r):
                    kind, h = outs[r]
                    g = rb0 + r
                    pe.wait_ge(prob_ready, g + 1)
                    if g >= 2:
                        pe.wait_ge(pT_out, g - 1)
                    src = prob[(last_s[r] - (kind == "diff")) % AHEAD]
                    b = bank[3 + r % 2]
                    for i in range(4 if kind == "mem" else 3):
                        j = 2 * (i % 2) + i // 2 if kind == "mem" else i
                        tr = m.transpose(b[:, P * j:P * (j + 1)], src[:, P * i:P * (i + 1)], ident[:])
                    tr.then_inc(pT_ready, 1)

                def values(r):
                    kind, h = outs[r]
                    g = rb0 + r
                    pe.wait_ge(pT_out, g + 1)
                    pT = probT[r % 2]
                    if kind == "diff":
                        if r >= 2:
                            pe.wait_ge(o_out, r - 1)
                        b = bank[5 + r % 2]
                        cols = slice(DV * h, DV * (h + 1))
                        m.matmul(b[:, 0:P], pT[:, 0:P], v[:, 0, cols], start=True, stop=True)
                        m.matmul(b[:, P:2 * P], pT[:, P:2 * P], v[:, 0, cols], start=True, stop=False)
                        mm = m.matmul(b[:, P:2 * P], pT[:, 2 * P:3 * P], v[:, 1, cols], start=False, stop=True)
                    else:
                        pair = r // 2
                        if layer == 0 and pair >= 2:
                            pe.wait_ge(fill_lo, int(FILL[2]) + pair - 1)
                        if layer == 1:
                            pe.wait_ge(o_out, DIFF_H)
                        b = bank[5 + pair % 2]
                        po = HD * (h % 2)
                        cols = slice(HD * h, HD * (h + 1))
                        val = v if kind == "fox" else mv[layer]
                        m.matmul(b[po:po + HD, 0:SEQ], val[:, 0, cols], pT[:, 0:SEQ], start=True, stop=False)
                        if kind == "fox":
                            mm = m.matmul(b[po:po + HD, P:SEQ], val[:, 1, cols], pT[:, 2 * P:3 * P], start=False,
                                          stop=True)
                        else:
                            mm = m.matmul(b[po:po + HD, 0:SEQ], val[:, 1, cols], pT[:, SEQ:2 * SEQ], start=False,
                                          stop=True)
                    mm.then_inc(pv_ready, 1)

                scores_until(AHEAD - 1)
                for r in range(len(outs)):
                    transposes(r)
                    if r:
                        values(r - 1)
                    scores_until(last_s[r] + AHEAD)
                values(len(outs) - 1)

            pe.wait_ge(consts, 1)
            norm_transposes(0)
            project(0)
            project(1)
            norm_transposes(1)
            project(2)
            project(3)
            norm_transposes(2)
            pe.wait_ge(small_lo_ready, 1)
            pe.wait_ge(small_hi_ready, 1)
            pe.wait_ge(fill_lo, int(FILL[2]))
            small_product(bank[3], 2, 0, FOX_H).then_inc(flT_ready, 1)
            for p in range(P_A, P_OUT0):
                project(p)
                if p == P_A:
                    pe.wait_ge(flT_out, 1)
                    small_transposes(bank[2], FOX_H).then_inc(fl_ready, 1)
                if p == P_A + 3:
                    pe.wait_ge(logf_ready, 1)
                    m.matmul(bank[3][0:FOX_H, 256:512], fg[:, 2, 0, :], upper[:], start=True, stop=False)
                    m.matmul(bank[3][0:FOX_H, 384:512], fg[:, 2, 1, :], upper[:, 0:P], start=False,
                             stop=True).then_inc(cum_ready, 1)
            pe.wait_ge(ncum_ready, 1)
            pe.wait_ge(proj_out, P_OUT0)
            attention_pe(0)
            for p in range(P_OUT0, P_KV):
                project(p)
            norm_transposes(3)
            pe.wait_ge(fill_lo, int(FILL[4]))
            pe.wait_ge(proj_out, P_KV)

            hi, lo = op_hi[0], op_lo[0]

            def ffn_up(kind, j, it=0):
                c = U_FFN + ffn_pos(kind, j)
                pe.wait_ge(lo_ready, c + RAW * it + 1)
                wh, wl = wide(whi, c % SPLIT), wide(wlo, c % SPLIT)
                b = bank[4 + 2 * (j % 2) + (kind == "U")]
                for c2 in range(2):
                    sl = slice(P * c2, P * (c2 + 1))
                    last = product(b[:, WIDE * c2:WIDE * (c2 + 1)],
                                   [((wh[:, k, sl], wl[:, k, sl]), (hi[:, k, :], lo[:, k, :])) for k in range(KC)])
                last.then_inc(unit_used, 1)

            def ffn_down(j, it=0, moved=0, first=False, final=False):
                c = U_FFN + ffn_pos("D", j)
                pe.wait_ge(h2_lo, j + 1 + moved)
                pe.wait_ge(lo_ready, c + RAW * it + 1)
                wh = whi[:, c % SPLIT, :].rearrange("p (k n) -> p k n", k=2)
                wl = wlo[:, c % SPLIT, :].rearrange("p (k n) -> p k n", k=2)
                for t in range(NT):
                    for h in range(2):
                        cols = slice(512 * h, 512 * (h + 1))
                        sls = [slice(WIDE * k + P * t, WIDE * k + P * (t + 1)) for k in range(2)]
                        last = product(bank[2 * t + h][:],
                                       [((h2T_hi[j % 2][:, s], h2T_lo[j % 2][:, s]), (wh[:, k, cols], wl[:, k, cols]))
                                        for k, s in enumerate(sls)], start=first, stop=final)
                last.then_inc(unit_used, 1)

            def ffn_pair(it, first=False):
                for j in (1, 2):
                    if j == 2 or not first:
                        pe.wait_ge(mul_done, j - 1 + 2 * it)
                    ffn_up("G", j, it)
                    ffn_up("U", j, it)
                    ffn_down(j - 1, it, 2 * it, first=first and j == 1)

            ffn_up("G", 0)
            ffn_up("U", 0)
            ffn_pair(0, first=True)
            with pe.Fori(1, (FFN_STEPS - 1) // 2) as it:
                ffn_pair(it)
            ffn_down(FFN_STEPS - 1, 0, 0, final=True)

            def transposes_of(src, ready, val, sem_out):
                pe.wait_ge(ready, val)
                for b in range(3):
                    for c in range(2):
                        for t in range(NT):
                            k = 2 * b + c
                            last = m.transpose(bank[b][:, WIDE * c + P * t:WIDE * c + P * (t + 1)],
                                               src[:, t, P * k:P * (k + 1)], ident[:])
                    last.then_inc(sem_out, 1)

            norm_transposes(4)
            project(P_KV)
            project(P_KV + 1)
            norm_transposes(5)
            project(P_KV + 2)
            for p in range(P_QD, P_VD):
                project(p)
            transposes_of(tok, rot_ready, 1, qk_tr)
            for p in range(P_VD, P_OUT1 - 1):
                project(p)
            pe.wait_ge(qk_out, 3)
            transposes_of(qtok, rot_ready, 2, qk_tr)
            project(P_OUT1 - 1)
            pe.wait_ge(qk_out, 6)
            pe.wait_ge(proj_out, P_OUT1)
            attention_pe(1)
            transposes_of(tok, o_norm, 2, o_tr)
            for p in range(P_OUT1, P_END):
                project(p)
            norm_transposes(6)
            pe.wait_ge(fill_lo, int(FILL[8]))
            pe.wait_ge(proj_out, P_END)
            small_product(bank[5], 8, FOX_H, FOX_H + N_EXP).then_inc(logitT_ready, 1)
            pe.wait_ge(logitT_out, 1)
            small_transposes(bank[4], N_EXP).then_inc(logit_ready, 1)
            pe.wait_ge(member_ready, 1)
            b = bank[4]
            m.matmul(b[:, 32:40], upper_bf[:], member_bf[:, 0, :], start=True, stop=True)
            m.matmul(b[:, 40:48], ones_bf[:], member_bf[:, 0, :], start=True, stop=False)
            m.matmul(b[:, 40:48], upper_bf[:], member_bf[:, 1, :], start=False, stop=True)
            m.matmul(b[:, 64:72], ones_bf[:], member_bf[:, 0, :], start=True, stop=False)
            m.matmul(b[:, 64:72], ones_bf[:], member_bf[:, 1, :], start=False, stop=True).then_inc(rank_ready, 1)

            def experts_pe(ps):
                ub = U_MOE + ps * N_EXP * MOE_UNITS
                hb = FFN_STEPS + MOE_STEPS * N_EXP * ps
                xb = 2 * (N_EXP + 1) * ps
                ab = 4 + 4 * N_EXP * ps
                ob = (N_EXP + 1) * ps
                eb = N_EXP * ps

                def one_pass(dst, st_hi, st_lo, mv_hi, mv_lo, start, stop):
                    m.matmul(dst, st_hi, mv_hi, start=start, stop=False)
                    return m.matmul(dst, st_lo, mv_lo, start=False, stop=stop)

                def gather(waits):
                    for i in range(2):
                        for s, val in waits[i]:
                            pe.wait_ge(s, val)
                        b = bank[tb_bank(f"gather{i}")]
                        for c in range(4):
                            cols = slice(P * (4 * i + c), P * (4 * i + c + 1))
                            for t in range(NT):
                                last = one_pass(b[:, P * c:P * (c + 1)], hn_hi[:, t, cols], hn_lo[:, t, cols],
                                                slot_oh[:, t, :], slot_oh[:, t, :], t == 0, t == NT - 1)
                        last.then_inc(tb_ready, 1)

                def back(e):
                    pe.wait_ge(ye_lo_ready, 2 * (eb + e))
                    pe.wait_ge(ohT_out, eb + e)
                    for i in range(4):
                        s, val = [(xg_lo_ready, xb + 2 * e + 2), (h2_lo, hb + MOE_STEPS * e),
                                  (x_added, ab + 4 * e - 3), (x_added, ab + 4 * e - 2)][i]
                        pe.wait_ge(s, val)
                        t, h = i // 2, i % 2
                        oneT = slot_ohT[:, P * t:P * (t + 1)]
                        one_pass(bank[tb_bank(f"back{i}")][:].rearrange("p (c n) -> p c n", c=4), oneT, oneT,
                                 ye_hi[:, 4 * h:4 * h + 4, :], ye_lo[:, 4 * h:4 * h + 4, :], True,
                                 True).then_inc(tb_ready, 1)

                def expert(e, first=False):
                    def up(kind, j, a):
                        c = ub + moe_pos(kind, j, a)
                        pe.wait_ge(lo_ready, c + MOE_UNITS * e + 1)
                        wh = whi[:, c % SPLIT, :].rearrange("p (k n) -> p k n", k=4)
                        wl = wlo[:, c % SPLIT, :].rearrange("p (k n) -> p k n", k=4)
                        product(bank[2 + 2 * (j % 2) + (kind == "U")][:],
                                [((xg_hi[:, 4 * a + k, :], xg_lo[:, 4 * a + k, :]), (wh[:, k, :], wl[:, k, :]))
                                 for k in range(4)], start=a == 0, stop=a == 1).then_inc(unit_used, 1)

                    def down(j, a):
                        c = ub + moe_pos("D", j, a)
                        pe.wait_ge(h2_lo, hb + MOE_STEPS * e + j + 1)
                        pe.wait_ge(lo_ready, c + MOE_UNITS * e + 1)
                        wh = whi[:, c % SPLIT, :].rearrange("p (k n) -> p k n", k=2)
                        wl = wlo[:, c % SPLIT, :].rearrange("p (k n) -> p k n", k=2)
                        for h in range(2):
                            cols = slice(512 * h, 512 * (h + 1))
                            sls = [slice(P * (2 * a + k), P * (2 * a + k + 1)) for k in range(2)]
                            last = product(bank[h][:],
                                           [((h2T_hi[j % 2][:, s], h2T_lo[j % 2][:, s]),
                                             (wh[:, k, cols], wl[:, k, cols])) for k, s in enumerate(sls)],
                                           start=j == 0 and a == 0, stop=j == MOE_STEPS - 1 and a == 1)
                        last.then_inc(unit_used, 1)

                    def h2_transposes(j):
                        pe.wait_ge(mul_done, hb + MOE_STEPS * e + j + 1)
                        if j == 0:
                            pe.wait_ge(x_added, ab + 4 * e)
                        elif j == 2:
                            pe.wait_ge(ohT_out, eb + e + 1)
                        elif j == MOE_STEPS - 1:
                            pe.wait_ge(xg_lo_ready, xb + 2 * e + 3)
                        else:
                            pe.wait_ge(h2_lo, hb + MOE_STEPS * e + max(j - 1, 1))
                        for c in range(4):
                            last = m.transpose(bank[tb_bank(f"T{j}")][:, P * c:P * (c + 1)],
                                               h2[j % 2][:, P * c:P * (c + 1)], ident[:])
                        last.then_inc(tb_ready, 1)

                    pe.wait_ge(xg_lo_ready, xb + 2 * e + 2)
                    for j in range(MOE_STEPS):
                        pe.wait_ge(mul_done, hb + MOE_STEPS * e + max(j - 1, 0))
                        up("G", j, 0)
                        if j:
                            h2_transposes(j - 1)
                        up("G", j, 1)
                        up("U", j, 0)
                        if j == 0 and not first:
                            back(e)
                        up("U", j, 1)
                        if j == 1:
                            for t in range(NT):
                                last = m.transpose(bank[tb_bank("oneT")][:, P * t:P * (t + 1)],
                                                   slot_oh[:, t, :].bitcast(F32), ident[:])
                            last.then_inc(tb_ready, 1)
                        if j == MOE_STEPS - 1:
                            gather([[(oh_ready, ob + e + 2), (h2_lo, hb + MOE_STEPS * e + 5)],
                                    [(h2_lo, hb + MOE_STEPS * e + 6)]])
                        if j:
                            down(j - 1, 0)
                            if j == MOE_STEPS - 1:
                                h2_transposes(j)
                            down(j - 1, 1)
                    down(MOE_STEPS - 1, 0)
                    down(MOE_STEPS - 1, 1)

                pe.wait_ge(hn_lo_ready, 1)
                gather([[(oh_ready, ob + 1)], []])
                expert(0, first=True)
                with pe.Fori(1, N_EXP) as e:
                    expert(e)
                back(N_EXP)

            experts_pe(0)
            pe.wait_ge(route_ready, 1)
            flag = pe.value_load(over_i[0:1, 0:1], min_val=0, max_val=1)
            with pe.If(flag == 1):
                experts_pe(1)


_INS = ["x", "mem", "positions", "mix_norm_g", "ffn_norm_g", "mem_norm_g", "w_mem_kv", "w_out", "w_in_a", "b_forget",
        "w_q_b", "lambda_q1", "lambda_k1", "lambda_q2", "lambda_k2", "subln_g", "kv_norm_g", "w_kv_shared",
        "w_gate_up_dense", "w_down_dense", "w_router", "w_gate_up_moe", "w_down_moe", "final_norm_g"]


def kernel(**inputs):
    import concourse.bacc as _bacc
    from concourse import mybir as _mybir
    from concourse.bass_utils import run_bass_kernel_spmd as _run

    nc = _bacc.Bacc("TRN2", target_bir_lowering=False, num_devices=1, dynamic_dma_scratch_size=8192)
    arrays, args = {}, []
    for name in _INS:
        a = np.ascontiguousarray(inputs[name])
        arrays[f"in_{name}_dram"] = a
        args.append(nc.dram_tensor(f"in_{name}_dram", a.shape, _mybir.dt.from_np(a.dtype), kind="ExternalInput").ap())
    args.append(nc.dram_tensor("out_0_dram", (1, SEQ, D), F32, kind="ExternalOutput").ap())
    build(nc, *args)
    r = _run(nc, [arrays], core_ids=[0])
    return r.results[0]["out_0_dram"]
```

```python
import math
from contextlib import ExitStack

import concourse.bass as bass
from concourse import mybir
import numpy as np

P = 128
F32, F32R, BF16 = mybir.dt.float32, mybir.dt.float32r, mybir.dt.bfloat16
I32, U32 = mybir.dt.int32, mybir.dt.uint32
ALU, ACT, AX = mybir.AluOpType, mybir.ActivationFunctionType, mybir.AxisListType

D, SEQ, MEM = 1024, 256, 256
KC = D // P
NT = SEQ // P
HD = 64
FOX_H, DIFF_H, MEM_H = 12, 6, 4
FOX_W, MEM_W = FOX_H * HD, MEM_H * HD
DV = 2 * HD
D_FF, N_EXP, E_FF = 2816, 8, 3584
ROT = 16
HALF = ROT // 2
THETA = 500000.0
EPS = 1e-5
SCALE = HD ** -0.5
NEG = -1.0e30
LAM_INIT = 0.8 - 0.6 * math.exp(-0.3)

UNIT = 2048
RAW, SPLIT = 6, 3
AHEAD = 4
WIDE = 256

PROJ = ([("mk", 0), ("mv", 0)]
        + [("q", i) for i in range(3)] + [("k", i) for i in range(3)] + [("v", i) for i in range(3)] + [("qm", 0)]
        + [("out", i) for i in range(4)] + [("mk", 1), ("mv", 1)]
        + [("kd", i) for i in range(3)] + [("qd", i) for i in range(3)]
        + [("vd", i) for i in range(3)] + [("qm", 1)]
        + [("out", i) for i in range(4)])
P_A, P_OUT0, P_M1, P_KV, P_QD, P_VD, P_OUT1, P_END = 2, 12, 16, 18, 21, 24, 28, 32
FFN_STEPS = D_FF // WIDE
FFN_UNITS = 3 * FFN_STEPS
U_FFN = P_KV
U_KV = U_FFN + FFN_UNITS
U_MOE = U_KV + (P_END - P_KV)
MOE_STEPS = E_FF // 512
MOE_UNITS = 6 * MOE_STEPS
EXTRAS = [U_MOE + MOE_UNITS * (N_EXP - 1) + pos for pos in (2, 8, 14, 20)]
TB_USES = (["T0", "oneT"] + [f"T{j}" for j in range(1, 6)] + ["gather0", "gather1", "T6"]
           + [f"back{i}" for i in range(4)])
TB = len(TB_USES)
FILL = list(np.cumsum([4, 4, 4, 8, 4, 4, 4, 5, 4]))
NORM_FILL = [0, 1, 2, 4, 5, 6, 8]
FILL_BUF = [0, 1, 0, 1, 1, 0, 1, 0, 1]


def unit_of(p):
    return p if p < P_KV else U_KV + p - P_KV


def is_extra(c):
    return c in EXTRAS


def ring(c):
    return c - sum(x < c for x in EXTRAS)


def unit_at(r):
    for x in EXTRAS:
        r += x <= r
    return r


def fill_of(p):
    if P_KV <= p < P_OUT1:
        return 5 if PROJ[p][0] in ("kd", "vd") else 6
    for f, end in ((0, P_A), (1, P_OUT0), (3, P_M1), (2, P_KV), (7, P_END)):
        if p < end:
            return f


def ffn_pos(kind, j):
    if kind == "D":
        return 4 + 3 * j if j < FFN_STEPS - 1 else FFN_UNITS - 1
    base = 0 if j == 0 else 3 * j - 1
    return base + (kind == "U")


def moe_pos(kind, j, a):
    if kind == "D":
        return (8 + 6 * j if j < MOE_STEPS - 1 else MOE_UNITS - 2) + a
    base = 0 if j == 0 else 6 * j - 2
    return base + 2 * (kind == "U") + a


def tb_count(use):
    return TB_USES.index(use) + 1


def tb_bank(use):
    return 6 + tb_count(use) % 2


def attention_plan(layer):
    if layer == 0:
        scores = [("fox", h) for h in range(FOX_H)] + [("mem", h) for h in range(MEM_H)]
        outs, last = scores, list(range(16))
    else:
        scores = [("diff", h) for h in range(2 * DIFF_H)] + [("mem", h) for h in range(MEM_H)]
        outs = [("diff", h) for h in range(DIFF_H)] + [("mem", h) for h in range(MEM_H)]
        last = [2 * r + 1 for r in range(DIFF_H)] + [12 + h for h in range(MEM_H)]
    return scores, outs, last


Y_BUF = [FILL_BUF[3], FILL_BUF[7]]
S_BASE = [0, 16]
R_BASE = [0, 16]


def build(nc, x, mem, positions, mix_norm_g, ffn_norm_g, mem_norm_g, w_mem_kv, w_out, w_in_a, b_forget, w_q_b,
          lambda_q1, lambda_k1, lambda_q2, lambda_k2, subln_g, kv_norm_g, w_kv_shared, w_gate_up_dense,
          w_down_dense, w_router, w_gate_up_moe, w_down_moe, final_norm_g, out):
    with ExitStack() as ctx:
        def sb(name, shape, dt=F32):
            return ctx.enter_context(nc.sbuf_tensor(name, shape, dt))

        def sem(name):
            return ctx.enter_context(nc.semaphore(name))

        raw = sb("raw", [P, RAW, UNIT])
        whi = sb("whi", [P, SPLIT, UNIT], F32R)
        wlo = sb("wlo", [P, SPLIT, UNIT], F32R)
        X = sb("X", [P, NT, D])
        hn = sb("hn", [P, NT, D])
        gain = sb("gain", [P, D])
        op_hi = [sb(f"op_hi{i}", [P, KC, SEQ], F32R) for i in range(2)]
        op_lo = [sb(f"op_lo{i}", [P, KC, SEQ], F32R) for i in range(2)]
        tok = sb("tok", [P, NT, D])
        attn = sb("attn", [P, len(EXTRAS) - 1, UNIT])

        def part(i, lo, hi, chunks):
            return attn[:, i, lo:hi].rearrange("p (c n) -> p c n", c=chunks)

        qT, kT, v = part(0, 0, 2 * FOX_W, 6), part(1, 0, 2 * FOX_W, 6), part(2, 0, 2 * FOX_W, NT)
        qmT = part(0, 2 * FOX_W, UNIT, 2)
        mkT = [sb("mkT0", [P, 2, MEM]), part(1, 2 * FOX_W, UNIT, 2)]
        mv = [sb("mv0", [P, 2, MEM_W]), part(2, 2 * FOX_W, UNIT, 2)]
        extra_slot = [attn[:, i, :] for i in range(len(EXTRAS) - 1)] + [tok[:].rearrange("p t d -> p (t d)")]
        start_gain = [gain[:], attn[:, 2, 0:D], attn[:, 1, 0:D]]
        prob = [sb(f"prob{i}", [P, 512]) for i in range(AHEAD)]
        probT = [sb(f"probT{i}", [P, 512]) for i in range(2)]
        h2T_hi = [sb(f"h2T_hi{i}", [P, 512], F32R) for i in range(2)]
        h2T_lo = [sb(f"h2T_lo{i}", [P, 512], F32R) for i in range(2)]
        gate_act, h2 = prob[0:2], probT[0:2]
        slot_oh = sb("slot_oh", [P, NT, P], F32R)
        slot_ohT = sb("slot_ohT", [P, SEQ], F32R)
        qtok = hn
        small_T = prob[3][0:FOX_H, 0:SEQ]
        hn_hi, hn_lo = (o[0][:].rearrange("p k n -> p (k n)").rearrange("p (t d) -> p t d", t=NT)
                        for o in (op_hi, op_lo))
        xg_hi, xg_lo = op_hi[1][:, :, 0:P], op_lo[1][:, :, 0:P]
        ye_hi, ye_lo = op_hi[1][:, :, P:2 * P], op_lo[1][:, :, P:2 * P]

        ident = sb("ident", [P, P])
        ident_bf = sb("ident_bf", [P, P], BF16)
        upper = sb("upper", [P, SEQ])
        slot_no = upper
        upper_bf = sb("upper_bf", [P, P], BF16)
        ones_bf = sb("ones_bf", [P, P], BF16)
        causal = sb("causal", [P, P], BF16)
        chunked = sb("chunked", [P, P], BF16)
        small_w = sb("small_w", [P, KC, 20])
        small_hi = sb("small_hi", [P, KC, 20], F32R)
        small_lo = sb("small_lo", [P, KC, 20], F32R)
        b_f = sb("b_f", [P, FOX_H])
        subln = sb("subln", [P, DV])
        lam_v = prob[1][:, 0:4 * HD].rearrange("p (a n) -> p a n", a=4)
        lam = sb("lam", [P, 8])
        pos_i = sb("pos_i", [P, NT], I32)
        pos_f = sb("pos_f", [P, NT])
        inv_f = sb("inv_f", [P, HALF])
        ang = sb("ang", [P, 3, NT, HALF])
        cosv = sb("cosv", [P, NT, HALF])
        sinv = sb("sinv", [P, NT, HALF])
        rot = prob[2][:, 0:4 * 12 * HALF].rearrange("p (a h n) -> p a h n", a=4, h=12)
        stat = sb("stat", [P, 8, 4, NT])
        ss_part = sb("ss_part", [P, NT, 4])
        warm = sb("warm", [P, 1])
        fg = sb("fg", [P, 3, NT, FOX_H])
        ncum = sb("ncum", [FOX_H, SEQ])
        negm = sb("negm", [P, 32, NT])
        rsum = sb("rsum", [P, 32, NT])
        rinv = sb("rinv", [P, 32, NT])
        o_sq = hn[:, :, FOX_W:D].rearrange("p t (i n) -> p i t n", i=2)
        o_ss = sb("o_ss", [P, 4, NT * DIFF_H])
        lg = sb("lg", [P, NT, N_EXP])
        top = sb("top", [P, NT, 8])
        top_i = sb("top_i", [P, NT, 8], U32)
        top_f = sb("top_f", [P, NT, 8])
        gates = sb("gates", [P, NT, 4])
        oh = sb("oh", [P, 2, NT, N_EXP])
        comb = sb("comb", [P, NT, N_EXP])
        member = sb("member", [P, NT, N_EXP + 1])
        member_bf = sb("member_bf", [P, NT, N_EXP], BF16)
        rank = sb("rank", [P, NT, N_EXP + 1])
        iota8 = sb("iota8", [P, N_EXP])
        over = sb("over", [P, 2])
        over_i = sb("over_i", [P, 1], I32)

        bank = [ctx.enter_context(nc.psum_tensor(f"bank{i}", [P, 512], F32)) for i in range(8)]
        score_bank = [bank[0], bank[1], bank[2], bank[7]]

        raw_in = [sem(f"raw_in{i}") for i in range(RAW)]
        extra_in = [sem(f"extra_in{i}") for i in range(len(EXTRAS))]
        hi_ready = sem("hi_ready")
        lo_ready = sem("lo_ready")
        unit_used = sem("unit_used")
        x_in, small_in = sem("x_in"), sem("small_in")
        mem_in = [sem(f"mem_in{t}") for t in range(NT)]
        start_gain_in = [sem(f"start_gain_in{n}") for n in range(3)]
        gain_in = sem("gain_in")
        consts = sem("consts")
        ident_ready = sem("ident_ready")
        masks = sem("masks")
        small_hi_ready, small_lo_ready = sem("small_hi_ready"), sem("small_lo_ready")
        norm_ss = sem("norm_ss")
        norm_var = sem("norm_var")
        norm_std = sem("norm_std")
        hn_ready = sem("hn_ready")
        tr_ready = sem("tr_ready")
        fill_hi = sem("fill_hi")
        fill_lo = sem("fill_lo")
        proj_out = sem("proj_out")
        flT_ready, flT_out = sem("flT_ready"), sem("flT_out")
        logitT_ready, logitT_out = sem("logitT_ready"), sem("logitT_out")
        fl_ready, fl_sum, fl_ln, logf_ready = sem("fl_ready"), sem("fl_sum"), sem("fl_ln"), sem("logf_ready")
        cum_ready, ncum_ready = sem("cum_ready"), sem("ncum_ready")
        lam_ready, lam_exp, ang_ready, sin_ready = sem("lam_ready"), sem("lam_exp"), sem("ang_ready"), sem("sin_ready")
        rot_ready = sem("rot_ready")
        qk_tr = sem("qk_tr")
        qk_out = sem("qk_out")
        score_ready = sem("score_ready")
        rowmax = sem("rowmax")
        exp_done = sem("exp_done")
        prob_ready = sem("prob_ready")
        pT_ready = sem("pT_ready")
        pT_out = sem("pT_out")
        pv_ready = sem("pv_ready")
        o_out = sem("o_out")
        o_squared = sem("o_squared")
        o_norm = sem("o_norm")
        o_tr = sem("o_tr")
        silu_done = sem("silu_done")
        mul_done = sem("mul_done")
        h2_hi, h2_lo = sem("h2_hi"), sem("h2_lo")
        x_added = sem("x_added")
        logit_ready, top_ready, gate_exp = sem("logit_ready"), sem("top_ready"), sem("gate_exp")
        member_ready, rank_ready, route_ready = sem("member_ready"), sem("rank_ready"), sem("route_ready")
        oh_ready = sem("oh_ready")
        tb_ready = sem("tb_ready")
        ohT_out = sem("ohT_out")
        xg_hi_ready, xg_lo_ready = sem("xg_hi_ready"), sem("xg_lo_ready")
        ye_hi_ready, ye_lo_ready = sem("ye_hi_ready"), sem("ye_lo_ready")
        hn_hi_ready, hn_lo_ready = sem("hn_hi_ready"), sem("hn_lo_ready")
        slots_ready = sem("slots_ready")
        x_final = sem("x_final")
        out_done = sem("out_done")
        act_step, dve_step = sem("act_step"), sem("dve_step")

        def ss_count(n):
            return n + 1 - (n > 4)

        def rows(w):
            return w.rearrange("(k p) n -> p k n", p=P)

        mem_kv_v = [rows(w_mem_kv[i]) for i in range(2)]
        in_a_v, q_b_v, kv_v = rows(w_in_a[0]), rows(w_q_b[0]), rows(w_kv_shared)
        out_v = [rows(w_out[i]) for i in range(2)]
        gu_v, down_v = rows(w_gate_up_dense[0]), rows(w_down_dense[0])

        def proj_source(p):
            what, i = PROJ[p]
            c = WIDE * i
            if what in ("mk", "mv"):
                c = MEM_W * (what == "mv")
                return mem_kv_v[i][:, :, c:c + WIDE]
            if what in ("q", "k", "v"):
                c += FOX_W * "qkv".index(what)
                return in_a_v[:, :, c:c + WIDE]
            if what == "qm" and i == 0:
                return in_a_v[:, :, 3 * FOX_W + FOX_H:3 * FOX_W + FOX_H + MEM_W]
            if what == "qm":
                return q_b_v[:, :, FOX_W:FOX_W + MEM_W]
            if what == "out":
                return out_v[p >= P_OUT1][:, :, c:c + WIDE]
            if what == "kd":
                return kv_v[:, :, c:c + WIDE]
            if what == "vd":
                return kv_v[:, :, FOX_W + c:FOX_W + c + WIDE]
            return q_b_v[:, :, c:c + WIDE]

        def wide(t3, slot):
            return t3[:, slot, :].rearrange("p (k n) -> p k n", k=KC)

        block = ctx.enter_context(nc.Block())

        @block.sync
        def _(sp):
            def load(c, turns, src, shape):
                if is_extra(c):
                    i = EXTRAS.index(c)
                    sp.wait_ge(o_tr, 3)
                    dst, landed = extra_slot[i].rearrange("p (k n) -> p k n", k=shape), extra_in[i]
                else:
                    r = ring(c)
                    if not (isinstance(turns, int) and r + RAW * turns < RAW):
                        sp.wait_ge(lo_ready, unit_at(r - RAW) + RAW * turns + 1)
                    dst, landed = raw[:, r % RAW, :].rearrange("p (k n) -> p k n", k=shape), raw_in[r % RAW]
                sp.dma_start(dst, src).then_inc(landed, 16)

            for t in range(NT):
                sp.dma_start(tok[:, t, :], mem[0, P * t:P * (t + 1), :]).then_inc(mem_in[t], 16)
            sp.dma_start(gain[:], mem_norm_g[0:1, :].to_broadcast([P, D])).then_inc(start_gain_in[0], 16)
            for p in range(P_KV):
                load(unit_of(p), 0, proj_source(p), KC)
                if p == 0:
                    sp.dma_start(X[:], x[0].rearrange("(t p) d -> p t d", p=P)).then_inc(x_in, 16)

            def ffn_load(kind, j, turns=0, moved=0):
                c = U_FFN + ffn_pos(kind, j)
                if kind == "D":
                    src = down_v[:, bass.ds(2 * (j + moved), 2), :]
                    return load(c, turns, src, 2)
                col = (D_FF if kind == "U" else 0) + WIDE * (j + moved)
                load(c, turns, gu_v[:, :, bass.ds(col, WIDE)], KC)

            ffn_load("G", 0)
            ffn_load("U", 0)
            with sp.Fori(0, (FFN_STEPS - 1) // 2) as it:
                for j in (1, 2):
                    ffn_load("G", j, it, 2 * it)
                    ffn_load("U", j, it, 2 * it)
                    ffn_load("D", j - 1, it, 2 * it)
            ffn_load("D", FFN_STEPS - 1)
            for p in range(P_KV, P_END):
                load(unit_of(p), 0, proj_source(p), KC)

            def expert_loads(ps):
                def expert(e, extra=False):
                    gu_e = w_gate_up_moe[0].rearrange("e (k p) n -> e p k n", p=P)[bass.ds(e, 1)].squeeze(0)
                    dn_e = w_down_moe[0].rearrange("e (k p) n -> e p k n", p=P)[bass.ds(e, 1)].squeeze(0)
                    base = U_MOE + (ps * N_EXP + (e if isinstance(e, int) else 1)) * MOE_UNITS
                    turns = 0 if isinstance(e, int) else (MOE_UNITS // RAW) * e - MOE_UNITS // RAW

                    def go(kind, j):
                        for a in range(2):
                            c = base + moe_pos(kind, j, a)
                            if kind == "D":
                                src = dn_e[:, 4 * j + 2 * a:4 * j + 2 * a + 2, :]
                            else:
                                col = (E_FF if kind == "U" else 0) + 512 * j
                                src = gu_e[:, 4 * a:4 * a + 4, col:col + 512]
                            if extra == is_extra(c):
                                load(c, turns, src, 2 if kind == "D" else 4)

                    for j in range(MOE_STEPS):
                        go("G", j)
                        go("U", j)
                        if j:
                            go("D", j - 1)
                        if not j and ps == 0 and not extra and isinstance(e, int) and e == 0:
                            expert(N_EXP - 1, extra=True)
                    go("D", MOE_STEPS - 1)

                expert(0)
                with sp.Fori(1, N_EXP - 1) as e:
                    expert(e)
                expert(N_EXP - 1)

            expert_loads(0)
            sp.wait_ge(route_ready, 1)
            flag = sp.value_load(over_i[0:1, 0:1], min_val=0, max_val=1)
            with sp.If(flag == 1):
                expert_loads(1)
            for t in range(NT):
                sp.wait_ge(hn_ready, 30 + 2 * t)
                sp.dma_start(out[0, P * t:P * (t + 1), :], hn[:, t, :]).then_inc(out_done, 16)
            sp.wait_ge(out_done, 16 * NT)

        @block.gpsimd
        def _(pool):
            gains = [mem_norm_g[0], mix_norm_g[0], mem_norm_g[1], ffn_norm_g[0], kv_norm_g, mix_norm_g[1],
                     ffn_norm_g[1], final_norm_g]

            def load_gain(n):
                pool.wait_ge(hn_ready, 4 * n)
                g = gains[n].rearrange("(a d) -> a d", a=1)
                pool.dma_start(gain[:], g.to_broadcast([P, D])).then_inc(gain_in, 16)

            for n, g in ((1, mix_norm_g[0:1, :]), (2, mem_norm_g[1:2, :])):
                pool.dma_start(start_gain[n], g.to_broadcast([P, D])).then_inc(start_gain_in[n], 16)
            g = nc.gpsimd
            g.memset(ident[:], 0.0).then_inc(masks, 1)
            g.memset(warm[:], 1.0).then_inc(masks, 1)
            pool.wait_ge(masks, 2)
            g.affine_select(out=ident[:], in_=ident[:], compare_op=ALU.not_equal, fill=1.0, base=0,
                            pattern=[[-1, P]], channel_multiplier=1).then_inc(ident_ready, 1)
            smalls = [
                (small_w[:, :, 0:FOX_H], in_a_v[:, :, 3 * FOX_W:3 * FOX_W + FOX_H]),
                (small_w[:, :, FOX_H:20], rows(w_router[0])),
                (b_f[:], b_forget[0:1, :].to_broadcast([P, FOX_H])),
                (subln[:], subln_g[0:1, :].to_broadcast([P, DV])),
                (pos_i[:], positions[0].rearrange("(t p) -> p t", p=P)),
            ] + [(lam_v[:, i, :], l[0:1, :].to_broadcast([P, HD]))
                 for i, l in enumerate((lambda_q1, lambda_k1, lambda_q2, lambda_k2))]
            assert len(smalls) == 9
            with nc.allow_non_contiguous_dma("small columns"):
                for dst, src in smalls:
                    pool.dma_start(dst, src).then_inc(small_in, 16)

            g.memset(upper[:], 1.0).then_inc(masks, 1)
            g.memset(ones_bf[:], 1.0).then_inc(masks, 1)
            g.memset(causal[:], 0.0).then_inc(masks, 1)
            g.memset(chunked[:], 0.0).then_inc(masks, 1)
            pool.wait_ge(masks, 6)
            g.affine_select(out=upper[:], in_=upper[:], compare_op=ALU.is_ge, fill=0.0, base=0,
                            pattern=[[1, SEQ]], channel_multiplier=-1).then_inc(masks, 1)
            g.affine_select(out=causal[:], in_=causal[:], compare_op=ALU.is_ge, fill=NEG, base=0,
                            pattern=[[-1, P]], channel_multiplier=1).then_inc(masks, 1)
            g.affine_select(out=chunked[:, HD:P], in_=chunked[:, HD:P], compare_op=ALU.is_ge, fill=NEG, base=-HD,
                            pattern=[[0, HD]], channel_multiplier=1).then_inc(masks, 1)
            pool.wait_ge(masks, 9)
            pool.wait_ge(ident_ready, 1)
            g.tensor_copy(ident_bf[:], ident[:]).then_inc(masks, 1)
            g.tensor_copy(upper_bf[:], upper[:, 0:P]).then_inc(masks, 1)
            g.iota(iota8[:], pattern=[[1, N_EXP]], base=0, channel_multiplier=0,
                   allow_small_or_imprecise_dtypes=True).then_inc(masks, 1)
            for i in range(HALF):
                f = float(np.float32(THETA) ** np.float32(-(np.float32(i) * np.float32(2.0) / np.float32(ROT))))
                g.memset(inv_f[:, i:i + 1], f).then_inc(masks, 1)
            g.memset(member[:, :, N_EXP:N_EXP + 1], 0.0).then_inc(masks, 1)
            pool.wait_ge(masks, 13 + HALF)
            g.memset(rank[:, :, N_EXP:N_EXP + 1], 0.0).then_inc(consts, 1)
            for n in range(3, 8):
                load_gain(n)
                if n == 3:
                    pool.wait_ge(cum_ready, 1)
                    g.iota(slot_no[:], pattern=[[1, SEQ]], base=0, channel_multiplier=0,
                           allow_small_or_imprecise_dtypes=True).then_inc(slots_ready, 1)

        @block.scalar
        def _(act):
            a = nc.scalar
            own = [0]

            def step(ins):
                own[0] += 1
                ins.then_inc(act_step, 1)
                act.wait_ge(act_step, own[0])

            def split_hi(c, turns=0):
                if is_extra(c):
                    src = extra_slot[EXTRAS.index(c)]
                    act.wait_ge(extra_in[EXTRAS.index(c)], 16)
                else:
                    r = ring(c)
                    src = raw[:, r % RAW, :]
                    act.wait_ge(raw_in[r % RAW], (r // RAW + 1) * 16 + turns * 16)
                if not (isinstance(turns, int) and c + RAW * turns < SPLIT):
                    act.wait_ge(unit_used, c + RAW * turns - SPLIT + 1)
                a.copy(whi[:, c % SPLIT, :], src).then_inc(hi_ready, 1)

            def sqrt_table():
                a.activation(warm[:], warm[:], ACT.Sqrt)

            def square_piece(t, cols, i):
                return a.activation(hn[:, t, cols], X[:, t, cols], ACT.Square, accum_out=ss_part[:, t, i:i + 1])

            def norm_act(n, src, ready):
                if src is not None:
                    if n:
                        act.wait_ge(tr_ready, 4 * n)
                    for t in range(NT):
                        act.wait_ge(ready[min(t, len(ready) - 1)], 16)
                        ins = a.activation(hn[:, t, :], src[:, t, :], ACT.Square, accum_out=stat[:, n, 0, t:t + 1])
                    ins.then_inc(norm_ss, 1)
                act.wait_ge(norm_var, ss_count(n) + (n > 4))
                a.activation(stat[:, n, 2, :], stat[:, n, 1, :], ACT.Sqrt).then_inc(norm_std, 1)

            def norm_fill_hi(n):
                if n < 7:
                    buf = op_hi[FILL_BUF[NORM_FILL[n]]]
                    for g in range(4):
                        act.wait_ge(tr_ready, 4 * n + g + 1)
                        t, h = g // 2, g % 2
                        a.copy(buf[:, 4 * h:4 * h + 4, t * P:(t + 1) * P],
                               bank[g][:].rearrange("p (c n) -> p c n", c=4)).then_inc(fill_hi, 1)

            def split_until(n, state=[0]):
                while state[0] < n:
                    split_hi(unit_of(state[0]))
                    state[0] += 1

            act.wait_ge(ident_ready, 1)
            sqrt_table()
            norm_act(0, tok, mem_in)
            split_until(1)
            norm_fill_hi(0)
            norm_act(1, X, [x_in])
            split_until(2)
            split_until(3)
            norm_fill_hi(1)
            norm_act(2, tok, mem_in)
            split_until(4)
            act.wait_ge(small_in, 16 * 9)
            a.copy(small_hi[:], small_w[:]).then_inc(small_hi_ready, 1)
            split_until(5)
            norm_fill_hi(2)
            split_until(P_A + 7)
            act.wait_ge(lam_ready, 1)
            a.activation(lam[:, 2:4], lam[:, 0:2], ACT.Exp).then_inc(lam_exp, 1)
            act.wait_ge(fl_sum, 1)
            step(a.activation(fg[:, 1], fg[:, 1], ACT.Exp))
            a.activation(fg[:, 1], fg[:, 1], ACT.Ln, bias=1.0).then_inc(fl_ln, 1)
            split_until(P_A + 12)
            act.wait_ge(ang_ready, 1)
            a.activation(sinv[:], ang[:, 1], ACT.Sin)
            a.activation(cosv[:], ang[:, 2], ACT.Sin).then_inc(sin_ready, 1)
            split_until(P_OUT0 + 3)

            def attention_act(layer):
                scores, outs, last = attention_plan(layer)
                sb0, rb0 = S_BASE[layer], R_BASE[layer]
                done = [0]

                def exps(upto):
                    while done[0] <= min(upto, len(scores) - 1):
                        s = done[0]
                        g = sb0 + s
                        act.wait_ge(rowmax, g + 1)
                        if s >= AHEAD:
                            owner = min(r for r in range(len(outs)) if last[r] >= s - AHEAD)
                            act.wait_ge(pT_ready, rb0 + owner + 1)
                        elif layer:
                            act.wait_ge(pT_ready, rb0)
                        w0 = P if scores[s][0] != "mem" else MEM
                        w1 = MEM
                        a.activation(prob[s % AHEAD][:, 0:w0], score_bank[s % AHEAD][:, 0:w0], ACT.Exp,
                                     bias=negm[:, g, 0:1], accum_out=rsum[:, g, 0:1])
                        a.activation(prob[s % AHEAD][:, w0:w0 + w1], score_bank[s % AHEAD][:, w0:w0 + w1], ACT.Exp,
                                     bias=negm[:, g, 1:2], accum_out=rsum[:, g, 1:2]).then_inc(exp_done, 1)
                        done[0] += 1

                def fill(r):
                    kind, h = outs[r]
                    if kind == "diff":
                        act.wait_ge(o_out, r + 1)
                        for t in range(NT):
                            ins = a.activation(o_sq[:, r % 2, t, :], tok[:, t, DV * h:DV * (h + 1)], ACT.Square,
                                               accum_out=o_ss[:, 0, DIFF_H * t + h:DIFF_H * t + h + 1])
                        ins.then_inc(o_squared, 1)
                        return
                    if h % 2 == 0:
                        return
                    c = h // 2 + (6 if kind == "mem" else 0)
                    act.wait_ge(pv_ready, rb0 + r + 1)
                    a.copy(op_hi[Y_BUF[layer]][:, c, :], bank[5 + (r // 2) % 2][:, 0:SEQ]).then_inc(fill_hi, 1)

                exps(AHEAD - 1)
                for r in range(len(outs)):
                    w = 512 if outs[r][0] == "mem" else 384
                    act.wait_ge(pT_ready, rb0 + r + 1)
                    if rb0 + r >= 2:
                        act.wait_ge(pv_ready, rb0 + r - 1)
                    a.copy(probT[r % 2][:, 0:w], bank[3 + r % 2][:, 0:w]).then_inc(pT_out, 1)
                    if r:
                        fill(r - 1)
                    exps(last[r] + AHEAD)
                    if layer and r == DIFF_H:
                        act.wait_ge(norm_var, 6)
                        a.activation(o_ss[:, 2], o_ss[:, 1], ACT.Sqrt).then_inc(norm_std, 1)
                fill(len(outs) - 1)

            def out_squares(first, units):
                sqrt_table()
                for i in range(4):
                    if i < 3:
                        split_hi(units[i])
                    act.wait_ge(proj_out, first + i + 1)
                    for t in range(NT):
                        ins = square_piece(t, slice(WIDE * i, WIDE * (i + 1)), i)
                ins.then_inc(norm_ss, 1)

            attention_act(0)
            out_squares(P_OUT0, [P_OUT0 + 3, P_M1, P_M1 + 1])
            norm_act(3, None, None)
            split_hi(U_FFN)
            norm_fill_hi(3)
            split_hi(U_FFN + 1)

            def ffn_silu(j, turns=0):
                act.wait_ge(unit_used, U_FFN + ffn_pos("G", j) + 1 + RAW * turns)
                a.activation(gate_act[j % 2][:], bank[4 + 2 * (j % 2)][:], ACT.Silu).then_inc(silu_done, 1)

            def ffn_h2_hi(j, moved=0):
                act.wait_ge(mul_done, j + 1 + moved)
                a.copy(h2T_hi[j % 2][:], h2[j % 2][:]).then_inc(h2_hi, 1)

            ffn_silu(0)
            with act.Fori(0, (FFN_STEPS - 1) // 2) as it:
                for j in (1, 2):
                    split_hi(U_FFN + ffn_pos("G", j), it)
                    ffn_h2_hi(j - 1, 2 * it)
                    split_hi(U_FFN + ffn_pos("U", j), it)
                    ffn_silu(j, it)
                    split_hi(U_FFN + ffn_pos("D", j - 1), it)
            split_hi(U_FFN + FFN_UNITS - 1)
            ffn_h2_hi(FFN_STEPS - 1)

            split_hi(U_KV)
            split_hi(U_KV + 1)
            sqrt_table()
            for q in range(4):
                act.wait_ge(x_added, q + 1)
                ins = square_piece(q // 2, slice(512 * (q % 2), 512 * (q % 2 + 1)), q % 2)
            ins.then_inc(norm_ss, 1)
            norm_act(4, None, None)
            norm_fill_hi(4)
            split_hi(U_KV + 2)
            split_hi(U_KV + 3)
            norm_fill_hi(5)
            for u in range(4, 12):
                split_hi(U_KV + u)
            attention_act(1)
            for b in range(3):
                act.wait_ge(o_tr, b + 1)
                a.copy(op_hi[Y_BUF[1]][:, 2 * b:2 * b + 2, :],
                       bank[b][:].rearrange("p (c n) -> p c n", c=2)).then_inc(fill_hi, 1)
            split_hi(U_KV + 12)
            out_squares(P_OUT1, [U_KV + 13, U_MOE, U_MOE + 1])
            norm_act(6, None, None)
            norm_fill_hi(6)
            a.copy(hn_hi, hn[:]).then_inc(hn_hi_ready, 1)
            split_hi(U_MOE + 2)
            act.wait_ge(top_ready, 1)
            a.activation(gates[:, :, 1], gates[:, :, 0], ACT.Exp).then_inc(gate_exp, 1)

            def experts_act(ps):
                ub = U_MOE + ps * N_EXP * MOE_UNITS
                tb = 2 + TB * N_EXP * ps
                hb = FFN_STEPS + MOE_STEPS * N_EXP * ps

                def halves(use, base, dst, done):
                    for i in range(2):
                        act.wait_ge(tb_ready, base + tb_count(f"{use}{i}"))
                        a.copy(dst[:, 4 * i:4 * i + 4, :],
                               bank[tb_bank(f"{use}{i}")][:].rearrange("p (c n) -> p c n", c=4)).then_inc(done, 1)

                def output_hi(e):
                    act.wait_ge(unit_used, ub + MOE_UNITS * e)
                    for i in range(2):
                        a.copy(ye_hi[:, 4 * i:4 * i + 4, :],
                               bank[i][:].rearrange("p (c n) -> p c n", c=4)).then_inc(ye_hi_ready, 1)

                def expert(e, turns, first=False, final=False):
                    unit0 = ub + MOE_UNITS * (e if isinstance(e, int) else 1)

                    def hi(kind, j, k):
                        if not (first and ps == 0 and moe_pos(kind, j, k) < 3):
                            split_hi(unit0 + moe_pos(kind, j, k), turns)

                    def evac_T(j):
                        act.wait_ge(tb_ready, tb + TB * e + tb_count(f"T{j}") - (2 if final and j == MOE_STEPS - 1 else 0))
                        a.copy(h2T_hi[j % 2][:], bank[tb_bank(f"T{j}")][:]).then_inc(h2_hi, 1)

                    def silu(j):
                        act.wait_ge(unit_used, ub + moe_pos("G", j, 1) + 1 + MOE_UNITS * e)
                        act.wait_ge(mul_done, hb + MOE_STEPS * e + max(j - 1, 0))
                        a.activation(gate_act[j % 2][:], bank[2 + 2 * (j % 2)][:], ACT.Silu).then_inc(silu_done, 1)

                    hi("G", 0, 0)
                    hi("G", 0, 1)
                    if not first:
                        output_hi(e)
                    hi("U", 0, 0)
                    hi("U", 0, 1)
                    hi("G", 1, 0)
                    silu(0)
                    for j in range(1, MOE_STEPS):
                        if j > 1:
                            hi("G", j, 0)
                        hi("G", j, 1)
                        hi("U", j, 0)
                        evac_T(j - 1)
                        hi("U", j, 1)
                        hi("D", j - 1, 0)
                        silu(j)
                        hi("D", j - 1, 1)
                        if j == 1:
                            act.wait_ge(tb_ready, tb + TB * e + tb_count("oneT"))
                            a.copy(slot_ohT[:], bank[tb_bank("oneT")][:, 0:SEQ]).then_inc(ohT_out, 1)
                    if not final:
                        halves("gather", tb + TB * e, xg_hi, xg_hi_ready)
                    hi("D", MOE_STEPS - 1, 0)
                    evac_T(MOE_STEPS - 1)
                    hi("D", MOE_STEPS - 1, 1)

                halves("gather", tb - tb_count("gather1"), xg_hi, xg_hi_ready)
                expert(0, 0, first=True)
                with act.Fori(1, N_EXP - 1) as e:
                    expert(e, (MOE_UNITS // RAW) * e - MOE_UNITS // RAW)
                expert(N_EXP - 1, 0, final=True)
                output_hi(N_EXP)

            experts_act(0)
            act.wait_ge(route_ready, 1)
            flag = act.value_load(over_i[0:1, 0:1], min_val=0, max_val=1)
            with act.If(flag == 1):
                experts_act(1)
            sqrt_table()
            act.wait_ge(x_final, 1)
            for t in range(NT):
                a.activation(hn[:, t, :], X[:, t, :], ACT.Square, accum_out=stat[:, 7, 0, t:t + 1]).then_inc(norm_ss, 1)
            for t in range(NT):
                act.wait_ge(norm_var, 8 + t)
                a.activation(stat[:, 7, 2, t:t + 1], stat[:, 7, 1, t:t + 1], ACT.Sqrt).then_inc(norm_std, 1)

        @block.vector
        def _(dve):
            d = nc.vector
            own = [0]

            def step(ins):
                own[0] += 1
                ins.then_inc(dve_step, 1)
                dve.wait_ge(dve_step, own[0])

            def split_lo(c, turns=0):
                dve.wait_ge(hi_ready, c + RAW * turns + 1)
                src = extra_slot[EXTRAS.index(c)] if is_extra(c) else raw[:, ring(c) % RAW, :]
                d.tensor_tensor(wlo[:, c % SPLIT, :], src, whi[:, c % SPLIT, :].bitcast(F32),
                                ALU.subtract).then_inc(lo_ready, 1)

            def split_until(n, state=[0]):
                while state[0] < n:
                    split_lo(unit_of(state[0]))
                    state[0] += 1

            def norm_dve(n, src, eps_count, parts=0):
                dve.wait_ge(norm_ss, ss_count(n))
                if parts:
                    step(d.tensor_reduce(stat[:, n, 0, :], ss_part[:, :, 0:parts], AX.X, ALU.add))
                d.tensor_scalar(stat[:, n, 1, :], stat[:, n, 0, :], 1.0 / D, EPS, ALU.mult,
                                ALU.add).then_inc(norm_var, 1)
                dve.wait_ge(norm_std, eps_count)
                step(d.reciprocal(stat[:, n, 3, :], stat[:, n, 2, :]))
                apply_norm(n, src, n)

            def apply_norm(n, src, of):
                if n < 3:
                    dve.wait_ge(start_gain_in[n], 16)
                else:
                    dve.wait_ge(gain_in, 16 * (n - 2))
                g = start_gain[n] if n < 3 else gain
                for t in range(NT):
                    for h in range(2):
                        cols = slice(512 * h, 512 * (h + 1))
                        d.scalar_tensor_tensor(out=hn[:, t, cols], in0=src[:, t, cols], scalar=stat[:, of, 3, t:t + 1],
                                               in1=g[:, cols], op0=ALU.mult, op1=ALU.mult).then_inc(hn_ready, 1)

            def norm_fill_lo(n):
                f = NORM_FILL[n]
                hi, lo = op_hi[FILL_BUF[f]], op_lo[FILL_BUF[f]]
                for g in range(4):
                    t, h = g // 2, g % 2
                    dve.wait_ge(fill_hi, int(FILL[f]) - 3 + g)
                    d.tensor_tensor(lo[:, 4 * h:4 * h + 4, t * P:(t + 1) * P],
                                    bank[g][:].rearrange("p (c n) -> p c n", c=4),
                                    hi[:, 4 * h:4 * h + 4, t * P:(t + 1) * P].bitcast(F32),
                                    ALU.subtract).then_inc(fill_lo, 1)

            def take(p):
                what, i = PROJ[p]
                dve.wait_ge(unit_used, unit_of(p) + 1)
                b2 = bank[4 + p % 4][:].rearrange("p (c n) -> p c n", c=2)
                cols = slice(WIDE * i, WIDE * (i + 1))
                if what == "mk":
                    ins = d.tensor_copy(mkT[i][:], b2)
                elif what == "mv":
                    ins = d.tensor_copy(mv[i][:], b2)
                elif what == "q":
                    ins = d.tensor_scalar(qT[:, 2 * i:2 * i + 2, :], b2, SCALE, None, ALU.mult)
                elif what == "k":
                    ins = d.tensor_copy(kT[:, 2 * i:2 * i + 2, :], b2)
                elif what in ("v", "vd"):
                    ins = d.tensor_copy(v[:, :, cols], b2)
                elif what == "qm":
                    ins = d.tensor_scalar(qmT[:], b2, SCALE, None, ALU.mult)
                elif what == "out":
                    ins = d.tensor_tensor(X[:, :, cols], X[:, :, cols], b2, ALU.add)
                elif what == "kd":
                    ins = d.tensor_copy(tok[:, :, cols], b2)
                else:
                    ins = d.tensor_scalar(qtok[:, :, cols], b2, SCALE, None, ALU.mult)
                ins.then_inc(proj_out, 1)

            norm_dve(0, tok, 1)
            split_until(1)
            norm_fill_lo(0)
            norm_dve(1, X, 2)
            split_until(2)
            split_until(3)
            take(0)
            norm_fill_lo(1)
            norm_dve(2, tok, 3)
            split_until(4)
            take(1)
            dve.wait_ge(small_hi_ready, 1)
            d.tensor_tensor(small_lo[:], small_w[:], small_hi[:].bitcast(F32), ALU.subtract).then_inc(small_lo_ready, 1)
            split_until(5)
            norm_fill_lo(2)

            def lambda_dots():
                dve.wait_ge(small_in, 16 * 9)
                lam4 = lam_v.rearrange("p (a b) n -> p a b n", a=2)
                step(d.tensor_tensor(lam4[:, :, 0, :], lam4[:, :, 0, :], lam4[:, :, 1, :], ALU.mult))
                d.tensor_reduce(lam[:, 0:2], lam4[:, :, 0, :], AX.X, ALU.add).then_inc(lam_ready, 1)
                d.tensor_scalar(subln[:], subln[:], 1.0 - LAM_INIT, None, ALU.mult)

            def forget_sums():
                dve.wait_ge(fl_ready, 1)
                for t in range(NT):
                    ins = d.tensor_tensor(fg[:, 0, t, :], bank[2][:, FOX_H * t:FOX_H * (t + 1)], b_f[:], ALU.add)
                step(ins)
                step(d.tensor_scalar(fg[:, 2], fg[:, 0], -1.0, None, ALU.mult))
                d.tensor_tensor(fg[:, 1], fg[:, 0], fg[:, 2], ALU.min).then_inc(fl_sum, 1)

            def forget_logs():
                dve.wait_ge(fl_ln, 1)
                dve.wait_ge(fl_sum, 1)
                d.scalar_tensor_tensor(out=fg[:, 2], in0=fg[:, 0], scalar=0.0, in1=fg[:, 1], op0=ALU.min,
                                       op1=ALU.subtract).then_inc(logf_ready, 1)
                dve.wait_ge(lam_exp, 1)
                step(d.tensor_tensor(lam[:, 4:5], lam[:, 3:4], lam[:, 2:3], ALU.subtract))
                step(d.tensor_scalar(lam[:, 5:6], lam[:, 4:5], LAM_INIT, None, ALU.subtract))

            neg_lam = lam[:, 5:6]

            def angles_start():
                dve.wait_ge(small_in, 16 * 9)
                dve.wait_ge(consts, 1)
                step(d.tensor_copy(pos_f[:], pos_i[:]))
                for t in range(NT):
                    ins = d.tensor_scalar(ang[:, 0, t, :], inv_f[:], pos_f[:, t:t + 1], None, ALU.mult)
                step(ins)

            def angles(w):
                two_pi = 2 * math.pi
                c1 = 6.28125
                c2 = float(np.float32(np.float64(two_pi - c1) * 2 ** 20 // 1 / 2 ** 20))
                c3 = float(np.float32(two_pi - c1 - c2))
                magic = float(3 * 2 ** 22)
                turn = rot[:, w, 0:NT, :]
                step(d.tensor_scalar(turn, ang[:, 0], 1.0 / two_pi, 0.25 * (w - 1), ALU.mult, ALU.add))
                step(d.tensor_scalar(turn, turn, magic, None, ALU.add))
                step(d.tensor_scalar(turn, turn, magic, None, ALU.subtract))
                prev = ang[:, 0]
                for c in (c1, c2, c3):
                    step(d.scalar_tensor_tensor(out=ang[:, w], in0=turn, scalar=-c, in1=prev, op0=ALU.mult,
                                                op1=ALU.add))
                    prev = ang[:, w]
                if w == 2:
                    step(d.tensor_scalar(ang[:, w], ang[:, w], math.pi / 2, None, ALU.add))
                ins = d.tensor_scalar(ang[:, w], ang[:, w], 3.1415925, -3.1415925, ALU.min, ALU.max)
                if w == 2:
                    ins.then_inc(ang_ready, 1)
                else:
                    step(ins)

            split_until(P_A + 3)
            for p in range(P_A, P_OUT0):
                take(p)
                split_until(min(p + 4, P_OUT0 + 3))
                if p == P_A + 1:
                    dve.wait_ge(flT_ready, 1)
                    d.tensor_copy(small_T, bank[3][0:FOX_H, 0:SEQ]).then_inc(flT_out, 1)
                if p == P_A + 2:
                    lambda_dots()
                    forget_sums()
                if p == P_A + 4:
                    forget_logs()
                if p == P_A + 6:
                    dve.wait_ge(cum_ready, 1)
                    d.tensor_scalar(ncum[:], bank[3][0:FOX_H, 256:512], -1.0, None, ALU.mult).then_inc(ncum_ready, 1)
                    angles_start()
                if p in (P_A + 7, P_A + 8):
                    angles(p - P_A - 6)

            def attention_dve(layer):
                scores, outs, last = attention_plan(layer)
                sb0, rb0 = S_BASE[layer], R_BASE[layer]
                done = [0]

                def maxima(upto):
                    while done[0] <= min(upto, len(scores) - 1):
                        s = done[0]
                        g = sb0 + s
                        dve.wait_ge(score_ready, g + 1)
                        w0 = P if scores[s][0] != "mem" else MEM
                        d.tensor_reduce(negm[:, g, 0:1], score_bank[s % AHEAD][:, 0:w0], AX.X, ALU.max, negate=True)
                        d.tensor_reduce(negm[:, g, 1:2], score_bank[s % AHEAD][:, w0:w0 + MEM], AX.X, ALU.max,
                                        negate=True).then_inc(rowmax, 1)
                        done[0] += 1

                def fill(r):
                    kind, h = outs[r]
                    if kind == "diff":
                        dve.wait_ge(pv_ready, rb0 + r + 1)
                        d.tensor_copy(tok[:, :, DV * h:DV * (h + 1)],
                                      bank[5 + r % 2][:, 0:256].rearrange("p (t n) -> p t n", t=NT)).then_inc(o_out, 1)
                        return
                    if h % 2 == 0:
                        return
                    c = h // 2 + (6 if kind == "mem" else 0)
                    base = int(FILL[2] if layer == 0 else FILL[6])
                    dve.wait_ge(fill_hi, base + (c + 1 if layer == 0 else c - 5))
                    d.tensor_tensor(op_lo[Y_BUF[layer]][:, c, :], bank[5 + (r // 2) % 2][:, 0:SEQ],
                                    op_hi[Y_BUF[layer]][:, c, :].bitcast(F32), ALU.subtract).then_inc(fill_lo, 1)

                def normalise(r):
                    kind, h = outs[r]
                    s = last[r]
                    g = sb0 + s
                    dve.wait_ge(exp_done, g + 1)
                    w0 = P if kind != "mem" else MEM
                    if kind == "diff":
                        step(d.reciprocal(rinv[:, g - 1:g + 1, :], rsum[:, g - 1:g + 1, :]))
                        step(d.tensor_scalar(rinv[:, g, :], rinv[:, g, :], neg_lam, None, ALU.mult))
                        p1, p2 = prob[(s - 1) % AHEAD], prob[s % AHEAD]
                        for t, (c, w) in enumerate(((0, P), (P, MEM))):
                            step(d.tensor_scalar(p1[:, c:c + w], p1[:, c:c + w], rinv[:, g - 1, t:t + 1], None,
                                                 ALU.mult))
                            ins = d.scalar_tensor_tensor(out=p1[:, c:c + w], in0=p2[:, c:c + w],
                                                         scalar=rinv[:, g, t:t + 1], in1=p1[:, c:c + w],
                                                         op0=ALU.mult, op1=ALU.add)
                        ins.then_inc(prob_ready, 1)
                    else:
                        step(d.reciprocal(rinv[:, g, :], rsum[:, g, :]))
                        pr = prob[s % AHEAD]
                        d.tensor_scalar(pr[:, 0:w0], pr[:, 0:w0], rinv[:, g, 0:1], None, ALU.mult)
                        d.tensor_scalar(pr[:, w0:w0 + MEM], pr[:, w0:w0 + MEM], rinv[:, g, 1:2], None,
                                        ALU.mult).then_inc(prob_ready, 1)

                maxima(AHEAD - 1)
                normalise(0)
                for r in range(len(outs)):
                    if r + 1 < len(outs):
                        normalise(r + 1)
                    if r:
                        fill(r - 1)
                    maxima(last[r] + AHEAD)
                    if layer and r == DIFF_H:
                        sub_norm_var()
                    if layer and r in (DIFF_H + 1, DIFF_H + 2):
                        sub_norm(r - DIFF_H - 1)
                fill(len(outs) - 1)

            o4 = tok[:, :, 0:FOX_W].rearrange("p t (h n) -> p t h n", n=DV)

            def sub_norm_var():
                dve.wait_ge(o_squared, DIFF_H)
                d.tensor_scalar(o_ss[:, 1], o_ss[:, 0], 1.0 / DV, EPS, ALU.mult, ALU.add).then_inc(norm_var, 1)

            def sub_norm(t):
                if t == 0:
                    dve.wait_ge(norm_std, 6)
                    step(d.reciprocal(o_ss[:, 3], o_ss[:, 2]))
                    dve.wait_ge(o_out, DIFF_H)
                for h in range(DIFF_H):
                    i = DIFF_H * t + h
                    ins = d.scalar_tensor_tensor(out=o4[:, t, h], in0=o4[:, t, h], scalar=o_ss[:, 3, i:i + 1],
                                                 in1=subln[:], op0=ALU.mult, op1=ALU.mult)
                ins.then_inc(o_norm, 1)

            attention_dve(0)
            for p in range(P_OUT0, P_M1):
                take(p)
                if p < P_M1 - 1:
                    split_lo(unit_of(p + 3))
            dve.wait_ge(proj_out, P_M1)
            norm_dve(3, X, 4, parts=4)
            split_lo(U_FFN)
            take(P_M1)
            norm_fill_lo(3)
            split_lo(U_FFN + 1)
            take(P_M1 + 1)

            def ffn_mul(j, turns=0, moved=0):
                dve.wait_ge(unit_used, U_FFN + ffn_pos("U", j) + 1 + RAW * turns)
                dve.wait_ge(silu_done, j + 1 + moved)
                if j:
                    dve.wait_ge(h2_lo, j + moved)
                d.tensor_tensor(h2[j % 2][:], gate_act[j % 2][:], bank[5 + 2 * (j % 2)][:],
                                ALU.mult).then_inc(mul_done, 1)

            def ffn_h2_lo(j, moved=0):
                dve.wait_ge(h2_hi, j + 1 + moved)
                d.tensor_tensor(h2T_lo[j % 2][:], h2[j % 2][:], h2T_hi[j % 2][:].bitcast(F32),
                                ALU.subtract).then_inc(h2_lo, 1)

            ffn_mul(0)
            with dve.Fori(0, (FFN_STEPS - 1) // 2) as it:
                for j in (1, 2):
                    split_lo(U_FFN + ffn_pos("G", j), it)
                    ffn_h2_lo(j - 1, 2 * it)
                    split_lo(U_FFN + ffn_pos("U", j), it)
                    split_lo(U_FFN + ffn_pos("D", j - 1), it)
                    ffn_mul(j, it, 2 * it)
            split_lo(U_FFN + FFN_UNITS - 1)
            ffn_h2_lo(FFN_STEPS - 1)
            split_lo(U_KV)
            split_lo(U_KV + 1)
            dve.wait_ge(unit_used, U_KV)
            for t in range(NT):
                for h in range(2):
                    cols = slice(512 * h, 512 * (h + 1))
                    d.tensor_tensor(X[:, t, cols], X[:, t, cols], bank[2 * t + h][:], ALU.add).then_inc(x_added, 1)
            dve.wait_ge(x_added, 4)
            norm_dve(4, X, 5, parts=2)
            norm_fill_lo(4)

            def rotate(qk, count):
                for t in range(NT):
                    heads = qk[:, t, 0:FOX_W].rearrange("p (h n) -> p h n", n=HD)
                    x1, x2 = heads[:, :, 0:HALF], heads[:, :, HALF:ROT]
                    cos = cosv[:, t:t + 1, :].to_broadcast([P, 12, HALF])
                    sin = sinv[:, t:t + 1, :].to_broadcast([P, 12, HALF])
                    for i, (a, b) in enumerate(((x1, cos), (x2, sin), (x2, cos), (x1, sin))):
                        ins = d.tensor_tensor(rot[:, i], a, b, ALU.mult)
                        step(ins)
                    step(d.tensor_tensor(x1, rot[:, 0], rot[:, 1], ALU.subtract))
                    ins = d.tensor_tensor(x2, rot[:, 2], rot[:, 3], ALU.add)
                    if t == NT - 1:
                        ins.then_inc(rot_ready, 1)
                        dve.wait_ge(rot_ready, count)
                    else:
                        step(ins)

            def qk_take(first, dst):
                for b in range(3):
                    dve.wait_ge(qk_tr, first + b + 1)
                    d.tensor_copy(dst[:, 2 * b:2 * b + 2, :],
                                  bank[b][:].rearrange("p (c n) -> p c n", c=2)).then_inc(qk_out, 1)

            split_lo(U_KV + 2)
            apply_norm(5, X, 4)
            take(P_KV)
            split_lo(U_KV + 3)
            take(P_KV + 1)
            norm_fill_lo(5)
            take(P_KV + 2)
            split_lo(U_KV + 4)
            dve.wait_ge(proj_out, P_QD)
            dve.wait_ge(sin_ready, 1)
            rotate(tok, 1)
            split_lo(U_KV + 5)
            take(P_QD)
            split_lo(U_KV + 6)
            take(P_QD + 1)
            split_lo(U_KV + 7)
            take(P_QD + 2)
            qk_take(0, kT)
            dve.wait_ge(proj_out, P_VD)
            rotate(qtok, 2)
            split_lo(U_KV + 8)
            take(P_VD)
            split_lo(U_KV + 9)
            take(P_VD + 1)
            take(P_VD + 2)
            qk_take(3, qT)
            split_lo(U_KV + 10)
            split_lo(U_KV + 11)
            take(P_OUT1 - 1)
            attention_dve(1)
            for b in range(3):
                dve.wait_ge(fill_hi, int(FILL[6]) + 3 + b)
                d.tensor_tensor(op_lo[Y_BUF[1]][:, 2 * b:2 * b + 2, :], bank[b][:].rearrange("p (c n) -> p c n", c=2),
                                op_hi[Y_BUF[1]][:, 2 * b:2 * b + 2, :].bitcast(F32), ALU.subtract).then_inc(fill_lo, 1)
            split_lo(U_KV + 12)
            for p in range(P_OUT1, P_END):
                take(p)
                if p < P_END - 1:
                    split_lo([U_KV + 13, U_MOE, U_MOE + 1][p - P_OUT1])
            dve.wait_ge(proj_out, P_END)
            norm_dve(6, X, 7, parts=4)
            norm_fill_lo(6)
            dve.wait_ge(logitT_ready, 1)
            d.tensor_copy(small_T[0:N_EXP, :], bank[5][0:N_EXP, 0:SEQ]).then_inc(logitT_out, 1)
            dve.wait_ge(hn_hi_ready, 1)
            d.tensor_tensor(hn_lo, hn[:], hn_hi.bitcast(F32), ALU.subtract).then_inc(hn_lo_ready, 1)
            dve.wait_ge(logit_ready, 1)
            step(d.tensor_copy(lg[:], bank[4][:, 0:NT * N_EXP].rearrange("p (t n) -> p t n", t=NT)))
            for t in range(NT):
                ins = d.max(out=top[:, t, :], in_=lg[:, t, :])
            step(ins)
            for t in range(NT):
                ins = d.max_index(out=top_i[:, t, :], in_max=top[:, t, :], in_values=lg[:, t, :])
            step(ins)
            step(d.tensor_copy(top_f[:], top_i[:]))
            for t in range(NT):
                for i in range(2):
                    ins = d.tensor_scalar(oh[:, i, t, :], iota8[:], top_f[:, t, i:i + 1], None, ALU.is_equal)
            step(ins)
            step(d.tensor_tensor(member[:, :, 0:N_EXP], oh[:, 0], oh[:, 1], ALU.add))
            d.tensor_copy(member_bf[:], member[:, :, 0:N_EXP]).then_inc(member_ready, 1)
            d.tensor_tensor(gates[:, :, 0], top[:, :, 1], top[:, :, 0], ALU.subtract).then_inc(top_ready, 1)
            dve.wait_ge(rank_ready, 1)
            step(d.tensor_scalar(rank[:, :, 0:N_EXP], bank[4][:, 32:32 + NT * N_EXP].rearrange("p (t n) -> p t n", t=NT),
                                 1.0, None, ALU.subtract))

            def combine_weights():
                dve.wait_ge(gate_exp, 1)
                step(d.tensor_scalar(gates[:, :, 2], gates[:, :, 1], 1.0, None, ALU.add))
                step(d.reciprocal(gates[:, :, 2], gates[:, :, 2]))
                step(d.tensor_tensor(gates[:, :, 3], gates[:, :, 1], gates[:, :, 2], ALU.mult))
                for t in range(NT):
                    ins = d.tensor_scalar(comb[:, t, :], oh[:, 0, t, :], gates[:, t, 2:3], None, ALU.mult)
                step(ins)
                for t in range(NT):
                    ins = d.scalar_tensor_tensor(out=comb[:, t, :], in0=oh[:, 1, t, :], scalar=gates[:, t, 3:4],
                                                 in1=comb[:, t, :], op0=ALU.mult, op1=ALU.add)
                step(ins)
                step(d.tensor_reduce(over[:, 0:1], bank[4][:, 64:64 + N_EXP], AX.X, ALU.max))
                step(d.tensor_scalar(over[:, 1:2], over[:, 0:1], float(P), None, ALU.is_gt))
                d.tensor_copy(over_i[:], over[:, 1:2]).then_inc(route_ready, 1)

            def experts_dve(ps):
                ub = U_MOE + ps * N_EXP * MOE_UNITS
                tb = 2 + TB * N_EXP * ps
                hb = FFN_STEPS + MOE_STEPS * N_EXP * ps
                xb = 2 * N_EXP * ps
                ab = 4 + 4 * N_EXP * ps

                def one_hot(e):
                    for t in range(NT):
                        ins = d.tensor_scalar(slot_oh[:, t, :], slot_no[:, P * ps:P * (ps + 1)],
                                              rank[:, t, bass.ds(e, 1)], member[:, t, bass.ds(e, 1)],
                                              ALU.is_equal, ALU.mult)
                    ins.then_inc(oh_ready, 1)

                def halves(use, count, hi, lo, ready, done):
                    for i in range(2):
                        dve.wait_ge(ready, count + i + 1)
                        b = bank[tb_bank(f"gather{i}")] if use == "gather" else bank[i]
                        d.tensor_tensor(lo[:, 4 * i:4 * i + 4, :], b[:].rearrange("p (c n) -> p c n", c=4),
                                        hi[:, 4 * i:4 * i + 4, :].bitcast(F32), ALU.subtract).then_inc(done, 1)

                def output_lo(e):
                    halves("output", 2 * (N_EXP * ps + e) - 2, ye_hi, ye_lo, ye_hi_ready, ye_lo_ready)

                def add_back(e, i):
                    t, h = i // 2, i % 2
                    cols = slice(512 * h, 512 * (h + 1))
                    dve.wait_ge(tb_ready, tb + TB * e - TB + tb_count(f"back{i}")
                                - (2 if isinstance(e, int) and e == N_EXP else 0))
                    dve.wait_ge(x_added, ab + 4 * e - 4)
                    d.scalar_tensor_tensor(out=X[:, t, cols], in0=bank[tb_bank(f"back{i}")][:],
                                           scalar=comb[:, t, bass.ds(e - 1, 1)], in1=X[:, t, cols],
                                           op0=ALU.mult, op1=ALU.add).then_inc(x_added, 1)

                def expert(e, turns, first=False, final=False):
                    unit0 = ub + MOE_UNITS * (e if isinstance(e, int) else 1)

                    def lo(kind, j, k):
                        if not (first and ps == 0 and moe_pos(kind, j, k) < 3):
                            split_lo(unit0 + moe_pos(kind, j, k), turns)

                    def evac_T(j):
                        dve.wait_ge(h2_hi, hb + MOE_STEPS * e + j + 1)
                        d.tensor_tensor(h2T_lo[j % 2][:], bank[tb_bank(f"T{j}")][:], h2T_hi[j % 2][:].bitcast(F32),
                                        ALU.subtract).then_inc(h2_lo, 1)

                    def mul(j):
                        dve.wait_ge(unit_used, ub + moe_pos("U", j, 1) + 1 + MOE_UNITS * e)
                        dve.wait_ge(silu_done, hb + MOE_STEPS * e + j + 1)
                        if j >= 2:
                            dve.wait_ge(tb_ready, tb + TB * e + tb_count(f"T{j - 2}"))
                        elif not first:
                            dve.wait_ge(tb_ready, tb + TB * e - TB + tb_count("T6"))
                        d.tensor_tensor(h2[j % 2][:], gate_act[j % 2][:], bank[3 + 2 * (j % 2)][:],
                                        ALU.mult).then_inc(mul_done, 1)

                    lo("G", 0, 0)
                    lo("G", 0, 1)
                    if not first:
                        output_lo(e)
                    lo("U", 0, 0)
                    lo("U", 0, 1)
                    if not first:
                        add_back(e, 0)
                        add_back(e, 1)
                    lo("G", 1, 0)
                    if not first:
                        add_back(e, 2)
                        add_back(e, 3)
                    mul(0)
                    for j in range(1, MOE_STEPS):
                        if j > 1:
                            lo("G", j, 0)
                        lo("G", j, 1)
                        lo("U", j, 0)
                        evac_T(j - 1)
                        lo("U", j, 1)
                        if j == 3 and not final:
                            dve.wait_ge(tb_ready, tb + TB * e + tb_count("oneT"))
                            one_hot(e + 1)
                        lo("D", j - 1, 0)
                        lo("D", j - 1, 1)
                        mul(j)
                    if not final:
                        halves("gather", xb + 2 + 2 * e, xg_hi, xg_lo, xg_hi_ready, xg_lo_ready)
                    lo("D", MOE_STEPS - 1, 0)
                    evac_T(MOE_STEPS - 1)
                    lo("D", MOE_STEPS - 1, 1)

                one_hot(0)
                if ps == 0:
                    combine_weights()
                    split_lo(U_MOE + 2)
                halves("gather", xb, xg_hi, xg_lo, xg_hi_ready, xg_lo_ready)
                expert(0, 0, first=True)
                with dve.Fori(1, N_EXP - 1) as e:
                    expert(e, (MOE_UNITS // RAW) * e - MOE_UNITS // RAW)
                expert(N_EXP - 1, 0, final=True)
                output_lo(N_EXP)
                for i in range(4):
                    add_back(N_EXP, i)
                dve.wait_ge(x_added, ab + 4 * N_EXP)

            dve.wait_ge(slots_ready, 1)
            experts_dve(0)
            dve.wait_ge(route_ready, 1)
            flag = dve.value_load(over_i[0:1, 0:1], min_val=0, max_val=1)
            with dve.If(flag == 1):
                experts_dve(1)
            d.memset(over[:, 1:2], 0.0).then_inc(x_final, 1)
            dve.wait_ge(gain_in, 16 * 5)
            for t in range(NT):
                dve.wait_ge(norm_ss, 7 + t)
                d.tensor_scalar(stat[:, 7, 1, t:t + 1], stat[:, 7, 0, t:t + 1], 1.0 / D, EPS, ALU.mult,
                                ALU.add).then_inc(norm_var, 1)
                dve.wait_ge(norm_std, 8 + t)
                step(d.reciprocal(stat[:, 7, 3, t:t + 1], stat[:, 7, 2, t:t + 1]))
                for h in range(2):
                    cols = slice(512 * h, 512 * (h + 1))
                    d.scalar_tensor_tensor(out=hn[:, t, cols], in0=X[:, t, cols], scalar=stat[:, 7, 3, t:t + 1],
                                           in1=gain[:, cols], op0=ALU.mult, op1=ALU.mult).then_inc(hn_ready, 1)

        @block.tensor
        def _(pe):
            m = nc.tensor

            def product(dst, pairs, start=True, stop=True):
                n = len(pairs)
                for i, ((sh, sl), (mh, ml)) in enumerate(pairs):
                    m.matmul(dst, sh, mh, start=start and i == 0, stop=False)
                    m.matmul(dst, sh, ml, start=False, stop=False)
                    last = m.matmul(dst, sl, mh, start=False, stop=stop and i == n - 1)
                return last

            def norm_transposes(n):
                if n:
                    pe.wait_ge(fill_lo, int(FILL[NORM_FILL[n] - 1]))
                for g in range(4):
                    t, h = g // 2, g % 2
                    pe.wait_ge(hn_ready, 4 * n + g + 1)
                    for c in range(4):
                        k = 4 * h + c
                        last = m.transpose(bank[g][:, P * c:P * (c + 1)], hn[:, t, P * k:P * (k + 1)], ident[:])
                    last.then_inc(tr_ready, 1)

            def project(p):
                what, _ = PROJ[p]
                f = fill_of(p)
                hi, lo = op_hi[FILL_BUF[f]], op_lo[FILL_BUF[f]]
                u = unit_of(p)
                pe.wait_ge(fill_lo, int(FILL[f]))
                pe.wait_ge(lo_ready, u + 1)
                if p >= 4:
                    pe.wait_ge(proj_out, p - 3)
                wh, wl = wide(whi, u % SPLIT), wide(wlo, u % SPLIT)
                b = bank[4 + p % 4]
                for c in range(2):
                    dst = b[:, WIDE * c:WIDE * (c + 1)]
                    sl = slice(P * c, P * (c + 1))
                    if what in ("mk", "q", "k", "qm"):
                        last = product(dst, [((wh[:, k, sl], wl[:, k, sl]), (hi[:, k, :], lo[:, k, :]))
                                             for k in range(KC)])
                    else:
                        last = product(dst, [((hi[:, k, sl], lo[:, k, sl]), (wh[:, k, :], wl[:, k, :]))
                                             for k in range(KC)])
                last.then_inc(unit_used, 1)

            def small_product(dst, f, lo_col, hi_col):
                hi, lo = op_hi[FILL_BUF[f]], op_lo[FILL_BUF[f]]
                return product(dst[0:hi_col - lo_col, 0:SEQ],
                               [((small_hi[:, k, lo_col:hi_col], small_lo[:, k, lo_col:hi_col]),
                                 (hi[:, k, :], lo[:, k, :])) for k in range(KC)])

            def small_transposes(dst, n):
                for t in range(NT):
                    last = m.transpose(dst[:, n * t:n * (t + 1)], small_T[0:n, P * t:P * (t + 1)], ident[0:n, 0:n])
                return last

            def attention_pe(layer):
                scores, outs, last_s = attention_plan(layer)
                sb0, rb0 = S_BASE[layer], R_BASE[layer]
                done = [0]

                def score(s):
                    kind, h = scores[s]
                    g = sb0 + s
                    if s >= AHEAD:
                        pe.wait_ge(exp_done, g + 1 - AHEAD)
                    b = score_bank[s % AHEAD]
                    po, c = HD * (h % 2), h // 2
                    for t in range(NT):
                        sl = slice(P * t, P * (t + 1))
                        if kind == "mem":
                            mm = m.matmul(b[:, MEM * t:MEM * (t + 1)], qmT[po:po + HD, c, sl],
                                          mkT[layer][po:po + HD, c, :], start=True, stop=True)
                            continue
                        w = P * (t + 1)
                        o0 = P * t
                        m.matmul(b[:, o0:o0 + w], qT[po:po + HD, c, sl], kT[po:po + HD, c, 0:w], start=True,
                                 stop=False)
                        if kind == "fox":
                            m.matmul(b[:, o0:o0 + w], ident[0:FOX_H, h:h + 1].to_broadcast([FOX_H, P]),
                                     ncum[:, 0:w], start=False, stop=False)
                        mask = causal if kind == "fox" else chunked
                        mm = m.matmul(b[:, o0 + w - P:o0 + w], ident_bf[:], mask[:], start=False, stop=True)
                    mm.then_inc(score_ready, 1)

                def scores_until(upto):
                    while done[0] <= min(upto, len(scores) - 1):
                        score(done[0])
                        done[0] += 1

                def transposes(r):
                    kind, h = outs[r]
                    g = rb0 + r
                    pe.wait_ge(prob_ready, g + 1)
                    if g >= 2:
                        pe.wait_ge(pT_out, g - 1)
                    src = prob[(last_s[r] - (kind == "diff")) % AHEAD]
                    b = bank[3 + r % 2]
                    for i in range(4 if kind == "mem" else 3):
                        j = 2 * (i % 2) + i // 2 if kind == "mem" else i
                        tr = m.transpose(b[:, P * j:P * (j + 1)], src[:, P * i:P * (i + 1)], ident[:])
                    tr.then_inc(pT_ready, 1)

                def values(r):
                    kind, h = outs[r]
                    g = rb0 + r
                    pe.wait_ge(pT_out, g + 1)
                    pT = probT[r % 2]
                    if kind == "diff":
                        if r >= 2:
                            pe.wait_ge(o_out, r - 1)
                        b = bank[5 + r % 2]
                        cols = slice(DV * h, DV * (h + 1))
                        m.matmul(b[:, 0:P], pT[:, 0:P], v[:, 0, cols], start=True, stop=True)
                        m.matmul(b[:, P:2 * P], pT[:, P:2 * P], v[:, 0, cols], start=True, stop=False)
                        mm = m.matmul(b[:, P:2 * P], pT[:, 2 * P:3 * P], v[:, 1, cols], start=False, stop=True)
                    else:
                        pair = r // 2
                        if layer == 0 and pair >= 2:
                            pe.wait_ge(fill_lo, int(FILL[2]) + pair - 1)
                        if layer == 1:
                            pe.wait_ge(o_out, DIFF_H)
                        b = bank[5 + pair % 2]
                        po = HD * (h % 2)
                        cols = slice(HD * h, HD * (h + 1))
                        val = v if kind == "fox" else mv[layer]
                        m.matmul(b[po:po + HD, 0:SEQ], val[:, 0, cols], pT[:, 0:SEQ], start=True, stop=False)
                        if kind == "fox":
                            mm = m.matmul(b[po:po + HD, P:SEQ], val[:, 1, cols], pT[:, 2 * P:3 * P], start=False,
                                          stop=True)
                        else:
                            mm = m.matmul(b[po:po + HD, 0:SEQ], val[:, 1, cols], pT[:, SEQ:2 * SEQ], start=False,
                                          stop=True)
                    mm.then_inc(pv_ready, 1)

                scores_until(AHEAD - 1)
                for r in range(len(outs)):
                    transposes(r)
                    if r:
                        values(r - 1)
                    scores_until(last_s[r] + AHEAD)
                values(len(outs) - 1)

            pe.wait_ge(ident_ready, 1)
            norm_transposes(0)
            project(0)
            norm_transposes(1)
            project(1)
            for p in range(P_A, P_OUT0):
                project(p)
                if p == P_A:
                    norm_transposes(2)
                if p == P_A + 1:
                    pe.wait_ge(small_lo_ready, 1)
                    pe.wait_ge(small_hi_ready, 1)
                    pe.wait_ge(fill_lo, int(FILL[2]))
                    small_product(bank[3], 1, 0, FOX_H).then_inc(flT_ready, 1)
                if p == P_A + 2:
                    pe.wait_ge(flT_out, 1)
                    small_transposes(bank[2], FOX_H).then_inc(fl_ready, 1)
                if p == P_A + 5:
                    pe.wait_ge(logf_ready, 1)
                    pe.wait_ge(consts, 1)
                    m.matmul(bank[3][0:FOX_H, 256:512], fg[:, 2, 0, :], upper[:], start=True, stop=False)
                    m.matmul(bank[3][0:FOX_H, 384:512], fg[:, 2, 1, :], upper[:, 0:P], start=False,
                             stop=True).then_inc(cum_ready, 1)
            pe.wait_ge(ncum_ready, 1)
            pe.wait_ge(proj_out, P_OUT0)
            attention_pe(0)
            for p in range(P_OUT0, P_M1 + 1):
                project(p)
            norm_transposes(3)
            project(P_M1 + 1)
            pe.wait_ge(fill_lo, int(FILL[4]))
            pe.wait_ge(proj_out, P_M1 + 1)

            hi, lo = op_hi[FILL_BUF[4]], op_lo[FILL_BUF[4]]

            def ffn_up(kind, j, it=0):
                c = U_FFN + ffn_pos(kind, j)
                pe.wait_ge(lo_ready, c + RAW * it + 1)
                wh, wl = wide(whi, c % SPLIT), wide(wlo, c % SPLIT)
                b = bank[4 + 2 * (j % 2) + (kind == "U")]
                for c2 in range(2):
                    sl = slice(P * c2, P * (c2 + 1))
                    last = product(b[:, WIDE * c2:WIDE * (c2 + 1)],
                                   [((wh[:, k, sl], wl[:, k, sl]), (hi[:, k, :], lo[:, k, :])) for k in range(KC)])
                last.then_inc(unit_used, 1)

            def ffn_down(j, it=0, moved=0, first=False, final=False):
                c = U_FFN + ffn_pos("D", j)
                pe.wait_ge(h2_lo, j + 1 + moved)
                pe.wait_ge(lo_ready, c + RAW * it + 1)
                wh = whi[:, c % SPLIT, :].rearrange("p (k n) -> p k n", k=2)
                wl = wlo[:, c % SPLIT, :].rearrange("p (k n) -> p k n", k=2)
                for t in range(NT):
                    for h in range(2):
                        cols = slice(512 * h, 512 * (h + 1))
                        sls = [slice(WIDE * k + P * t, WIDE * k + P * (t + 1)) for k in range(2)]
                        last = product(bank[2 * t + h][:],
                                       [((h2T_hi[j % 2][:, s], h2T_lo[j % 2][:, s]), (wh[:, k, cols], wl[:, k, cols]))
                                        for k, s in enumerate(sls)], start=first, stop=final)
                last.then_inc(unit_used, 1)

            def ffn_pair(it, first=False):
                for j in (1, 2):
                    if j == 2 or not first:
                        pe.wait_ge(mul_done, j - 1 + 2 * it)
                    ffn_up("G", j, it)
                    ffn_up("U", j, it)
                    ffn_down(j - 1, it, 2 * it, first=first and j == 1)

            ffn_up("G", 0)
            pe.wait_ge(proj_out, P_KV)
            ffn_up("U", 0)
            ffn_pair(0, first=True)
            with pe.Fori(1, (FFN_STEPS - 1) // 2) as it:
                ffn_pair(it)
            ffn_down(FFN_STEPS - 1, 0, 0, final=True)

            def transposes_of(src, ready, val, sem_out):
                pe.wait_ge(ready, val)
                for b in range(3):
                    for c in range(2):
                        for t in range(NT):
                            k = 2 * b + c
                            last = m.transpose(bank[b][:, WIDE * c + P * t:WIDE * c + P * (t + 1)],
                                               src[:, t, P * k:P * (k + 1)], ident[:])
                    last.then_inc(sem_out, 1)

            norm_transposes(4)
            project(P_KV)
            project(P_KV + 1)
            norm_transposes(5)
            project(P_KV + 2)
            for p in range(P_QD, P_VD):
                project(p)
            transposes_of(tok, rot_ready, 1, qk_tr)
            for p in range(P_VD, P_OUT1 - 1):
                project(p)
            pe.wait_ge(qk_out, 3)
            transposes_of(qtok, rot_ready, 2, qk_tr)
            project(P_OUT1 - 1)
            pe.wait_ge(qk_out, 6)
            pe.wait_ge(proj_out, P_OUT1)
            attention_pe(1)
            transposes_of(tok, o_norm, 2, o_tr)
            for p in range(P_OUT1, P_END):
                project(p)
            norm_transposes(6)
            pe.wait_ge(fill_lo, int(FILL[8]))
            pe.wait_ge(proj_out, P_END)
            small_product(bank[5], 8, FOX_H, FOX_H + N_EXP).then_inc(logitT_ready, 1)
            pe.wait_ge(logitT_out, 1)
            small_transposes(bank[4], N_EXP).then_inc(logit_ready, 1)
            pe.wait_ge(member_ready, 1)
            b = bank[4]
            m.matmul(b[:, 32:40], upper_bf[:], member_bf[:, 0, :], start=True, stop=True)
            m.matmul(b[:, 40:48], ones_bf[:], member_bf[:, 0, :], start=True, stop=False)
            m.matmul(b[:, 40:48], upper_bf[:], member_bf[:, 1, :], start=False, stop=True)
            m.matmul(b[:, 64:72], ones_bf[:], member_bf[:, 0, :], start=True, stop=False)
            m.matmul(b[:, 64:72], ones_bf[:], member_bf[:, 1, :], start=False, stop=True).then_inc(rank_ready, 1)

            def experts_pe(ps):
                ub = U_MOE + ps * N_EXP * MOE_UNITS
                hb = FFN_STEPS + MOE_STEPS * N_EXP * ps
                xb = 2 * N_EXP * ps
                ab = 4 + 4 * N_EXP * ps
                ob = N_EXP * ps
                eb = N_EXP * ps

                def one_pass(dst, st_hi, st_lo, mv_hi, mv_lo, start, stop):
                    m.matmul(dst, st_hi, mv_hi, start=start, stop=False)
                    return m.matmul(dst, st_lo, mv_lo, start=False, stop=stop)

                def gather(waits):
                    for i in range(2):
                        for s, val in waits[i]:
                            pe.wait_ge(s, val)
                        b = bank[tb_bank(f"gather{i}")]
                        for c in range(4):
                            cols = slice(P * (4 * i + c), P * (4 * i + c + 1))
                            for t in range(NT):
                                last = one_pass(b[:, P * c:P * (c + 1)], hn_hi[:, t, cols], hn_lo[:, t, cols],
                                                slot_oh[:, t, :], slot_oh[:, t, :], t == 0, t == NT - 1)
                        last.then_inc(tb_ready, 1)

                def back(e):
                    pe.wait_ge(ye_lo_ready, 2 * (eb + e))
                    pe.wait_ge(ohT_out, eb + e)
                    for i in range(4):
                        after_last = isinstance(e, int) and e == N_EXP
                        s, val = [(h2_lo, hb + MOE_STEPS * e - 1) if after_last else (xg_lo_ready, xb + 2 * e + 2),
                                  (h2_lo, hb + MOE_STEPS * e),
                                  (x_added, ab + 4 * e - 3), (x_added, ab + 4 * e - 2)][i]
                        pe.wait_ge(s, val)
                        t, h = i // 2, i % 2
                        oneT = slot_ohT[:, P * t:P * (t + 1)]
                        one_pass(bank[tb_bank(f"back{i}")][:].rearrange("p (c n) -> p c n", c=4), oneT, oneT,
                                 ye_hi[:, 4 * h:4 * h + 4, :], ye_lo[:, 4 * h:4 * h + 4, :], True,
                                 True).then_inc(tb_ready, 1)

                def expert(e, first=False, final=False):
                    def up(kind, j, a):
                        c = ub + moe_pos(kind, j, a)
                        pe.wait_ge(lo_ready, c + MOE_UNITS * e + 1)
                        wh = whi[:, c % SPLIT, :].rearrange("p (k n) -> p k n", k=4)
                        wl = wlo[:, c % SPLIT, :].rearrange("p (k n) -> p k n", k=4)
                        product(bank[2 + 2 * (j % 2) + (kind == "U")][:],
                                [((xg_hi[:, 4 * a + k, :], xg_lo[:, 4 * a + k, :]), (wh[:, k, :], wl[:, k, :]))
                                 for k in range(4)], start=a == 0, stop=a == 1).then_inc(unit_used, 1)

                    def down(j, a):
                        c = ub + moe_pos("D", j, a)
                        pe.wait_ge(h2_lo, hb + MOE_STEPS * e + j + 1)
                        pe.wait_ge(lo_ready, c + MOE_UNITS * e + 1)
                        wh = whi[:, c % SPLIT, :].rearrange("p (k n) -> p k n", k=2)
                        wl = wlo[:, c % SPLIT, :].rearrange("p (k n) -> p k n", k=2)
                        for h in range(2):
                            cols = slice(512 * h, 512 * (h + 1))
                            sls = [slice(P * (2 * a + k), P * (2 * a + k + 1)) for k in range(2)]
                            last = product(bank[h][:],
                                           [((h2T_hi[j % 2][:, s], h2T_lo[j % 2][:, s]),
                                             (wh[:, k, cols], wl[:, k, cols])) for k, s in enumerate(sls)],
                                           start=j == 0 and a == 0, stop=j == MOE_STEPS - 1 and a == 1)
                        last.then_inc(unit_used, 1)

                    def h2_transposes(j):
                        pe.wait_ge(mul_done, hb + MOE_STEPS * e + j + 1)
                        if j == 0:
                            pe.wait_ge(x_added, ab + 4 * e)
                        elif j == 2:
                            pe.wait_ge(ohT_out, eb + e + 1)
                        elif j == MOE_STEPS - 1 and final:
                            pe.wait_ge(h2_lo, hb + MOE_STEPS * e + j - 1)
                        elif j == MOE_STEPS - 1:
                            pe.wait_ge(xg_lo_ready, xb + 2 * e + 3)
                        else:
                            pe.wait_ge(h2_lo, hb + MOE_STEPS * e + max(j - 1, 1))
                        for c in range(4):
                            last = m.transpose(bank[tb_bank(f"T{j}")][:, P * c:P * (c + 1)],
                                               h2[j % 2][:, P * c:P * (c + 1)], ident[:])
                        last.then_inc(tb_ready, 1)

                    pe.wait_ge(xg_lo_ready, xb + 2 * e + 2)
                    for j in range(MOE_STEPS):
                        pe.wait_ge(mul_done, hb + MOE_STEPS * e + max(j - 1, 0))
                        up("G", j, 0)
                        if j:
                            h2_transposes(j - 1)
                        up("G", j, 1)
                        up("U", j, 0)
                        if j == 0 and not first:
                            back(e)
                        up("U", j, 1)
                        if j == 1:
                            for t in range(NT):
                                last = m.transpose(bank[tb_bank("oneT")][:, P * t:P * (t + 1)],
                                                   slot_oh[:, t, :].bitcast(F32), ident[:])
                            last.then_inc(tb_ready, 1)
                        if j == MOE_STEPS - 1 and not final:
                            gather([[(oh_ready, ob + e + 2), (h2_lo, hb + MOE_STEPS * e + 5)],
                                    [(h2_lo, hb + MOE_STEPS * e + 6)]])
                        if j:
                            down(j - 1, 0)
                            if j == MOE_STEPS - 1:
                                h2_transposes(j)
                            down(j - 1, 1)
                    down(MOE_STEPS - 1, 0)
                    down(MOE_STEPS - 1, 1)

                pe.wait_ge(hn_lo_ready, 1)
                gather([[(oh_ready, ob + 1)], []])
                expert(0, first=True)
                with pe.Fori(1, N_EXP - 1) as e:
                    expert(e)
                expert(N_EXP - 1, final=True)
                back(N_EXP)

            experts_pe(0)
            pe.wait_ge(route_ready, 1)
            flag = pe.value_load(over_i[0:1, 0:1], min_val=0, max_val=1)
            with pe.If(flag == 1):
                experts_pe(1)


_INS = ["x", "mem", "positions", "mix_norm_g", "ffn_norm_g", "mem_norm_g", "w_mem_kv", "w_out", "w_in_a", "b_forget",
        "w_q_b", "lambda_q1", "lambda_k1", "lambda_q2", "lambda_k2", "subln_g", "kv_norm_g", "w_kv_shared",
        "w_gate_up_dense", "w_down_dense", "w_router", "w_gate_up_moe", "w_down_moe", "final_norm_g"]


def kernel(**inputs):
    import concourse.bacc as _bacc
    from concourse import mybir as _mybir
    from concourse.bass_utils import run_bass_kernel_spmd as _run

    nc = _bacc.Bacc("TRN2", target_bir_lowering=False, num_devices=1, dynamic_dma_scratch_size=8192)
    arrays, args = {}, []
    for name in _INS:
        a = np.ascontiguousarray(inputs[name])
        arrays[f"in_{name}_dram"] = a
        args.append(nc.dram_tensor(f"in_{name}_dram", a.shape, _mybir.dt.from_np(a.dtype), kind="ExternalInput").ap())
    args.append(nc.dram_tensor("out_0_dram", (1, SEQ, D), F32, kind="ExternalOutput").ap())
    build(nc, *args)
    r = _run(nc, [arrays], core_ids=[0])
    return r.results[0]["out_0_dram"]
```
